# Optimizing a Trainium2 kernel written in Bass

```python
import jax, jax.numpy as jnp
from jax import lax
import numpy as np

D_MODEL = 1024
BATCH = 1
SEQ = 256
DEPTH = 2

HEAD_DIM = 64
ROPE_THETA = 10000.0
Q_BLOCK = 128
NORM_EPS = 1e-6
NEG_INF = -1e30

NSA_HEADS = 8
NSA_GROUPS = 2
NSA_HPG = NSA_HEADS // NSA_GROUPS
CMP_LEN = 32
CMP_STRIDE = 16
CMP_HIDDEN = 256
SEL_LEN = 64
SEL_TOPN = 16
WINDOW = 512
FORCE_SCORE = 1e4

RET_HEADS = 4
RET_QK_DIM = 64
RET_V_DIM = 128
RET_CHUNK = 128

FOX_HEADS = 8

D_FF = 2816
N_EXPERTS = 8
TOP_K = 2
D_FF_EXPERT = 3584
N_DENSE = (DEPTH + 1) // 2
N_MOE = DEPTH // 2

NSA_Q = NSA_HEADS * HEAD_DIM
NSA_KV = NSA_GROUPS * HEAD_DIM
RET_QK = RET_HEADS * RET_QK_DIM
RET_V = RET_HEADS * RET_V_DIM
FOX_W = FOX_HEADS * HEAD_DIM
IN_SPLITS = (NSA_Q, NSA_KV, NSA_KV, NSA_KV, NSA_KV, NSA_KV, NSA_KV, 3 * NSA_HEADS,
             RET_QK, RET_QK, RET_V, RET_V,
             FOX_W, FOX_W, FOX_W, FOX_HEADS,
             3 * D_MODEL)
D_IN = sum(IN_SPLITS)

kernel_name = 'hybrid_nsa_retention_fox_moe_block'

def rms_norm(x, g):
    xf = x.astype(jnp.float32)
    y = xf * lax.rsqrt(jnp.mean(xf * xf, axis=-1, keepdims=True) + NORM_EPS)
    return (y * g.astype(jnp.float32)).astype(x.dtype)

def rope(x, pos):
    d = x.shape[-1]
    inv = ROPE_THETA ** (-jnp.arange(0, d, 2, dtype=jnp.float32) / d)
    ang = pos[:, None] * inv[None, :]
    ang = jnp.concatenate([ang, ang], axis=-1)[:, None, :]
    xf = x.astype(jnp.float32)
    x1, x2 = jnp.split(xf, 2, axis=-1)
    rot = jnp.concatenate([-x2, x1], axis=-1)
    return (xf * jnp.cos(ang) + rot * jnp.sin(ang)).astype(x.dtype)

def _masked_softmax(s, mask):
    s = jnp.where(mask, s.astype(jnp.float32), NEG_INF)
    return jnp.where(mask, jax.nn.softmax(s, axis=-1), 0.0)

def _gather_blocks(blocks, idx):
    return jax.vmap(jax.vmap(lambda bl, ix: bl[ix]))(blocks, idx)

def _compress(x, pe, w1, w2, tok_idx):
    B, _, G, dh = x.shape
    blk = x[:, tok_idx] + pe[:, None, :]
    blk = jnp.moveaxis(blk, 3, 1)
    blk = blk.reshape(B, G, tok_idx.shape[0], CMP_LEN * dh)
    return jax.nn.silu(blk @ w1) @ w2

def native_sparse_attention(q, k_cmp, v_cmp, k_sel, v_sel, k_win, v_win, gate_logits,
                            ck_pe, ck_w1, ck_w2, cv_pe, cv_w1, cv_w2):
    B, T, H, dh = q.shape
    G = NSA_GROUPS
    f32 = jnp.float32
    q, k_cmp, v_cmp, k_sel, v_sel, k_win, v_win = [a.astype(f32) for a in (q, k_cmp, v_cmp, k_sel, v_sel, k_win, v_win)]
    n_cmp = (T - CMP_LEN) // CMP_STRIDE + 1
    n_sel = T // SEL_LEN
    top_n = min(SEL_TOPN, n_sel)
    n_qb = T // Q_BLOCK
    scale = dh ** -0.5

    tok_idx = jnp.arange(n_cmp)[:, None] * CMP_STRIDE + jnp.arange(CMP_LEN)[None, :]
    kc = _compress(k_cmp, ck_pe, ck_w1, ck_w2, tok_idx)
    vc = _compress(v_cmp, cv_pe, cv_w1, cv_w2, tok_idx)
    cmp_start = jnp.arange(n_cmp) * CMP_STRIDE
    cmp_end = cmp_start + CMP_LEN - 1
    sel_start = jnp.arange(n_sel) * SEL_LEN
    overlap = ((cmp_start[:, None] < sel_start[None, :] + SEL_LEN)
               & (cmp_start[:, None] + CMP_LEN > sel_start[None, :])).astype(f32)
    sel_id = jnp.arange(n_sel)

    ks_blk = k_sel.reshape(B, n_sel, SEL_LEN, G, dh).transpose(0, 3, 1, 2, 4)
    vs_blk = v_sel.reshape(B, n_sel, SEL_LEN, G, dh).transpose(0, 3, 1, 2, 4)
    kw_pad = jnp.pad(k_win, ((0, 0), (WINDOW, 0), (0, 0), (0, 0))).transpose(0, 2, 1, 3)
    vw_pad = jnp.pad(v_win, ((0, 0), (WINDOW, 0), (0, 0), (0, 0))).transpose(0, 2, 1, 3)
    qg = q.reshape(B, T, G, NSA_HPG, dh).transpose(0, 2, 3, 1, 4)

    def block(i):
        t0 = i * Q_BLOCK
        tq = t0 + jnp.arange(Q_BLOCK)
        qb = lax.dynamic_slice_in_dim(qg, t0, Q_BLOCK, axis=3) * scale
        s = jnp.einsum('bghqd,bgnd->bghqn', qb, kc)
        p = _masked_softmax(s, cmp_end[None, :] <= tq[:, None])
        o_cmp = jnp.einsum('bghqn,bgnd->bghqd', p, vc)
        imp = jnp.einsum('bghqn,ns->bgqs', p, overlap)
        cur = (tq // SEL_LEN)[:, None]
        forced = (sel_id == 0) | (sel_id == cur) | (sel_id == cur - 1)
        score = jnp.where(forced, FORCE_SCORE, imp)
        score = jnp.where(sel_id <= cur, score, NEG_INF)
        _, idx = lax.top_k(score, top_n)
        kg = _gather_blocks(ks_blk, idx).reshape(B, G, Q_BLOCK, top_n * SEL_LEN, dh)
        vg = _gather_blocks(vs_blk, idx).reshape(B, G, Q_BLOCK, top_n * SEL_LEN, dh)
        tok = (idx[..., None] * SEL_LEN + jnp.arange(SEL_LEN)).reshape(B, G, 1, Q_BLOCK, top_n * SEL_LEN)
        s = jnp.einsum('bghqd,bgqkd->bghqk', qb, kg)
        p = _masked_softmax(s, tok <= tq[:, None])
        o_sel = jnp.einsum('bghqk,bgqkd->bghqd', p, vg)
        kw = lax.dynamic_slice_in_dim(kw_pad, t0, Q_BLOCK + WINDOW, axis=2)
        vw = lax.dynamic_slice_in_dim(vw_pad, t0, Q_BLOCK + WINDOW, axis=2)
        kpos = t0 - WINDOW + jnp.arange(Q_BLOCK + WINDOW)
        rel = tq[:, None] - kpos[None, :]
        wmask = (rel >= 0) & (rel < WINDOW) & (kpos[None, :] >= 0)
        s = jnp.einsum('bghqd,bgkd->bghqk', qb, kw)
        o_win = jnp.einsum('bghqk,bgkd->bghqd', _masked_softmax(s, wmask), vw)
        return o_cmp, o_sel, o_win

    outs = lax.map(block, jnp.arange(n_qb))
    o_cmp, o_sel, o_win = [o.transpose(1, 0, 4, 2, 3, 5).reshape(B, T, H, dh) for o in outs]
    g = jax.nn.sigmoid(gate_logits.astype(f32)).reshape(B, T, 3, H, 1)
    o = g[:, :, 0] * o_cmp + g[:, :, 1] * o_sel + g[:, :, 2] * o_win
    return o.reshape(B, T, H * dh)

def retention(q, k, v, g):
    f32 = jnp.float32
    q, k, v, g = [a.astype(f32) for a in (q, k, v, g)]
    B, T, H, dk = q.shape
    dv = v.shape[-1]
    C = RET_CHUNK
    n_c = T // C
    log_g = jnp.log(1.0 - 2.0 ** (-5.0 - jnp.arange(H, dtype=f32)))
    n = jnp.arange(C, dtype=f32)
    diff = n[:, None] - n[None, :]
    causal = diff >= 0
    decay_in = jnp.where(causal[None], jnp.exp(jnp.where(causal, diff, 0.0)[None] * log_g[:, None, None]), 0.0)
    q_decay = jnp.exp((n[None, :] + 1.0) * log_g[:, None])[None, :, :, None]
    k_decay = jnp.exp((C - 1.0 - n)[None, :] * log_g[:, None])[None, :, :, None]
    chunk_decay = jnp.exp(C * log_g)[None, :, None, None]

    def to_chunks(a):
        return a.reshape(B, n_c, C, H, a.shape[-1]).transpose(1, 0, 3, 2, 4)

    def step(state, inp):
        qc, kc, vc = inp
        inner = jnp.einsum('bhnd,bhmd->bhnm', qc, kc) * decay_in
        o = jnp.einsum('bhnm,bhme->bhne', inner, vc) + jnp.einsum('bhnd,bhde->bhne', qc * q_decay, state)
        state = state * chunk_decay + jnp.einsum('bhmd,bhme->bhde', kc * k_decay, vc)
        return state, o

    state0 = jnp.zeros((B, H, dk, dv), f32)
    _, o = lax.scan(step, state0, (to_chunks(q), to_chunks(k), to_chunks(v)))
    o = o.transpose(1, 0, 3, 2, 4).reshape(B, T, H, dv)
    mu = jnp.mean(o, axis=-1, keepdims=True)
    var = jnp.mean(jnp.square(o - mu), axis=-1, keepdims=True)
    o = (o - mu) * lax.rsqrt(var + NORM_EPS)
    return (jax.nn.silu(g) * o).reshape(B, T, H * dv)

def forgetting_attention(q, k, v, f_logit):
    f32 = jnp.float32
    B, T, H, dh = q.shape
    n_qb = T // Q_BLOCK
    scale = dh ** -0.5
    qh, kh, vh = [a.astype(f32).transpose(0, 2, 1, 3) for a in (q, k, v)]
    cum = jnp.cumsum(jax.nn.log_sigmoid(f_logit.astype(f32)), axis=1).transpose(0, 2, 1)
    kpos = jnp.arange(T)

    def block(i):
        t0 = i * Q_BLOCK
        tq = t0 + jnp.arange(Q_BLOCK)
        qb = lax.dynamic_slice_in_dim(qh, t0, Q_BLOCK, axis=2)
        cq = lax.dynamic_slice_in_dim(cum, t0, Q_BLOCK, axis=2)
        s = jnp.einsum('bhqd,bhkd->bhqk', qb, kh) * scale + (cq[..., None] - cum[:, :, None, :])
        p = _masked_softmax(s, kpos[None, :] <= tq[:, None])
        return jnp.einsum('bhqk,bhkd->bhqd', p, vh)

    o = lax.map(block, jnp.arange(n_qb))
    return o.transpose(1, 0, 3, 2, 4).reshape(B, T, H * dh)

def token_mixing(h, w_in, ck_pe, ck_w1, ck_w2, cv_pe, cv_w1, cv_w2, fox_f_bias,
                 w_read_nsa, w_read_ret, w_read_fox, w_out):
    B, T, _ = h.shape
    pos = jnp.arange(T, dtype=jnp.float32)
    points = np.cumsum(IN_SPLITS)[:-1].tolist()
    (nq, nkc, nvc, nks, nvs, nkw, nvw, ngate, rq, rk, rv, rg,
     fq, fk, fv, ff, mg) = jnp.split(h @ w_in, points, axis=-1)

    def heads(a, n_h):
        return a.reshape(B, T, n_h, -1)

    G = NSA_GROUPS
    o_nsa = native_sparse_attention(
        rope(heads(nq, NSA_HEADS), pos), rope(heads(nkc, G), pos), heads(nvc, G),
        rope(heads(nks, G), pos), heads(nvs, G), rope(heads(nkw, G), pos), heads(nvw, G), ngate,
        ck_pe, ck_w1, ck_w2, cv_pe, cv_w1, cv_w2)
    o_ret = retention(rope(heads(rq, RET_HEADS), pos),
                      rope(heads(rk, RET_HEADS), pos) * (RET_QK_DIM ** -0.5),
                      heads(rv, RET_HEADS), heads(rg, RET_HEADS))
    o_fox = forgetting_attention(heads(fq, FOX_HEADS), heads(fk, FOX_HEADS), heads(fv, FOX_HEADS),
                                 ff + fox_f_bias)
    gates = jax.nn.sigmoid(mg.astype(jnp.float32)).reshape(B, T, 3, D_MODEL)
    merged = (gates[:, :, 0] * (o_nsa @ w_read_nsa)
              + gates[:, :, 1] * (o_ret @ w_read_ret)
              + gates[:, :, 2] * (o_fox @ w_read_fox))
    return (merged @ w_out).astype(h.dtype)

def swiglu(h, w1, w3, w2):
    return (jax.nn.silu(h @ w1) * (h @ w3)) @ w2

def moe_ffn(h, w_router, w1, w3, w2):
    logits = (h @ w_router).astype(jnp.float32)
    top_v, top_i = lax.top_k(logits, TOP_K)
    top_w = jax.nn.softmax(top_v, axis=-1)
    gate = jnp.sum(jax.nn.one_hot(top_i, N_EXPERTS, dtype=jnp.float32) * top_w[..., None], axis=-2).astype(h.dtype)
    y = jnp.zeros_like(h)
    for e in range(N_EXPERTS):
        y = y + gate[..., e:e + 1] * swiglu(h, w1[e], w3[e], w2[e])
    return y

def setup_inputs(seed: int = 0) -> dict:
    key = jax.random.key(seed)
    keys = iter(jax.random.split(key, 32))

    def nrm(shape, scale):
        return jax.random.normal(next(keys), shape, jnp.float32) * scale

    D = D_MODEL
    L_dh = CMP_LEN * HEAD_DIM
    return {
        'x': nrm((BATCH, SEQ, D), 1.0),
        'c': nrm((BATCH, D), 1.0),
        'ada_w': nrm((DEPTH, D, 6 * D), 0.5 * D ** -0.5),
        'ada_b': nrm((DEPTH, 6 * D), 0.02),
        'norm_mix': 1.0 + nrm((DEPTH, D), 0.02),
        'norm_ffn': 1.0 + nrm((DEPTH, D), 0.02),
        'w_in': nrm((DEPTH, D, D_IN), D ** -0.5),
        'cmp_k_pe': nrm((DEPTH, CMP_LEN, HEAD_DIM), 0.1),
        'cmp_k_w1': nrm((DEPTH, L_dh, CMP_HIDDEN), L_dh ** -0.5),
        'cmp_k_w2': nrm((DEPTH, CMP_HIDDEN, HEAD_DIM), CMP_HIDDEN ** -0.5),
        'cmp_v_pe': nrm((DEPTH, CMP_LEN, HEAD_DIM), 0.1),
        'cmp_v_w1': nrm((DEPTH, L_dh, CMP_HIDDEN), L_dh ** -0.5),
        'cmp_v_w2': nrm((DEPTH, CMP_HIDDEN, HEAD_DIM), CMP_HIDDEN ** -0.5),
        'fox_f_bias': 3.0 + nrm((DEPTH, FOX_HEADS), 0.5),
        'w_read_nsa': nrm((DEPTH, NSA_Q, D), NSA_Q ** -0.5),
        'w_read_ret': nrm((DEPTH, RET_V, D), RET_V ** -0.5),
        'w_read_fox': nrm((DEPTH, FOX_W, D), FOX_W ** -0.5),
        'w_out': nrm((DEPTH, D, D), D ** -0.5),
        'ffn_w1': nrm((N_DENSE, D, D_FF), D ** -0.5),
        'ffn_w3': nrm((N_DENSE, D, D_FF), D ** -0.5),
        'ffn_w2': nrm((N_DENSE, D_FF, D), D_FF ** -0.5),
        'router_w': nrm((N_MOE, D, N_EXPERTS), D ** -0.5),
        'moe_w1': nrm((N_MOE, N_EXPERTS, D, D_FF_EXPERT), D ** -0.5),
        'moe_w3': nrm((N_MOE, N_EXPERTS, D, D_FF_EXPERT), D ** -0.5),
        'moe_w2': nrm((N_MOE, N_EXPERTS, D_FF_EXPERT, D), D_FF_EXPERT ** -0.5),
        'final_norm': 1.0 + nrm((D,), 0.02),
    }

def reference(x, c, ada_w, ada_b, norm_mix, norm_ffn, w_in, cmp_k_pe, cmp_k_w1, cmp_k_w2,
              cmp_v_pe, cmp_v_w1, cmp_v_w2, fox_f_bias, w_read_nsa, w_read_ret, w_read_fox, w_out,
              ffn_w1, ffn_w3, ffn_w2, router_w, moe_w1, moe_w3, moe_w2, final_norm):
    for l in range(DEPTH):
        mod = jax.nn.silu(c) @ ada_w[l] + ada_b[l]
        sh1, sc1, g1, sh2, sc2, g2 = jnp.split(mod[:, None, :], 6, axis=-1)
        h = rms_norm(x, norm_mix[l]) * (1.0 + sc1) + sh1
        x = x + g1 * token_mixing(h, w_in[l], cmp_k_pe[l], cmp_k_w1[l], cmp_k_w2[l],
                                  cmp_v_pe[l], cmp_v_w1[l], cmp_v_w2[l], fox_f_bias[l],
                                  w_read_nsa[l], w_read_ret[l], w_read_fox[l], w_out[l])
        h = rms_norm(x, norm_ffn[l]) * (1.0 + sc2) + sh2
        if l % 2 == 0:
            f = swiglu(h, ffn_w1[l // 2], ffn_w3[l // 2], ffn_w2[l // 2])
        else:
            f = moe_ffn(h, router_w[l // 2], moe_w1[l // 2], moe_w3[l // 2], moe_w2[l // 2])
        x = x + g2 * f
    return rms_norm(x, final_norm)


_drawn_inputs = setup_inputs


def setup_inputs(seed=0):
    import zlib

    import numpy as np

    out = dict(_drawn_inputs(seed))
    spreads = {}
    factors = {'norm_mix': 4.91,
     'norm_ffn': 3.58,
     'cmp_k_pe': 8.0,
     'cmp_k_w2': 2.843,
     'cmp_v_pe': 6.912,
     'final_norm': 2.804}
    for name, (base, spread) in spreads.items():
        noise = np.random.default_rng([zlib.crc32(name.encode()), seed]).standard_normal(out[name].shape)
        drawn = base * np.exp(spread * noise) if base else spread * noise
        out[name] = __import__('jax').numpy.asarray(drawn.astype(out[name].dtype))
    for name, factor in factors.items():
        out[name] = (out[name] * factor).astype(out[name].dtype)
    return out
```

```python
from contextlib import ExitStack, contextmanager

import numpy as np
import concourse.bass as bass
from concourse import mybir

F32 = mybir.dt.float32
F32R = mybir.dt.float32r
I32 = mybir.dt.int32
BF16 = mybir.dt.bfloat16
ALU = mybir.AluOpType
ACT = mybir.ActivationFunctionType
AX_X = mybir.AxisListType.X

P = 128
D = 1024
KB = D // P
SEQ = 256
TT = SEQ // P
DEPTH = 2
HD = 64
EPS = 1e-6
NEG = -1e30
SCALE = HD ** -0.5
HG = 4
D_IN = 7456
C_NQ, C_NKC, C_NVC, C_NKS, C_NVS, C_NKW, C_NVW, C_NG = 0, 512, 640, 768, 896, 1024, 1152, 1280
C_RQ, C_RK, C_RV, C_RG = 1304, 1560, 1816, 2328
C_FQ, C_FK, C_FV, C_FF, C_MG = 2840, 3352, 3864, 4376, 4384

CMP_LEN, CMP_STRIDE, CMP_HID = 32, 16, 256
NCMP = (SEQ - CMP_LEN) // CMP_STRIDE + 1
FF = 2816
FFE = 3584
NE = 8
W = 512
CK = 4
CHUNK = CK * W
RAW = 6
HL = 2
AHEAD = HL - 1
ADA = 6 * D // W
WBLK = 9
PROJ = WBLK * W
assert PROJ >= C_MG and WBLK % 3 == 0
FFB = FF // W
EFB = FFE // W
assert FF == FFB * W + W // 2 and FFE == EFB * W

TABLES = {}
_at = 0
for _n, _w in (("ident", P), ("tri", P), ("ones", P), ("iota", P), ("mask", 2 * P), ("cmask", 2 * 2 * 4 * 16),
               ("cvalid", 2), ("rope", 2 * 2 * HD), ("decay", 4 * 2 * P), ("ties", NE * NE)):
    TABLES[_n] = (_at, _w)
    _at += _w
TABLE_W = _at

R_ADAB, R_NMIX, R_NFFN, R_PEK, R_PEV, R_C = 0, 48, 56, 64, 80, 96
ROWS = 104


def tables():
    f = np.float32
    t = np.zeros((P, TABLE_W), f)

    def put(name, a):
        at, w = TABLES[name]
        t[:, at:at + w] = np.asarray(a, f).reshape(P, w)

    i = np.arange(P)
    put("ident", np.eye(P))
    put("tri", i[:, None] <= i[None, :])
    put("ones", np.ones((P, P)))
    put("iota", np.broadcast_to(i, (P, P)))
    causal = np.where(i[None, :] <= i[:, None], 0.0, NEG)
    put("mask", np.concatenate([np.zeros((P, P)), causal], 1))
    tok = np.arange(SEQ).reshape(TT, P)
    end = np.arange(16) * CMP_STRIDE + CMP_LEN - 1
    open_ = (end[None, None, :] <= tok[:, :, None]) & (np.arange(16) < NCMP)
    cm = np.where(open_, 0.0, NEG).transpose(1, 0, 2)[:, :, None, :]
    cm = np.broadcast_to(cm, (P, TT, HG, 16))
    put("cmask", np.stack([cm, cm], 1))
    put("cvalid", open_.any(-1).T)
    inv = f(10000.0) ** (-np.arange(0, HD, 2, dtype=f) / f(HD))
    ang = np.arange(SEQ, dtype=f)[:, None] * inv[None, :]
    cos = np.concatenate([np.cos(ang)] * 2, 1)
    sin = np.concatenate([-np.sin(ang), np.sin(ang)], 1)
    put("rope", np.stack([cos.reshape(TT, P, HD), sin.reshape(TT, P, HD)], 0).transpose(2, 0, 1, 3))
    log_g = np.log(f(1.0) - f(2.0) ** (f(-5.0) - np.arange(4, dtype=f)))
    diff = (np.arange(2 * P)[None, :] - i[:, None]).astype(f)
    dec = np.where(diff[:, None, :] >= 0, np.exp(np.maximum(diff, 0)[:, None, :] * log_g[None, :, None]), 0.0)
    put("decay", dec * f(SCALE))
    put("ties", np.broadcast_to(np.tril(np.ones((NE, NE)), -1), (P, NE, NE)))
    return t


class Turn:

    def __init__(self, size=1, start=0):
        self.size, self.n, self.loops = size, start, []

    def take(self):
        self.n += 1
        return self.n - 1

    def done(self, v, times=1):
        out = (v + 1) * times
        for reg, per in self.loops:
            out = reg * (per * times) + out
        return out

    def slot(self, v):
        return v % self.size

    def before(self, v):
        out = v // self.size
        for reg, per in self.loops:
            out = reg * (per // self.size) + out
        return out


@contextmanager
def rounds(eng, first, end, turns):
    at = [t.n for t in turns]
    with eng.Fori(first, end) as reg:
        for t, per in turns.items():
            assert per % t.size == 0
            t.loops.append((reg - first if first else reg, per))
        yield reg
        for t, n in zip(turns, at):
            assert t.n == n + turns[t], (t.n - n, turns[t])
            t.loops.pop()
    if isinstance(end, int):
        for t, n in zip(turns, at):
            t.n = n + turns[t] * (end - first)


class Books:

    def __init__(self):
        self.raw, self.hl = Turn(RAW), Turn(HL)
        self.raw_in, self.hl_in = Turn(RAW), Turn(HL)
        self.A, self.T, self.O = Turn(4), Turn(2), Turn(2)
        self.Af, self.Of = Turn(), Turn()
        self.link = Turn()


CALLS = [("cmp", 0), ("sel", 0), ("win", 0), ("cmp", 1), ("sel", 1), ("win", 1), ("ret", 0), ("fox", 0), ("fox", 1)]
WHOLE = {5: 0, 6: 1, 8: 2}
S_COUNT = {"cmp": 1, "sel": 2, "win": 2, "ret": 1, "fox": 2}
P_COUNT = {"cmp": 1, "sel": 2, "win": 2, "ret": 0, "fox": 2}
S_SIGNALS = sum(S_COUNT[k] for k, _ in CALLS)
P_SIGNALS = sum(P_COUNT[k] for k, _ in CALLS)


def build(nc, a, table, out):
    ctx = ExitStack()
    with ctx:
        def sem(name):
            return ctx.enter_context(nc.semaphore(name))

        here = [(nc.sbuf_base + 63) // 64 * 64]

        def sb(name, shape, dt=F32, at=None):
            size = 4
            for s in shape[1:]:
                size *= s
            if dt == BF16:
                size //= 2
            off = here[0] if at is None else at
            t = nc.alloc_sbuf_tensor_at(name, shape, dt, offset=off)
            if at is None:
                here[0] += (size + 31) // 32 * 32
            return t

        raw = [sb(f"raw{i}", [P, CHUNK]) for i in range(RAW)]
        w_hi = [sb(f"w_hi{i}", [P, CHUNK], F32R) for i in range(HL)]
        w_lo = [sb(f"w_lo{i}", [P, CHUNK], F32R) for i in range(HL)]
        tab = sb("tab", [P, TABLE_W])
        x = sb("x", [P, TT, D])
        h_hi = sb("h_hi", [P, KB, SEQ], F32R)
        h_lo = sb("h_lo", [P, KB, SEQ], F32R)
        rows = [sb(f"rows{i}", [P, P]) for i in range(DEPTH)]
        cols = sb("cols", [P, DEPTH, P])
        csilu = sb("csilu", [P, KB])
        mod = sb("mod", [P, DEPTH, 48])
        small = sb("small", [P, 64])
        fbias = sb("fbias", [P, DEPTH, 8])
        w2c = sb("w2c", [P, DEPTH, 2, 2, HD])
        routw = sb("routw", [P, KB, NE])
        zeros = sb("zeros", [P, W], BF16)
        pool_mark = sb("pool_mark", [P, 4])
        gates3 = sb("gates3", [P, TT, 24])
        nrm = sb("nrm", [P, 16])
        flag = sb("flag", [P, 4], I32)
        oT_hi, oT_lo = [None] * 3, [None] * 3
        oT_hi[0] = sb("oTn_hi", [P, 4, SEQ], F32R)
        oT_lo[0] = sb("oTn_lo", [P, 4, SEQ], F32R)

        area = here[0]
        proj = sb("proj", [P, TT, PROJ])
        PR = PROJ * 4
        oT_hi[1] = sb("oTr_hi", [P, 4, SEQ], F32R, at=area)
        oT_lo[1] = sb("oTr_lo", [P, 4, SEQ], F32R, at=area + PR)
        oT_hi[2] = sb("oTf_hi", [P, 4, SEQ], F32R, at=area + C_RQ * 4 + 32)
        oT_lo[2] = sb("oTf_lo", [P, 4, SEQ], F32R, at=area + PR + C_RQ * 4 + 32)
        merged = [sb(f"merged{t}", [P, D], at=area + t * PR + C_FQ * 4) for t in range(TT)]
        work = here[0]
        qT = sb("qT", [P, HG, SEQ])
        kT = [sb(f"kT{i}", [P, HG, SEQ]) for i in range(2)]
        S = [sb(f"S{i}", [P, HG * 3 * P]) for i in range(2)]
        PT = sb("PT", [P, HG * 3 * P])
        o_sb = sb("o_sb", [P, TT, W])
        stat = sb("stat", [P, 96])
        fox_st = sb("fox_st", [P, 24])
        ret_st = sb("ret_st", [P, 20])
        o_part = sb("o_part", [P, HG * HD])
        end_work = here[0]
        acc = [sb(f"acc{i}", [P, W], at=area + 2048 * i) for i in range(2)]
        y = sb("y", [P, TT, D], at=area + 4096)
        hf = sb("hf", [P, KB, SEQ], at=area + 12288)
        rope_t = sb("rope_t", [P, TT, 10, HD], at=work)
        kk = sb("kk", [P, 4, SEQ], at=work)
        win = sb("win", [P, 2, 16, 2, NCMP], at=work + 4096)
        win_hi = sb("win_hi", [P, 2, 16 * 30 + 98], F32R, at=work + 4096 + 4096)
        win_lo = sb("win_lo", [P, 2, 16 * 30 + 98], F32R, at=work + 4096 + 4096 + 4640)
        hid = sb("hid", [P, 2, CMP_HID], at=work + 17632)
        hidT = sb("hidT", [P, 4, 30], at=work + 19680)
        kcT = sb("kcT", [P, 32])
        vc = sb("vc", [P, 2, HD])
        q_aug = sb("q_aug", [P, TT, HG, HD + 2])
        k_aug = sb("k_aug", [P, TT, HG, HD + 2])
        cum = sb("cum", [P, TT, 8, 2])
        fox = sb("fox", [P, 4, TT * 8])
        assert here[0] <= nc.sbuf_usable_end
        gate = sb("gate", [P, TT, W], at=work)
        gw = sb("gw", [P, D], at=work + 24576)
        tmp = sb("tmp", [P, W], at=work + 8192)
        yacc = sb("yacc", [P, TT, D], at=area + 20480)
        a_sb = sb("a_sb", [P, TT, W], at=area + 28672)
        aT_hi = sb("aT_hi", [P, CK, SEQ], F32R, at=work)
        aT_lo = sb("aT_lo", [P, CK, SEQ], F32R, at=work + 4096)
        x_f = sb("x_f", [P, KB, P], at=work + 8192)
        x_hi = sb("x_hi", [P, KB, P], F32R, at=work + 12288)
        x_lo = sb("x_lo", [P, KB, P], F32R, at=work + 16384)
        oe = sb("oe", [P, D], at=area)
        sel = sb("sel", [P, TT, P], at=work + 20480)
        selT = sb("selT", [P, TT * P], at=work + 21504)
        rt = sb("rt", [P, TT, NE, NE], at=work + 22528)
        rt2 = sb("rt2", [P, NE, NE], at=work + 23040 + 640)
        rs = sb("rs", [P, 10, TT * NE], at=work + 23040)
        slot16 = sb("slot16", [P, TT, 2 * NE])
        gate16 = sb("gate16", [P, TT, 2 * NE])
        assert work + 23040 + 10 * TT * NE * 4 <= end_work, (end_work - work)
        assert here[0] <= nc.sbuf_usable_end, (here[0], nc.sbuf_usable_end)

        def cst(name):
            at, w = TABLES[name]
            return tab[:, at:at + w]

        ident, tri, ones, iota = cst("ident"), cst("tri"), cst("ones"), cst("iota")
        mask = cst("mask")
        cmask = cst("cmask")[:, 0:TT * HG * 16].rearrange("p (t h n) -> p t h n", t=TT, h=HG)
        cvalid = cst("cvalid")
        rope = cst("rope").rearrange("p (s t d) -> p s t d", s=2, t=TT)
        decay = cst("decay").rearrange("p (h n) -> p h n", h=4)
        ties = cst("ties").rearrange("p (e j) -> p e j", e=NE)

        SMALL = 16 * (2 + DEPTH * 3 + 1)

        def bank(name):
            return ctx.enter_context(nc.psum_tensor(name, [P, W], F32))[:, :]
        pA = [bank(f"pA{i}") for i in range(4)]
        pT = [bank(f"pT{i}") for i in range(2)]
        pO = [bank(f"pO{i}") for i in range(2)]

        landed = [sem(f"landed{i}") for i in range(RAW)]
        hi_ready = sem("hi_ready")
        raw_done = sem("raw_done")
        chunk_used = sem("chunk_used")
        A_full = sem("A_full")
        T_full = sem("T_full")
        O_full = sem("O_full")
        A_free = [sem(f"A_free{i}") for i in range(4)]
        T_free = [sem(f"T_free{i}") for i in range(2)]
        O_free = [sem(f"O_free{i}") for i in range(2)]
        small_in = sem("small_in")
        rows_in = [sem(f"rows_in{i}") for i in range(DEPTH)]
        late_in = sem("late_in")
        cols_ready = sem("cols_ready")
        csilu_ready = sem("csilu_ready")
        ada_summed = sem("ada_summed")
        consts = sem("consts")
        dve_link = sem("dve_link")
        act_link = sem("act_link")
        pool_link = sem("pool_link")
        ms_ready = sem("ms_ready")
        rt_ready = sem("rt_ready")
        y_ready = sem("y_ready")
        hf_ready = sem("hf_ready")
        h_hi_ready = sem("h_hi_ready")
        h_ready = sem("h_ready")
        proj_ready = sem("proj_ready")
        roped = sem("roped")
        kk_ready = sem("kk_ready")
        win_ready = sem("win_ready")
        win_hi_ready = sem("win_hi_ready")
        win_lo_ready = sem("win_lo_ready")
        hid_ready = sem("hid_ready")
        hidT_ready = sem("hidT_ready")
        kc_ready = sem("kc_ready")
        sig_ready = sem("sig_ready")
        z_ready = sem("z_ready")
        e_ready = sem("e_ready")
        ls_ready = sem("ls_ready")
        cum_ready = sem("cum_ready")
        aug_ready = sem("aug_ready")
        qk_ready = sem("qk_ready")
        s_ready = sem("s_ready")
        p_ready = sem("p_ready")
        pT_ready = sem("pT_ready")
        var_ready = sem("var_ready")
        dev_ready = sem("dev_ready")
        o_ready = sem("o_ready")
        oT_hi_ready = sem("oT_hi_ready")
        oT_ready = sem("oT_ready")
        g_ready = sem("g_ready")
        g_used = sem("g_used")
        merged_ready = sem("merged_ready")
        mT_hi_ready = sem("mT_hi_ready")
        mT_ready = sem("mT_ready")
        grow_ready = sem("grow_ready")
        g_free = sem("g_free")
        u_free = sem("u_free")
        silu_ready = sem("silu_ready")
        a_ready = sem("a_ready")
        aT_hi_ready = sem("aT_hi_ready")
        aT_ready = sem("aT_ready")
        log_ready = sem("log_ready")
        re_ready = sem("re_ready")
        sel_ready = sem("sel_ready")
        slots_ready = sem("slots_ready")
        selT_ready = sem("selT_ready")
        xf_ready = sem("xf_ready")
        x_hi_ready = sem("x_hi_ready")
        x_ready = sem("x_ready")
        oe_ready = sem("oe_ready")
        fin_ready = sem("fin_ready")
        stored = sem("stored")

        ctx.enter_context(nc.allow_non_contiguous_dma("small parameter loads"))
        block = ctx.enter_context(nc.Block())

        def chunk_rows(w, k0, c0, width=W, kb=CK):
            return w[bass.ds(k0, kb * P), bass.ds(c0, width)].rearrange("(k p) n -> p k n", p=P)

        @block.sync
        def _(sp):
            b = Books()

            def load(src, kb=CK):
                g = b.raw.take()
                slot = raw[b.raw.slot(g)]
                if g >= RAW or b.raw.loops:
                    sp.wait_ge(raw_done, b.raw.done(g - RAW))
                sp.dma_start(slot[:, :].rearrange("p (k n) -> p k n", k=kb), src).then_inc(landed[b.raw.slot(g)], 16)

            def block8(w, c0):
                for k in range(KB // CK):
                    load(chunk_rows(w, k * CK * P, c0))

            sp.dma_start(tab[:, :], table).then_inc(small_in, 16)
            for l in range(DEPTH):
                for at, n, src in ((R_ADAB, 48, a["ada_b"][l].rearrange("(r p) -> r p", p=P)),
                                   (R_NMIX, 8, a["norm_mix"][l].rearrange("(r p) -> r p", p=P)),
                                   (R_NFFN, 8, a["norm_ffn"][l].rearrange("(r p) -> r p", p=P)),
                                   (R_PEK, 16, a["cmp_k_pe"][l].rearrange("(j s) d -> j (s d)", s=2)),
                                   (R_PEV, 16, a["cmp_v_pe"][l].rearrange("(j s) d -> j (s d)", s=2)),
                                   (R_C, 8, a["c"].rearrange("a (r p) -> (a r) p", p=P))):
                    sp.dma_start(rows[l][at:at + n, :], src).then_inc(rows_in[l], 16)
            sp.dma_start(x[:, :, :], a["x"][0].rearrange("(t p) d -> p t d", p=P)).then_inc(small_in, 16)
            for l in range(DEPTH):
                sp.dma_start(fbias[:, l, :], a["fox_f_bias"][l:l + 1, :].broadcast_to([P, 8])).then_inc(small_in, 16)
                for i, name in enumerate(("cmp_k_w2", "cmp_v_w2")):
                    sp.dma_start(w2c[:, l, i, :, :], a[name][l].rearrange("(k p) d -> p k d", p=P)).then_inc(small_in, 16)
            sp.dma_start(routw[:, :, :], a["router_w"][0].rearrange("(k p) e -> p k e", p=P)).then_inc(small_in, 16)

            for j in range(ADA):
                block8(a["ada_w"][0], j * W)
            for l in range(1, DEPTH):
                with rounds(sp, 0, 2, {b.raw: ADA}) as r:
                    for j in range(ADA // 2):
                        block8(a["ada_w"][l], r * (ADA // 2 * W) + j * W)
            for l in range(DEPTH):
                with rounds(sp, 0, WBLK // 3, {b.raw: 6}) as r:
                    for j in range(3):
                        block8(a["w_in"][l], r * (3 * W) + j * W)
                for name in ("cmp_k_w1", "cmp_v_w1"):
                    for half in range(2):
                        load(chunk_rows(a[name][l], half * 8 * P, 0, CMP_HID, 8), 8)
                for half in range(2):
                    for m, name in enumerate(("w_read_nsa", "w_read_ret", "w_read_fox")):
                        block8(a["w_in"][l], C_MG + m * D + half * W)
                        load(chunk_rows(a[name][l], 0, half * W))
                for half in range(2):
                    block8(a["w_out"][l], half * W)
                if l % 2 == 0:
                    w1, w3, w2 = (a[n][l // 2] for n in ("ffn_w1", "ffn_w3", "ffn_w2"))
                    block8(w1, 0)
                    block8(w3, 0)
                    with rounds(sp, 1, FFB, {b.raw: 6}) as r:
                        block8(w1, r * W)
                        block8(w3, r * W)
                        for half in range(2):
                            load(chunk_rows(w2, r * W - W, half * W))
                    load(chunk_rows(w1, 0, FFB * W, W // 2, KB), KB)
                    load(chunk_rows(w3, 0, FFB * W, W // 2, KB), KB)
                    for half in range(2):
                        load(chunk_rows(w2, (FFB - 1) * W, half * W))
                    load(chunk_rows(w2, FFB * W, 0, D, 2), 2)
                else:
                    def experts():
                        with rounds(sp, 0, NE, {b.raw: EFB * 6}) as e:
                            w1, w3, w2 = (a[n][l // 2].rearrange("e k n -> (e k) n") for n in ("moe_w1", "moe_w3", "moe_w2"))

                            def up(f0):
                                for w in (w1, w3):
                                    for k in range(2):
                                        load(chunk_rows(w, e * D + k * CK * P, f0))

                            def down(f0):
                                for half in range(2):
                                    load(chunk_rows(w2, e * FFE + f0, half * W))
                            up(0)
                            with rounds(sp, 1, EFB, {b.raw: 6}) as f:
                                up(f * W)
                                down(f * W - W)
                            down((EFB - 1) * W)
                    experts()
                    sp.wait_ge(slots_ready, 1)
                    items = sp.value_load(flag[0:1, 0:1], min_val=NE, max_val=2 * NE)
                    with sp.If(items > NE):
                        experts()
            sp.wait_ge(ms_ready, 2 * DEPTH + 1)
            sp.dma_start(gw[:, :], a["final_norm"].unsqueeze(0).broadcast_to([P, D])).then_inc(late_in, 16)
            sp.wait_ge(fin_ready, 1)
            sp.dma_start(out[0].rearrange("(t p) d -> p t d", p=P), y[:, :, :]).then_inc(stored, 16)
            sp.wait_ge(stored, 16)

        marks = {}

        @block.tensor
        def _(pe):
            b = Books()

            def take(turn, free, banks):
                v = turn.take()
                if turn.loops or turn.before(v):
                    pe.wait_ge(free[turn.slot(v)], turn.before(v))
                return banks[turn.slot(v)]

            take_A = lambda: take(b.A, A_free, pA)
            take_T = lambda: take(b.T, T_free, pT)
            take_O = lambda: take(b.O, O_free, pO)

            def evacuated(turn, free, uses):
                for v in range(turn.n - min(uses, turn.size), turn.n):
                    pe.wait_ge(free[turn.slot(v)], turn.before(v) + 1)

            def mm3(dst, xh, xl, wh, wl, first, last):
                nc.tensor.matmul(dst, xl, wh, start=first, stop=False, skip_group_check=True)
                nc.tensor.matmul(dst, xh, wl, start=False, stop=False, skip_group_check=True)
                return nc.tensor.matmul(dst, xh, wh, start=False, stop=last, skip_group_check=True)

            def mm(dst, lhsT, rhs, first=True, last=True):
                return nc.tensor.matmul(dst, lhsT, rhs, start=first, stop=last, skip_group_check=True)

            def chunk_in():
                g, h = b.raw.take(), b.hl.take()
                pe.wait_ge(raw_done, b.raw.done(g))
                return w_hi[b.hl.slot(h)], w_lo[b.hl.slot(h)]

            def product(dsts, lhs, chunks, kb=CK, width=W, first=True, last=True):
                for c in range(chunks):
                    wh, wl = chunk_in()
                    for t, dst in enumerate(dsts):
                        for k in range(kb):
                            xh, xl = lhs(c * kb + k, t)
                            ins = mm3(dst, xh, xl, wh[:, k * width:(k + 1) * width], wl[:, k * width:(k + 1) * width],
                                      first and c + k == 0, last and c == chunks - 1 and k == kb - 1)
                    ins.then_inc(chunk_used, 1)

            def of(hi, lo):
                return lambda j, t: (hi[:, j, t * P:(t + 1) * P], lo[:, j, t * P:(t + 1) * P])

            def turned(blocks, width):
                pt = take_T()
                for i, src in enumerate(blocks):
                    n, m = src.shape[0], src.shape[1]
                    ins = nc.tensor.transpose(pt[0:m, i * width:i * width + n], src, ident[0:n, 0:n])
                ins.then_inc(T_full, 1)

            def turn8(src):
                for q in range(KB // 2):
                    turned([src(t, 2 * q + j) for j in range(2) for t in range(TT)], P)

            def gate_row(l, which):
                for half in range(2):
                    dst = take_A()
                    for k in range(4):
                        at = which * 8 + half * 4 + k
                        ins = mm(dst[:, k * P:(k + 1) * P], mod[:, l, at:at + 1].broadcast_to([P, P]), ident)
                    ins.then_inc(A_full, 1)

            def head(c0, h, t, w=HD):
                return proj[:, t, c0 + h * w:c0 + (h + 1) * w]

            def heads_T(c0, g, n):
                for p0 in range(0, n, 2):
                    turned([head(c0, g * HG + h, t) for h in range(p0, min(p0 + 2, n)) for t in range(TT)], P)

            pe.wait_ge(small_in, SMALL)
            for l in range(DEPTH):
                pe.wait_ge(rows_in[l], 6 * 16)
                turned([rows[l][0:ROWS, :]], P)
            for l in range(DEPTH):
                m_bank = take_A()
                with rounds(pe, 0, 2, {b.raw: ADA}) as r:
                    for j in range(ADA // 2):
                        b.raw.take()
                        g = b.raw.take()
                        pe.wait_ge(raw_done, b.raw.done(g))
                        for k in range(4):
                            ins = mm(m_bank[:, bass.ds(r * 24 + (j * 4 + k), 1)], acc[j % 2][:, k * P:(k + 1) * P], ones[:, 0:1])
                        ins.then_inc(ada_summed, 1)

            def attention_scores(c, l):
                kind, g = CALLS[c]
                kt = kT[c % 2]
                if kind == "cmp":
                    heads_T(C_NQ, g, HG)
                    evacuated(b.T, T_free, 2)
                    dst = take_A()
                    for t in range(TT):
                        for h in range(HG):
                            at = (t * HG + h) * 16
                            ins = mm(dst[:, at:at + NCMP], qT[0:HD, h, t * P:(t + 1) * P], kcT[0:HD, g * NCMP:(g + 1) * NCMP])
                    ins.then_inc(A_full, 1)
                    return
                if kind in ("sel", "win"):
                    c0 = C_NKS if kind == "sel" else C_NKW
                    turned([head(c0, g, t) for t in range(TT)], P)
                    evacuated(b.T, T_free, 1)
                    kd, one = HD, True
                elif kind == "ret":
                    heads_T(C_RQ, 0, HG)
                    heads_T(C_RK, 0, HG)
                    evacuated(b.T, T_free, 2)
                    for p0 in range(0, HG, 2):
                        dst = take_A()
                        for h in range(p0, p0 + 2):
                            ins = mm(dst[:, (h - p0) * SEQ:(h - p0 + 1) * SEQ], kt[0:HD, h, 0:P], qT[0:HD, h, :])
                        ins.then_inc(A_full, 1)
                    dst = take_A()
                    for h in range(HG):
                        ins = mm(dst[:, h * P:(h + 1) * P], kt[0:HD, h, P:SEQ], qT[0:HD, h, P:SEQ])
                    ins.then_inc(A_full, 1)
                    return
                else:
                    pe.wait_ge(aug_ready, 2 * l + g + 1)
                    for aug in (q_aug, k_aug):
                        for p0 in range(0, HG, 2):
                            turned([aug[:, t, h, :] for h in range(p0, p0 + 2) for t in range(TT)], P)
                    marks[l, g] = b.T.n
                    evacuated(b.T, T_free, 2)
                    kd, one = HD + 2, False
                dst = take_A()
                for h in range(HG):
                    ins = mm(dst[:, h * P:(h + 1) * P], qT[0:kd, h, 0:P], kt[0:kd, 0 if one else h, 0:P])
                ins.then_inc(A_full, 1)
                for p0 in range(0, HG, 2):
                    dst = take_A()
                    for h in range(p0, p0 + 2):
                        ins = mm(dst[:, (h - p0) * SEQ:(h - p0 + 1) * SEQ], qT[0:kd, h, P:SEQ], kt[0:kd, 0 if one else h, :])
                    ins.then_inc(A_full, 1)

            def attention_values(c, l):
                kind, g = CALLS[c]
                s = S[c % 2]
                if kind == "ret":
                    n = l * len(CALLS)
                    pe.wait_ge(s_ready, S_SIGNALS * l + sum(S_COUNT[k] for k, _ in CALLS[:c + 1]))
                    for t in range(TT):
                        dst = take_O()
                        for h in range(HG):
                            for m in range(t + 1):
                                lhsT = s[:, h * SEQ + t * P:h * SEQ + (t + 1) * P] if m == 0 else s[:, 4 * SEQ + h * P:4 * SEQ + (h + 1) * P]
                                ins = mm(dst[:, h * P:(h + 1) * P], lhsT, proj[:, m, C_RV + h * P:C_RV + (h + 1) * P], m == 0, m == t)
                        ins.then_inc(O_full, 1)
                    return
                p_at = P_SIGNALS * l + sum(P_COUNT[k] for k, _ in CALLS[:c])
                if kind == "cmp":
                    pe.wait_ge(p_ready, p_at + 1)
                    for t in range(TT):
                        turned([s[:, (t * HG + h) * 16:(t * HG + h) * 16 + NCMP] for h in range(HG)], P)
                    evacuated(b.T, T_free, 2)
                    for t in range(TT):
                        dst = take_O()
                        for h in range(HG):
                            ins = mm(dst[:, h * HD:(h + 1) * HD], PT[0:NCMP, (t * HG + h) * P:(t * HG + h + 1) * P], vc[0:NCMP, g, :])
                        ins.then_inc(O_full, 1)
                    return
                v0 = {"sel": C_NVS + g * HD, "win": C_NVW + g * HD, "fox": C_FV + g * HG * HD}[kind]
                vs = HD if kind == "fox" else 0
                pe.wait_ge(p_ready, p_at + 1)
                turned([s[:, h * P:(h + 1) * P] for h in range(HG)], P)
                evacuated(b.T, T_free, 1)
                dst = take_O()
                for h in range(HG):
                    ins = mm(dst[:, h * HD:(h + 1) * HD], PT[:, h * P:(h + 1) * P], proj[:, 0, v0 + h * vs:v0 + h * vs + HD])
                ins.then_inc(O_full, 1)
                pe.wait_ge(p_ready, p_at + 2)
                for p0 in range(0, HG, 2):
                    turned([s[:, HG * P + h * SEQ + m * P:HG * P + h * SEQ + (m + 1) * P] for h in range(p0, p0 + 2) for m in range(2)], P)
                evacuated(b.T, T_free, 2)
                dst = take_O()
                for h in range(HG):
                    for m in range(2):
                        at = (HG + h * 2 + m) * P
                        ins = mm(dst[:, h * HD:(h + 1) * HD], PT[:, at:at + P], proj[:, m, v0 + h * vs:v0 + h * vs + HD], m == 0, m == 1)
                ins.then_inc(O_full, 1)

            n_gu, n_a, n_h = [0], [0], [0]

            for l in range(DEPTH):
                pe.wait_ge(y_ready, 2 * l + 1)
                turn8(lambda t, k: y[:, t, k * P:(k + 1) * P])
                n_h[0] += 4
                pe.wait_ge(h_ready, n_h[0])
                with rounds(pe, 0, WBLK // 3, {b.raw: 6, b.hl: 6, b.A: 4, b.O: 2}) as r:
                    for j in range(3):
                        banks = [take_O(), take_O()] if j == 2 else [take_A(), take_A()]
                        product(banks, of(h_hi, h_lo), 2)
                pe.wait_ge(roped, l + 1)
                turned([proj[:, t, c0:c0 + 2 * HD] for c0 in (C_NKC, C_NVC) for t in range(TT)], P)
                pe.wait_ge(win_lo_ready, l + 1)
                for kv in range(2):
                    dst = take_A()
                    product([dst[:, 0:CMP_HID]], lambda j, t: (win_hi[:, kv, j * 30:j * 30 + P], win_lo[:, kv, j * 30:j * 30 + P]),
                            2, 8, CMP_HID)
                pe.wait_ge(hid_ready, 2 * l + 2)
                turned([hid[0:30, kv, k * P:(k + 1) * P] for kv in range(2) for k in range(2)], 32)
                evacuated(b.T, T_free, 1)
                dst = take_O()
                for k in range(2):
                    mm(dst[0:HD, 0:30], w2c[:, l, 0, k, :], hidT[:, k, :], k == 0, k == 1)
                for g in range(2):
                    for k in range(2):
                        ins = mm(dst[0:NCMP, HD + g * HD:HD + (g + 1) * HD], hidT[:, 2 + k, g * NCMP:(g + 1) * NCMP], w2c[:, l, 1, k, :], k == 0, k == 1)
                ins.then_inc(O_full, 1)
                pe.wait_ge(ls_ready, l + 1)
                dst = take_O()
                ls = fox[:, 3, :].rearrange("p (t h) -> p t h", t=TT)
                mm(dst[:, 0:8], tri, ls[:, 0, :])
                mm(dst[:, 8:16], ones, ls[:, 0, :], True, False)
                mm(dst[:, 8:16], tri, ls[:, 1, :], False, True).then_inc(O_full, 1)
                evacuated(b.O, O_free, 2)
                for c in range(len(CALLS) + 1):
                    if c < len(CALLS):
                        attention_scores(c, l)
                    if c:
                        attention_values(c - 1, l)
                        if c - 1 in WHOLE:
                            m = WHOLE[c - 1]
                            pe.wait_ge(o_ready, 3 * l + m + 1)
                            for q in range(2):
                                turned([o_sb[:, t, (2 * q + j) * P:(2 * q + j + 1) * P] for j in range(2) for t in range(TT)], P)
                for half in range(2):
                    for m in range(3):
                        product([take_A(), take_A()], of(h_hi, h_lo), 2)
                        if half == 0:
                            pe.wait_ge(oT_ready, 6 * l + 2 * m + 2)
                        product([take_A(), take_A()], of(oT_hi[m], oT_lo[m]), 1)
                pe.wait_ge(merged_ready, l + 1)
                turn8(lambda t, k: merged[t][:, k * P:(k + 1) * P])
                gate_row(l, 2)
                n_h[0] += 4
                pe.wait_ge(h_ready, n_h[0])
                for half in range(2):
                    product([take_A(), take_A()], of(h_hi, h_lo), 2)
                pe.wait_ge(y_ready, 2 * l + 2)
                turn8(lambda t, k: y[:, t, k * P:(k + 1) * P])

                if l % 2 == 0:
                    n_h[0] += 4
                    pe.wait_ge(h_ready, n_h[0])
                    G, U, av = Turn(), Turn(), Turn()
                    evacuated(b.A, A_free, 4)

                    def gate_up(banks, turn, free, chunks, kb, width):
                        v = turn.take()
                        if turn.loops or v:
                            pe.wait_ge(free, turn.done(v - 1))
                        product([p[:, 0:width] for p in banks], of(h_hi, h_lo), chunks, kb, width)

                    def turn_a(nb):
                        v = av.take()
                        pe.wait_ge(a_ready, av.done(v))
                        for q in range(nb // 2):
                            turned([a_sb[:, t, (2 * q + j) * P:(2 * q + j + 1) * P] for j in range(2) for t in range(TT)], P)

                    def down(nb):
                        evacuated(b.T, T_free, nb // 2)
                        if nb == CK:
                            for half in range(2):
                                wh, wl = chunk_in()
                                for t in range(TT):
                                    dst = take_O()
                                    for k in range(CK):
                                        xh, xl = of(aT_hi, aT_lo)(k, t)
                                        ins = mm3(dst, xh, xl, wh[:, k * W:(k + 1) * W], wl[:, k * W:(k + 1) * W], k == 0, k == CK - 1)
                                    if t == 0:
                                        ins.then_inc(O_full, 1)
                                ins.then_inc(chunk_used, 1)
                        else:
                            wh, wl = chunk_in()
                            for half in range(2):
                                for t in range(TT):
                                    dst = take_O()
                                    for k in range(nb):
                                        xh, xl = of(aT_hi, aT_lo)(k, t)
                                        at = k * D + half * W
                                        ins = mm3(dst, xh, xl, wh[:, at:at + W], wl[:, at:at + W], k == 0, k == nb - 1)
                                    if half + t < 2:
                                        ins.then_inc(O_full, 1)
                            ins.then_inc(chunk_used, 1)
                    gate_up(pA[0:2], G, g_free, 2, CK, W)
                    gate_up(pA[2:4], U, u_free, 2, CK, W)
                    with rounds(pe, 1, FFB, {b.raw: 6, b.hl: 6, b.T: 2, b.O: 4, G: 1, U: 1, av: 1}) as f:
                        gate_up(pA[0:2], G, g_free, 2, CK, W)
                        turn_a(CK)
                        gate_up(pA[2:4], U, u_free, 2, CK, W)
                        down(CK)
                    gate_up(pA[0:2], G, g_free, 1, KB, W // 2)
                    turn_a(CK)
                    gate_up(pA[2:4], U, u_free, 1, KB, W // 2)
                    down(CK)
                    turn_a(2)
                    down(2)
                    pe.wait_ge(g_free, G.n)
                    pe.wait_ge(u_free, U.n)
                    gate_row(l, 5)
                else:
                    pe.wait_ge(hf_ready, 4 * (2 * l + 2))
                    dst = take_A()
                    for t in range(TT):
                        for k in range(KB):
                            ins = mm(dst[:, t * NE:(t + 1) * NE], hf[:, k, t * P:(t + 1) * P], routw[:, k, :], k == 0, k == KB - 1)
                    ins.then_inc(A_full, 1)
                    pe.wait_ge(sel_ready, 1)
                    dst = take_A()
                    chosen = rs[:, 0, :].rearrange("p (t e) -> p t e", t=TT)
                    mm(dst[:, 0:NE], tri, chosen[:, 0, :])
                    mm(dst[:, NE:2 * NE], ones, chosen[:, 0, :], True, False)
                    mm(dst[:, NE:2 * NE], tri, chosen[:, 1, :], False, True)
                    mm(dst[:, 2 * NE:3 * NE], ones, chosen[:, 0, :], True, False)
                    mm(dst[:, 2 * NE:3 * NE], ones, chosen[:, 1, :], False, True).then_inc(A_full, 1)
                    gate_row(l, 5)
                    pe.wait_ge(slots_ready, 1)
                    items = pe.value_load(flag[0:1, 0:1], min_val=NE, max_val=2 * NE)
                    evacuated(b.A, A_free, 4)
                    G, U, av, xv = Turn(start=FFB + 1), Turn(start=FFB + 1), Turn(start=FFB + 1), Turn()
                    with rounds(pe, 0, items, {b.raw: 42, b.hl: 42, b.T: 22, b.O: 2, G: EFB, U: EFB, av: EFB, xv: 1}) as e:
                        v = xv.take()
                        pe.wait_ge(sel_ready, xv.done(v) + 1)
                        for q in range(2):
                            pt = take_T()
                            for j in range(4):
                                k = 4 * q + j
                                for t in range(TT):
                                    ins = mm(pt[:, j * P:(j + 1) * P], y[:, t, k * P:(k + 1) * P], sel[:, t, :], t == 0, t == 1)
                            ins.then_inc(T_full, 1)
                        for t in range(TT):
                            turned([sel[:, t, :]], P)
                        outs = [take_O(), take_O()]
                        for o in outs:
                            mm(o[:, :], zeros[:, 0:P], zeros[:, :], True, False)
                        pe.wait_ge(x_ready, xv.done(v, 2))

                        def gate_up(dst, turn, free):
                            v = turn.take()
                            pe.wait_ge(free, turn.done(v - 1))
                            product([dst], lambda j, t: (x_hi[:, j, :], x_lo[:, j, :]), 2)

                        def turn_a():
                            v = av.take()
                            pe.wait_ge(a_ready, av.done(v))
                            for q in range(2):
                                turned([a_sb[:, 0, (2 * q + j) * P:(2 * q + j + 1) * P] for j in range(2)], P)

                        def down(last=False):
                            evacuated(b.T, T_free, 2)
                            for half in range(2):
                                wh, wl = chunk_in()
                                for k in range(CK):
                                    ins = mm3(outs[half][:, :], aT_hi[:, k, 0:P], aT_lo[:, k, 0:P],
                                              wh[:, k * W:(k + 1) * W], wl[:, k * W:(k + 1) * W], False, last and k == CK - 1)
                                ins.then_inc(chunk_used, 1)
                        gate_up(pA[0], G, g_free)
                        gate_up(pA[2], U, u_free)
                        with rounds(pe, 1, EFB, {b.raw: 6, b.hl: 6, b.T: 2, G: 1, U: 1, av: 1}):
                            gate_up(pA[0], G, g_free)
                            turn_a()
                            gate_up(pA[2], U, u_free)
                            down()
                        turn_a()
                        down(True)
                        evacuated(b.O, O_free, 2)
                        for t in range(TT):
                            for half in range(2):
                                dst = take_T()
                                mm(dst[:, :], selT[:, t * P:(t + 1) * P], oe[:, half * W:(half + 1) * W]).then_inc(T_full, 1)

        @block.gpsimd
        def _(pool):
            n_link = [0]

            def link(ins):
                n_link[0] += 1
                ins.then_inc(pool_link, 1)
                pool.wait_ge(pool_link, n_link[0])

            link(pool.memset(zeros[:, :], 0.0))
            pool.wait_ge(small_in, SMALL)
            for l in range(DEPTH):
                pool.wait_ge(proj_ready, l + 1)
                half = HD // 2
                for c0, nh in ((C_NKC, 2), (C_NQ, 8), (C_NKS, 2), (C_NKW, 2), (C_RQ, 8)):
                    for t in range(TT):
                        v = proj[:, t, c0:c0 + nh * HD].rearrange("p (h d) -> p h d", h=nh)
                        r = rope_t[:, t, 0:nh, :]
                        cos, sin = (rope[:, s, t, :].unsqueeze(1) for s in range(2))
                        pool.tensor_tensor(r[:, :, 0:half], v[:, :, half:HD], sin[:, :, 0:half].broadcast_to([P, nh, half]), ALU.mult)
                        link(pool.tensor_tensor(r[:, :, half:HD], v[:, :, 0:half], sin[:, :, half:HD].broadcast_to([P, nh, half]), ALU.mult))
                        link(pool.tensor_tensor(v, v, cos.broadcast_to([P, nh, HD]), ALU.mult))
                        link(pool.tensor_tensor(v, v, r, ALU.add))
                pool.drain().then_inc(roped, 1)
                pool.wait_ge(cum_ready, l + 1)
                for g in range(2):
                    if g or l:
                        pool.wait_ge(T_full, marks[l - 1 + g, 1 - g])
                    for aug, c0, own in ((q_aug, C_FQ, 0), (k_aug, C_FK, 1)):
                        src = proj[:, :, c0 + g * HG * HD:c0 + (g + 1) * HG * HD].rearrange("p t (h d) -> p t h d", h=HG)
                        for t in range(TT):
                            pool.tensor_copy(aug[:, t, :, 0:HD], src[:, t, :, :])
                            pool.tensor_copy(aug[:, t, :, HD + own:HD + own + 1], cum[:, t, g * HG:(g + 1) * HG, own:own + 1])
                            pool.memset(aug[:, t, :, HD + 1 - own:HD + 2 - own], 1.0)
                    pool.drain().then_inc(aug_ready, 1)

        @block.scalar
        def _(act):
            b = Books()
            link_n = [0]

            def link(ins):
                link_n[0] += 1
                ins.then_inc(act_link, 1)
                act.wait_ge(act_link, link_n[0])

            def copy(dst, src):
                return nc.scalar.activation(dst, src, ACT.Copy)

            def split(n):
                for _ in range(n):
                    g, h = b.raw_in.take(), b.hl_in.take()
                    act.wait_ge(landed[b.raw_in.slot(g)], (b.raw_in.before(g) + 1) * 16)
                    if h >= HL or b.hl_in.loops:
                        act.wait_ge(chunk_used, b.hl_in.done(h - HL))
                    copy(w_hi[b.hl_in.slot(h)][:, :], raw[b.raw_in.slot(g)][:, :]).then_inc(hi_ready, 1)

            def used(n=1):
                for _ in range(n):
                    b.raw.take()
                    v = b.hl.take()
                return v

            def T_in():
                v = b.T.take()
                act.wait_ge(T_full, b.T.done(v))
                return pT[b.T.slot(v)], T_free[b.T.slot(v)]

            def T_copy(dst_of):
                pt, free = T_in()
                copy(*dst_of(pt)).then_inc(free, 1)

            def skip(turn, n):
                for _ in range(n):
                    turn.take()

            act.wait_ge(cols_ready, 1)
            nc.scalar.activation(csilu[:, :], cols[:, 0, R_C:R_C + 8], ACT.Silu).then_inc(csilu_ready, 1)
            skip(b.T, DEPTH)
            for l in range(DEPTH):
                skip(b.A, 1)
                for _ in range(2 * ADA):
                    b.raw_in.take()
                    b.raw.take()
            n_norm, n_hf, n_m, n_dev = [0], [0], [0], [0]

            def root():
                n_norm[0] += 1
                act.wait_ge(ms_ready, n_norm[0])
                nc.scalar.activation(nrm[:, 2:4], nrm[:, 0:2], ACT.Sqrt).then_inc(rt_ready, 1)

            def hi_columns():
                for q in range(4):
                    b.T.take()
                    n_hf[0] += 1
                    act.wait_ge(hf_ready, n_hf[0])
                    copy(h_hi[:, 2 * q:2 * q + 2, :], hf[:, 2 * q:2 * q + 2, :]).then_inc(h_hi_ready, 1)

            def evacuate_qk(c, l):
                kind, g = CALLS[c]
                kt = kT[c % 2]
                pair = lambda dst, p0, kd: T_copy(lambda pt: (dst[0:kd, p0:p0 + 2, :], pt[0:kd, :].rearrange("p (h n) -> p h n", h=2)))
                if kind == "cmp":
                    pair(qT, 0, HD)
                    pair(qT, 2, HD)
                    skip(b.A, 1)
                elif kind in ("sel", "win"):
                    T_copy(lambda pt: (kt[0:HD, 0, :], pt[0:HD, 0:SEQ]))
                    skip(b.A, 3)
                else:
                    kd = HD if kind == "ret" else HD + 2
                    for dst in (qT, kt):
                        pair(dst, 0, kd)
                        pair(dst, 2, kd)
                    skip(b.A, 3)

            def exponentials(c, l):
                kind, g = CALLS[c]
                s, st = S[c % 2], stat[:, (c % 2) * 40:(c % 2) * 40 + 40]
                s_at = S_SIGNALS * l + sum(S_COUNT[k] for k, _ in CALLS[:c])
                if kind == "ret":
                    return
                if kind == "cmp":
                    act.wait_ge(s_ready, s_at + 1)
                    nc.scalar.activation(s[:, 0:P], s[:, 0:P], ACT.Exp, scale=SCALE).then_inc(p_ready, 1)
                    return
                for t in range(TT):
                    act.wait_ge(s_ready, s_at + t + 1)
                    for h in range(HG):
                        v = s[:, h * P:(h + 1) * P] if t == 0 else s[:, HG * P + h * SEQ:HG * P + (h + 1) * SEQ]
                        ins = nc.scalar.activation(v, v, ACT.Exp, bias=st[:, 8 + t * HG + h:9 + t * HG + h], scale=SCALE,
                                                   accum_out=st[:, 16 + t * HG + h:17 + t * HG + h])
                    ins.then_inc(p_ready, 1)

            def evacuate_p(c):
                kind, g = CALLS[c]
                if kind == "ret":
                    for t in range(TT):
                        skip(b.O, 1)
                        n_dev[0] += 1
                        act.wait_ge(var_ready, n_dev[0])
                        nc.scalar.activation(ret_st[:, 12:16], ret_st[:, 8:12], ACT.Sqrt).then_inc(dev_ready, 1)
                elif kind == "cmp":
                    for t in range(TT):
                        T_copy(lambda pt: (PT[0:NCMP, t * 4 * P:(t + 1) * 4 * P], pt[0:NCMP, :]))
                    skip(b.O, 2)
                else:
                    for i in range(3):
                        T_copy(lambda pt: (PT[:, i * 4 * P:(i + 1) * 4 * P], pt[:, :]))
                    skip(b.O, 2)

            for l in range(DEPTH):
                root()
                hi_columns()
                split(AHEAD)
                with rounds(act, 0, WBLK // 3, {b.raw: 6, b.hl: 6, b.raw_in: 6, b.hl_in: 6, b.A: 4, b.O: 2}):
                    for j in range(3):
                        split(2)
                        used(2)
                    skip(b.A, 4)
                    skip(b.O, 2)
                pt, free = T_in()
                for i in range(4):
                    kv, g = divmod(i, 2)
                    src = pt[g * HD:(g + 1) * HD, kv * SEQ:(kv + 1) * SEQ]
                    copy(kk[0:HD, i, :], src)
                    ins = copy(kk[HD:P, i, 0:SEQ - 1], src[:, 1:SEQ])
                ins.then_inc(free, 1)
                act.wait_ge(win_ready, l + 1)
                copy(win_hi[:, :, 0:480], win[:, :, :, :, :].rearrange("p v j g n -> p v (j g n)")).then_inc(win_hi_ready, 1)
                for kv in range(2):
                    split(2 - kv * AHEAD)
                    v = used(2)
                    av = b.A.take()
                    act.wait_ge(chunk_used, b.hl.done(v))
                    nc.scalar.activation(hid[0:30, kv, :], pA[b.A.slot(av)][0:30, 0:CMP_HID], ACT.Silu).then_inc(hid_ready, 1)
                    act.drain().then_inc(A_free[b.A.slot(av)], 1)
                pt, free = T_in()
                copy(hidT[:, :, :], pt[:, 0:P].rearrange("p (i n) -> p i n", i=4)[:, :, 0:30]).then_inc(free, 1)
                skip(b.O, 2)
                act.wait_ge(proj_ready, l + 1)
                rg = proj[:, :, C_RG:C_RG + W]
                nc.scalar.activation(rg, rg, ACT.Silu)
                nc.scalar.activation(gates3[:, :, :], proj[:, :, C_NG:C_NG + 24], ACT.Sigmoid).then_inc(sig_ready, 1)
                act.wait_ge(z_ready, l + 1)
                link(nc.scalar.activation(fox[:, 1, :], fox[:, 1, :], ACT.Exp))
                nc.scalar.activation(fox[:, 2, :], fox[:, 1, :], ACT.Ln, bias=1.0).then_inc(e_ready, 1)
                for c in range(len(CALLS) + 1):
                    if c < len(CALLS):
                        evacuate_qk(c, l)
                        exponentials(c, l)
                    if c:
                        evacuate_p(c - 1)
                        if c - 1 in WHOLE:
                            m = WHOLE[c - 1]
                            for q in range(2):
                                pt, free = T_in()
                                copy(oT_hi[m][:, 2 * q:2 * q + 2, :], pt[:, :].rearrange("p (k n) -> p k n", k=2)).then_inc(oT_hi_ready, 1)
                split(AHEAD)
                for half in range(2):
                    for m in range(3):
                        split(2)
                        v = used(2)
                        act.wait_ge(chunk_used, b.hl.done(v))
                        if n_m[0]:
                            act.wait_ge(g_used, n_m[0])
                        n_m[0] += 1
                        for t in range(TT):
                            av = b.A.take()
                            ins = nc.scalar.activation(gate[:, t, :], pA[b.A.slot(av)][:, :], ACT.Sigmoid)
                            ins.then_inc(A_free[b.A.slot(av)], 1)
                        skip(b.A, 2)
                        split(1)
                        used(1)
                for q in range(4):
                    pt, free = T_in()
                    copy(h_hi[:, 2 * q:2 * q + 2, :], pt[:, :].rearrange("p (k n) -> p k n", k=2)).then_inc(h_hi_ready, 1)
                skip(b.A, 2)
                split(4 - AHEAD)
                used(4)
                skip(b.A, 4)
                root()
                if l % 2 == 0:
                    hi_columns()
                    split(AHEAD)
                    G, av, bv = Turn(), Turn(), Turn()

                    def silu(width=W):
                        v = G.take()
                        act.wait_ge(chunk_used, b.hl.done(b.hl.n - 1))
                        for t in range(TT):
                            ins = nc.scalar.activation(a_sb[:, t, 0:width], pA[t][:, 0:width], ACT.Silu)
                        ins.then_inc(g_free, 1)

                    def hi_a(n):
                        for q in range(n):
                            pt, free = T_in()
                            copy(aT_hi[:, 2 * q:2 * q + 2, :], pt[:, :].rearrange("p (k n) -> p k n", k=2)).then_inc(aT_hi_ready, 1)
                    split(2)
                    used(2)
                    silu()
                    split(2)
                    used(2)
                    with rounds(act, 1, FFB, {b.raw: 6, b.hl: 6, b.raw_in: 6, b.hl_in: 6, b.T: 2, b.O: 4, G: 1}):
                        split(2)
                        used(2)
                        hi_a(2)
                        silu()
                        split(2)
                        used(2)
                        split(2)
                        used(2)
                        skip(b.O, 4)
                    split(1)
                    used(1)
                    hi_a(2)
                    silu(W // 2)
                    split(1)
                    used(1)
                    split(2)
                    used(2)
                    skip(b.O, 4)
                    hi_a(1)
                    split(1 - AHEAD)
                    used(1)
                    skip(b.O, 4)
                    skip(b.A, 2)
                else:
                    b.T.take(), b.T.take(), b.T.take(), b.T.take()
                    act.wait_ge(log_ready, 1)
                    nc.scalar.activation(rs[:, 2, :], rs[:, 2, :], ACT.Exp).then_inc(re_ready, 1)
                    act.wait_ge(slots_ready, 1)
                    items = act.value_load(flag[0:1, 0:1], min_val=NE, max_val=2 * NE)
                    G, xv = Turn(start=FFB + 1), Turn()
                    with rounds(act, 0, items, {b.raw: 42, b.hl: 42, b.raw_in: 42, b.hl_in: 42, b.T: 22, b.O: 2, G: EFB, xv: 1}) as e:
                        v = xv.take()
                        split(AHEAD)
                        for q in range(2):
                            b.T.take()
                            act.wait_ge(xf_ready, xv.done(v, 2) - 1 + q)
                            copy(x_hi[:, 4 * q:4 * q + 4, :], x_f[:, 4 * q:4 * q + 4, :]).then_inc(x_hi_ready, 1)
                        for t in range(TT):
                            T_copy(lambda pt: (selT[:, t * P:(t + 1) * P], pt[:, 0:P]))
                        skip(b.O, 2)

                        def silu():
                            G.take()
                            act.wait_ge(chunk_used, b.hl.done(b.hl.n - 1))
                            nc.scalar.activation(a_sb[:, 0, :], pA[0][:, :], ACT.Silu).then_inc(g_free, 1)

                        def hi_a():
                            for q in range(2):
                                pt, free = T_in()
                                copy(aT_hi[:, 2 * q:2 * q + 2, 0:P], pt[:, 0:SEQ].rearrange("p (k n) -> p k n", k=2)).then_inc(aT_hi_ready, 1)
                        split(2)
                        used(2)
                        silu()
                        split(2)
                        used(2)
                        with rounds(act, 1, EFB, {b.raw: 6, b.hl: 6, b.raw_in: 6, b.hl_in: 6, b.T: 2, G: 1}):
                            split(2)
                            used(2)
                            hi_a()
                            silu()
                            split(4)
                            used(4)
                        hi_a()
                        split(2 - AHEAD)
                        used(2)
                        skip(b.T, 4)
            root()

        @block.vector
        def _(dve):
            b = Books()
            link_n = [0]
            V = nc.vector

            def link(ins):
                link_n[0] += 1
                ins.then_inc(dve_link, 1)
                dve.wait_ge(dve_link, link_n[0])

            def split(n):
                for _ in range(n):
                    g, h = b.raw_in.take(), b.hl_in.take()
                    dve.wait_ge(hi_ready, b.hl_in.done(h))
                    s, m = b.raw_in.slot(g), b.hl_in.slot(h)
                    V.tensor_tensor(w_lo[m][:, :], raw[s][:, :], w_hi[m][:, :].bitcast(F32), ALU.subtract).then_inc(raw_done, 1)

            def used(n=1):
                for _ in range(n):
                    b.raw.take()
                    v = b.hl.take()
                return v

            def T_in():
                v = b.T.take()
                dve.wait_ge(T_full, b.T.done(v))
                return pT[b.T.slot(v)], T_free[b.T.slot(v)]

            def A_in(chunk=None):
                v = b.A.take()
                if chunk is None:
                    dve.wait_ge(A_full, b.Af.done(b.Af.take()))
                else:
                    dve.wait_ge(chunk_used, b.hl.done(chunk))
                return pA[b.A.slot(v)], A_free[b.A.slot(v)]

            def O_in(chunk=None):
                v = b.O.take()
                if chunk is None:
                    dve.wait_ge(O_full, b.Of.done(b.Of.take()))
                else:
                    dve.wait_ge(chunk_used, b.hl.done(chunk))
                return pO[b.O.slot(v)], O_free[b.O.slot(v)]

            def skip(turn, n):
                for _ in range(n):
                    turn.take()

            def bc(v, shape):
                return v.broadcast_to(shape)

            for l in range(DEPTH):
                pt, free = T_in()
                V.tensor_copy(cols[:, l, 0:ROWS], pt[:, 0:ROWS]).then_inc(cols_ready, 1)
                dve.drain().then_inc(free, 1)

            dve.wait_ge(csilu_ready, 1)
            dve.wait_ge(cols_ready, DEPTH)
            ada_b = Turn()
            for l in range(DEPTH):
                bv = b.A.take()
                with rounds(dve, 0, 2, {b.raw_in: ADA, b.raw: ADA, ada_b: ADA // 2, b.link: 6 * ADA // 2}) as r:
                    for j in range(ADA // 2):
                        n = ada_b.take()
                        if j >= 2:
                            dve.wait_ge(ada_summed, ada_b.done(n - 2))
                        for c in range(2):
                            g = b.raw_in.take()
                            b.raw.take()
                            s = raw[b.raw_in.slot(g)]
                            dve.wait_ge(landed[b.raw_in.slot(g)], (b.raw_in.before(g) + 1) * 16)
                            for k in range(CK):
                                src, sc = s[:, k * W:(k + 1) * W], csilu[:, c * CK + k:c * CK + k + 1]
                                if c + k == 0:
                                    ins = V.tensor_scalar(acc[j % 2][:, :], src, sc, None, ALU.mult)
                                else:
                                    ins = V.scalar_tensor_tensor(acc[j % 2][:, :], src, sc, acc[j % 2][:, :], ALU.mult, ALU.add)
                                if k == CK - 1:
                                    ins.then_inc(raw_done, 1)
                                    dve.wait_ge(raw_done, b.raw_in.done(g))
                                else:
                                    v = b.link.take()
                                    ins.then_inc(dve_link, 1)
                                    dve.wait_ge(dve_link, b.link.done(v))
                    dve.wait_ge(ada_summed, ada_b.done(n))
                link_n[0] = b.link.n
                link(V.tensor_tensor(mod[:, l, :], pA[b.A.slot(bv)][:, 0:48], cols[:, l, R_ADAB:R_ADAB + 48], ALU.add))
                for at, w in ((8, R_NMIX), (32, R_NFFN)):
                    ins = V.scalar_tensor_tensor(mod[:, l, at:at + 8], mod[:, l, at:at + 8], 1.0, cols[:, l, w:w + 8], ALU.add, ALU.mult)
                    link(ins)
                dve.drain().then_inc(A_free[b.A.slot(bv)], 1)
                b.link.n = link_n[0]
            dve.wait_ge(small_in, SMALL)

            n_rt, n_hi, n_aT, n_go = [0], [0], [0], [0]

            def normalise():
                for t in range(TT):
                    link(V.tensor_tensor_reduce(y[:, t, :], x[:, t, :], x[:, t, :], 1.0, 0.0, ALU.mult, ALU.add, nrm[:, 6 + t:7 + t]))
                V.tensor_scalar(nrm[:, 0:2], nrm[:, 6:8], 1.0 / D, EPS, ALU.mult, ALU.add).then_inc(ms_ready, 1)
                n_rt[0] += 1
                dve.wait_ge(rt_ready, n_rt[0])
                link(V.reciprocal(nrm[:, 4:6], nrm[:, 2:4]))
                for t in range(TT):
                    ins = V.tensor_scalar(y[:, t, :], x[:, t, :], nrm[:, 4 + t:5 + t], None, ALU.mult)
                return ins

            def modulate(l, which, both):
                sc, sh = (which * 24 + 8, which * 24)
                for q in range(4):
                    pt, free = T_in()
                    for j in range(2):
                        k = 2 * q + j
                        ins = V.tensor_scalar(hf[:, k, :], pt[:, j * SEQ:(j + 1) * SEQ], mod[:, l, sc + k:sc + k + 1],
                                              mod[:, l, sh + k:sh + k + 1], ALU.mult, ALU.add)
                        if j == 0:
                            pass
                    ins.then_inc(hf_ready, 1)
                    dve.drain().then_inc(free, 1)
                    if both:
                        n_hi[0] += 1
                        dve.wait_ge(h_hi_ready, n_hi[0])
                        V.tensor_tensor(h_lo[:, 2 * q:2 * q + 2, :], hf[:, 2 * q:2 * q + 2, :],
                                        h_hi[:, 2 * q:2 * q + 2, :].bitcast(F32), ALU.subtract).then_inc(h_ready, 1)

            def scores(c, l):
                kind, g = CALLS[c]
                s, st = S[c % 2], stat[:, (c % 2) * 40:(c % 2) * 40 + 40]
                skip(b.T, {"cmp": 2, "sel": 1, "win": 1, "ret": 4, "fox": 4}[kind])
                if kind == "ret":
                    for p0 in range(0, HG, 2):
                        pa, free = A_in()
                        V.tensor_tensor(s[:, p0 * SEQ:(p0 + 2) * SEQ], pa[:, :], decay[:, p0:p0 + 2, :].rearrange("p h n -> p (h n)"), ALU.mult).then_inc(free, 1)
                    pa, free = A_in()
                    link(V.tensor_tensor(s[:, 4 * SEQ:4 * SEQ + 4 * P].rearrange("p (h n) -> p h n", h=HG),
                                         pa[:, :].rearrange("p (h n) -> p h n", h=HG), decay[:, :, 0:P], ALU.mult))
                    dve.drain().then_inc(free, 1)
                    dve.drain().then_inc(s_ready, 1)
                    return
                if kind == "cmp":
                    pa, free = A_in()
                    sv = s[:, 0:P].rearrange("p (r n) -> p r n", n=16)[:, :, 0:NCMP]
                    cm = cmask.rearrange("p t h n -> p (t h) n")[:, :, 0:NCMP]
                    link(V.memset(s[:, 0:P], 0.0))
                    V.tensor_tensor(sv, pa[:, 0:P].rearrange("p (r n) -> p r n", n=16)[:, :, 0:NCMP], cm, ALU.add).then_inc(free, 1)
                    v = b.A.n - 1
                    dve.wait_ge(free, b.A.before(v) + 1)
                    link(V.tensor_reduce(st[:, 0:8], sv, AX_X, ALU.max))
                    V.tensor_tensor(sv, sv, bc(st[:, 0:8].unsqueeze(2), [P, 8, NCMP]), ALU.subtract).then_inc(s_ready, 1)
                    return
                for t in range(TT):
                    w = (t + 1) * P
                    for i in range(t + 1):
                        nh = HG // (t + 1)
                        pa, free = A_in()
                        at = HG * P * t + i * nh * w
                        dst = s[:, at:at + nh * w].rearrange("p (h n) -> p h n", h=nh)
                        mk = mask[:, 2 * P - w:2 * P].unsqueeze(1)
                        V.tensor_tensor(dst, pa[:, 0:nh * w].rearrange("p (h n) -> p h n", h=nh), bc(mk, [P, nh, w]), ALU.add).then_inc(free, 1)
                        v = b.A.n - 1
                        dve.wait_ge(free, b.A.before(v) + 1)
                    sv = s[:, HG * P * t:HG * P * t + HG * w].rearrange("p (h n) -> p h n", h=HG)
                    link(V.tensor_reduce(st[:, t * HG:(t + 1) * HG], sv, AX_X, ALU.max))
                    V.tensor_scalar(st[:, 8 + t * HG:8 + (t + 1) * HG], st[:, t * HG:(t + 1) * HG], -SCALE, None, ALU.mult).then_inc(s_ready, 1)

            def values(c, l):
                kind, g = CALLS[c]
                st = stat[:, (c % 2) * 40:(c % 2) * 40 + 40]
                s = S[c % 2]
                skip(b.T, {"cmp": 2, "sel": 3, "win": 3, "ret": 0, "fox": 3}[kind])
                if kind == "ret":
                    for t in range(TT):
                        po, free = O_in()
                        for h in range(HG):
                            link(V.bn_stats(fox_st[:, h * 6:(h + 1) * 6], po[:, h * P:(h + 1) * P]))
                            link(V.bn_aggr(ret_st[:, h * 2:h * 2 + 2], fox_st[:, h * 6:(h + 1) * 6]))
                        mv = ret_st[:, 0:8].rearrange("p (h s) -> p h s", s=2)
                        V.tensor_scalar(ret_st[:, 8:12], mv[:, :, 1], EPS, None, ALU.add).then_inc(var_ready, 1)
                        dve.wait_ge(dev_ready, TT * l + t + 1)
                        link(V.reciprocal(ret_st[:, 16:20], ret_st[:, 12:16]))
                        for h in range(HG):
                            link(V.tensor_scalar(o_sb[:, t, h * P:(h + 1) * P], po[:, h * P:(h + 1) * P], ret_st[:, 2 * h:2 * h + 1],
                                                 ret_st[:, 16 + h:17 + h], ALU.subtract, ALU.mult))
                        dve.drain().then_inc(free, 1)
                        link(V.tensor_tensor(o_sb[:, t, :], o_sb[:, t, :], proj[:, t, C_RG:C_RG + W], ALU.mult))
                    dve.drain().then_inc(o_ready, 1)
                    return
                p_at = P_SIGNALS * l + sum(P_COUNT[k] for k, _ in CALLS[:c])
                if kind == "cmp":
                    dve.wait_ge(p_ready, p_at + 1)
                    sv = s[:, 0:P].rearrange("p (r n) -> p r n", n=16)[:, :, 0:NCMP]
                    link(V.tensor_reduce(st[:, 16:24], sv, AX_X, ALU.add))
                else:
                    dve.wait_ge(p_ready, p_at + 2)
                link(V.reciprocal(st[:, 24:32], st[:, 16:24]))
                coef = st[:, 24:32]
                if kind != "fox":
                    coef = st[:, 32:40]
                    branch = {"cmp": 0, "sel": 1, "win": 2}[kind]
                    cv = coef.rearrange("p (t h) -> p t h", t=TT)
                    link(V.tensor_tensor(cv, st[:, 24:32].rearrange("p (t h) -> p t h", t=TT),
                                         gates3[:, :, branch * 8 + g * HG:branch * 8 + (g + 1) * HG], ALU.mult))
                    if kind == "cmp":
                        link(V.tensor_tensor(cv, cv, bc(cvalid.unsqueeze(2), [P, TT, HG]), ALU.mult))
                for t in range(TT):
                    po, free = O_in()
                    src = po[:, 0:HG * HD].rearrange("p (h d) -> p h d", h=HG)
                    dst = o_sb[:, t, g * HG * HD:(g + 1) * HG * HD].rearrange("p (h d) -> p h d", h=HG)
                    cf = bc(coef[:, t * HG:(t + 1) * HG].unsqueeze(2), [P, HG, HD])
                    if kind in ("cmp", "fox"):
                        V.tensor_tensor(dst, src, cf, ALU.mult).then_inc(free, 1)
                        dve.wait_ge(free, b.O.before(b.O.n - 1) + 1)
                    else:
                        part = o_part[:, :].rearrange("p (h d) -> p h d", h=HG)
                        V.tensor_tensor(part, src, cf, ALU.mult).then_inc(free, 1)
                        dve.wait_ge(free, b.O.before(b.O.n - 1) + 1)
                        link(V.tensor_tensor(dst, dst, part, ALU.add))
                if c in WHOLE:
                    dve.drain().then_inc(o_ready, 1)

            for l in range(DEPTH):
                normalise().then_inc(y_ready, 1)
                modulate(l, 0, True)
                split(AHEAD)
                with rounds(dve, 0, WBLK // 3, {b.raw: 6, b.hl: 6, b.raw_in: 6, b.hl_in: 6, b.A: 4, b.O: 2}) as r:
                    for j in range(3):
                        split(2)
                        v = used(2)
                        for t in range(TT):
                            src, free = O_in(v) if j == 2 else A_in(v)
                            V.tensor_copy(proj[:, t, bass.ds(r * (3 * W) + j * W, W)], src[:, :]).then_inc(free, 1)
                dve.drain().then_inc(proj_ready, 1)
                z = fox[:, 0, :].rearrange("p (t h) -> p t h", t=TT)
                dve.wait_ge(proj_ready, l + 1)
                link(V.tensor_tensor(z, proj[:, :, C_FF:C_FF + 8], bc(fbias[:, l, :].unsqueeze(1), [P, TT, 8]), ALU.add))
                link(V.tensor_scalar(fox[:, 1, :], fox[:, 0, :], -1.0, None, ALU.mult))
                V.tensor_tensor(fox[:, 1, :], fox[:, 1, :], fox[:, 0, :], ALU.min).then_inc(z_ready, 1)
                b.T.take()
                dve.wait_ge(T_free[b.T.slot(b.T.n - 1)], b.T.before(b.T.n - 1) + 1)
                V.memset(win_hi[:, :, 480:578].bitcast(F32), 0.0)
                V.memset(win_lo[:, :, 480:578].bitcast(F32), 0.0)
                for kv in range(2):
                    for g in range(2):
                        for jh in range(2):
                            v = kk[:, 2 * kv + g, :].rearrange("p (m j s) -> p s j m", j=8, s=2)[:, 0, :, jh:jh + NCMP]
                            pe_c = cols[:, l, R_PEK + 16 * kv + 8 * jh:R_PEK + 16 * kv + 8 * jh + 8].unsqueeze(2)
                            ins = V.tensor_tensor(win[:, kv, 8 * jh:8 * jh + 8, g, :], v, bc(pe_c, [P, 8, NCMP]), ALU.add)
                ins.then_inc(win_ready, 1)
                dve.wait_ge(win_hi_ready, l + 1)
                V.tensor_tensor(win_lo[:, :, 0:480], win[:, :, :, :, :].rearrange("p v j g n -> p v (j g n)"),
                                win_hi[:, :, 0:480].bitcast(F32), ALU.subtract).then_inc(win_lo_ready, 1)
                split(4 - AHEAD)
                used(4)
                skip(b.A, 2)
                b.T.take()
                dve.wait_ge(e_ready, l + 1)
                V.scalar_tensor_tensor(fox[:, 3, :], fox[:, 0, :], 0.0, fox[:, 2, :], ALU.min, ALU.subtract).then_inc(ls_ready, 1)
                po, free = O_in()
                V.tensor_copy(kcT[0:HD, 0:30], po[0:HD, 0:30])
                V.tensor_copy(vc[0:NCMP, :, :], po[0:NCMP, HD:3 * HD].rearrange("p (g d) -> p g d", g=2)).then_inc(free, 1)
                po, free = O_in()
                cs = po[:, 0:16].rearrange("p (t h) -> p t h", t=TT)
                V.tensor_scalar(cum[:, :, :, 0], cs, 1.0 / SCALE, None, ALU.mult)
                link(V.tensor_scalar(cum[:, :, :, 1], cs, -1.0 / SCALE, None, ALU.mult))
                dve.drain().then_inc(free, 1)
                dve.drain().then_inc(cum_ready, 1)
                dve.wait_ge(sig_ready, l + 1)
                for c in range(len(CALLS) + 1):
                    if c < len(CALLS):
                        scores(c, l)
                    if c:
                        values(c - 1, l)
                        if c - 1 in WHOLE:
                            m = WHOLE[c - 1]
                            for q in range(2):
                                pt, free = T_in()
                                dve.wait_ge(oT_hi_ready, 6 * l + 2 * m + q + 1)
                                V.tensor_tensor(oT_lo[m][:, 2 * q:2 * q + 2, :], pt[:, :].rearrange("p (k n) -> p k n", k=2),
                                                oT_hi[m][:, 2 * q:2 * q + 2, :].bitcast(F32), ALU.subtract).then_inc(oT_ready, 1)
                                dve.drain().then_inc(free, 1)
                split(AHEAD)
                for half in range(2):
                    for m in range(3):
                        split(2)
                        v = used(2)
                        skip(b.A, 2)
                        split(1)
                        v = used(1)
                        n_go[0] += 1
                        for t in range(TT):
                            pa, free = A_in(v)
                            if t == 0:
                                dve.wait_ge(A_free[b.A.slot(b.A.n - 2)], b.A.before(b.A.n - 2) + 1)
                            dst = merged[t][:, half * W:(half + 1) * W]
                            if m == 0:
                                V.tensor_tensor(dst, pa[:, :], gate[:, t, :], ALU.mult).then_inc(free, 1)
                            else:
                                V.tensor_tensor(tmp[:, :], pa[:, :], gate[:, t, :], ALU.mult).then_inc(free, 1)
                                dve.wait_ge(free, b.A.before(b.A.n - 1) + 1)
                                link(V.tensor_tensor(dst, dst, tmp[:, :], ALU.add))
                        dve.drain().then_inc(g_used, 1)
                dve.drain().then_inc(merged_ready, 1)
                for q in range(4):
                    pt, free = T_in()
                    n_hi[0] += 1
                    dve.wait_ge(h_hi_ready, n_hi[0])
                    V.tensor_tensor(h_lo[:, 2 * q:2 * q + 2, :], pt[:, :].rearrange("p (k n) -> p k n", k=2),
                                    h_hi[:, 2 * q:2 * q + 2, :].bitcast(F32), ALU.subtract).then_inc(h_ready, 1)
                    dve.drain().then_inc(free, 1)

                def gate_rows():
                    for half in range(2):
                        pa, free = A_in()
                        V.tensor_copy(gw[:, half * W:(half + 1) * W], pa[:, :]).then_inc(free, 1)
                        dve.wait_ge(free, b.A.before(b.A.n - 1) + 1)
                gate_rows()
                for half in range(2):
                    split(2 - half * AHEAD)
                    v = used(2)
                    for t in range(TT):
                        pa, free = A_in(v)
                        V.tensor_tensor(tmp[:, :], pa[:, :], gw[:, half * W:(half + 1) * W], ALU.mult).then_inc(free, 1)
                        dve.wait_ge(free, b.A.before(b.A.n - 1) + 1)
                        link(V.tensor_tensor(x[:, t, half * W:(half + 1) * W], x[:, t, half * W:(half + 1) * W], tmp[:, :], ALU.add))
                normalise().then_inc(y_ready, 1)
                if l % 2 == 0:
                    modulate(l, 1, True)
                    link(V.memset(yacc[:, :, :], 0.0))
                    split(AHEAD)
                    av, aq = Turn(), Turn()

                    def hidden(width=W):
                        v = av.take()
                        dve.wait_ge(g_free, av.done(v))
                        dve.wait_ge(chunk_used, b.hl.done(b.hl.n - 1))
                        for t in range(TT):
                            ins = V.tensor_tensor(a_sb[:, t, 0:width], a_sb[:, t, 0:width], pA[2 + t][:, 0:width], ALU.mult)
                        ins.then_inc(a_ready, 1)
                        dve.drain().then_inc(u_free, 1)

                    def lo_a(n):
                        for q in range(n):
                            pt, free = T_in()
                            v = aq.take()
                            dve.wait_ge(aT_hi_ready, aq.done(v))
                            V.tensor_tensor(aT_lo[:, 2 * q:2 * q + 2, :], pt[:, :].rearrange("p (k n) -> p k n", k=2),
                                            aT_hi[:, 2 * q:2 * q + 2, :].bitcast(F32), ALU.subtract).then_inc(free, 1)

                    def add_down(t, half, chunk=None):
                        po, free = O_in(chunk)
                        dst = yacc[:, t, half * W:(half + 1) * W]
                        V.tensor_tensor(dst, dst, po[:, :], ALU.add).then_inc(free, 1)

                    def down():
                        for half in range(2):
                            split(1)
                            v = used(1)
                            add_down(0, half)
                            add_down(1, half, v)
                    split(2)
                    used(2)
                    split(2)
                    used(2)
                    hidden()
                    with rounds(dve, 1, FFB, {b.raw: 6, b.hl: 6, b.raw_in: 6, b.hl_in: 6, b.T: 2, b.O: 4, b.Of: 2, av: 1, aq: 2}):
                        split(2)
                        used(2)
                        lo_a(2)
                        split(2)
                        used(2)
                        hidden()
                        down()
                    split(1)
                    used(1)
                    lo_a(2)
                    split(1)
                    used(1)
                    hidden(W // 2)
                    down()
                    lo_a(1)
                    split(1 - AHEAD)
                    v = used(1)
                    for i in range(4):
                        add_down(i % 2, i // 2, v if i == 3 else None)
                    dve.wait_ge(O_free[0], b.O.n // 2)
                    dve.wait_ge(O_free[1], b.O.n // 2)
                    gate_rows()
                else:
                    modulate(l, 1, False)
                    pa, free = A_in()
                    r = lambda i: rs[:, i, :]
                    te = lambda i: rs[:, i, :].rearrange("p (t e) -> p t e", t=TT)
                    V.tensor_copy(r(1), pa[:, 0:TT * NE]).then_inc(free, 1)
                    dve.wait_ge(free, b.A.before(b.A.n - 1) + 1)
                    link(V.tensor_reduce(r(3)[:, 0:TT], te(1), AX_X, ALU.max))
                    V.tensor_tensor(te(2), te(1), bc(r(3)[:, 0:TT].unsqueeze(2), [P, TT, NE]), ALU.subtract).then_inc(log_ready, 1)
                    for t in range(TT):
                        other = bc(te(1)[:, t, :].unsqueeze(1), [P, NE, NE])
                        own = bc(te(1)[:, t, :].unsqueeze(2), [P, NE, NE])
                        link(V.tensor_tensor(rt[:, t, :, :], other, own, ALU.is_equal))
                        link(V.tensor_tensor(rt[:, t, :, :], rt[:, t, :, :], ties, ALU.mult))
                        link(V.tensor_tensor(rt2[:, :, :], other, own, ALU.is_gt))
                        link(V.tensor_tensor(rt[:, t, :, :], rt[:, t, :, :], rt2[:, :, :], ALU.add))
                    link(V.tensor_reduce(te(4), rt[:, :, :, :], AX_X, ALU.add))
                    V.tensor_scalar(r(0), r(4), 2.0, None, ALU.is_lt).then_inc(sel_ready, 1)
                    dve.wait_ge(sel_ready, 1)
                    dve.wait_ge(re_ready, 1)
                    link(V.tensor_tensor(r(5), r(2), r(0), ALU.mult))
                    link(V.tensor_reduce(r(6)[:, 0:TT], te(5), AX_X, ALU.add))
                    link(V.reciprocal(r(7)[:, 0:TT], r(6)[:, 0:TT]))
                    for i in range(2):
                        link(V.tensor_tensor(gate16[:, :, i * NE:(i + 1) * NE], te(5), bc(r(7)[:, 0:TT].unsqueeze(2), [P, TT, NE]), ALU.mult))
                    pa, free = A_in()
                    link(V.tensor_tensor(te(8), pa[:, 0:2 * NE].rearrange("p (t e) -> p t e", t=TT), te(0), ALU.mult))
                    link(V.tensor_scalar(slot16[:, :, 0:NE], te(8), -1.0, None, ALU.add))
                    link(V.tensor_scalar(slot16[:, :, NE:2 * NE], te(8), -1.0 - P, None, ALU.add))
                    link(V.tensor_reduce(r(9)[:, 0:1], pa[:, 2 * NE:3 * NE], AX_X, ALU.max))
                    dve.drain().then_inc(free, 1)
                    link(V.tensor_scalar(r(9)[:, 1:2], r(9)[:, 0:1], float(P), float(NE), ALU.is_gt, ALU.mult))
                    link(V.tensor_scalar(flag[:, 0:1], r(9)[:, 1:2], float(NE), None, ALU.add))
                    gate_rows()
                    link(V.memset(yacc[:, :, :], 0.0))
                    dve.drain().then_inc(slots_ready, 1)
                    items = dve.value_load(flag[0:1, 0:1], min_val=NE, max_val=2 * NE)
                    av, aq, xv = Turn(start=FFB + 1), Turn(start=2 * FFB + 1), Turn()
                    with rounds(dve, 0, items, {b.raw: 42, b.hl: 42, b.raw_in: 42, b.hl_in: 42, b.T: 22, b.O: 2, av: EFB, aq: 2 * EFB, xv: 1}) as e:
                        xe = xv.take()
                        for t in range(TT):
                            ins = V.tensor_scalar(sel[:, t, :], iota, slot16[:, t, bass.ds(e, 1)], None, ALU.is_equal)
                        ins.then_inc(sel_ready, 1)
                        split(AHEAD)
                        for q in range(2):
                            pt, free = T_in()
                            for j in range(4):
                                k = 4 * q + j
                                ins = V.tensor_scalar(x_f[:, k, :], pt[:, j * P:(j + 1) * P], mod[:, l, 32 + k:33 + k],
                                                      mod[:, l, 24 + k:25 + k], ALU.mult, ALU.add)
                            ins.then_inc(xf_ready, 1)
                            dve.drain().then_inc(free, 1)
                        for q in range(2):
                            dve.wait_ge(x_hi_ready, xv.done(xe, 2) - 1 + q)
                            V.tensor_tensor(x_lo[:, 4 * q:4 * q + 4, :], x_f[:, 4 * q:4 * q + 4, :],
                                            x_hi[:, 4 * q:4 * q + 4, :].bitcast(F32), ALU.subtract).then_inc(x_ready, 1)
                        skip(b.T, 2)

                        def hidden():
                            v = av.take()
                            dve.wait_ge(g_free, av.done(v))
                            dve.wait_ge(chunk_used, b.hl.done(b.hl.n - 1))
                            V.tensor_tensor(a_sb[:, 0, :], a_sb[:, 0, :], pA[2][:, :], ALU.mult).then_inc(a_ready, 1)
                            dve.drain().then_inc(u_free, 1)

                        def lo_a():
                            for q in range(2):
                                pt, free = T_in()
                                v = aq.take()
                                dve.wait_ge(aT_hi_ready, aq.done(v))
                                V.tensor_tensor(aT_lo[:, 2 * q:2 * q + 2, 0:P], pt[:, 0:SEQ].rearrange("p (k n) -> p k n", k=2),
                                                aT_hi[:, 2 * q:2 * q + 2, 0:P].bitcast(F32), ALU.subtract).then_inc(free, 1)
                        split(4)
                        used(4)
                        hidden()
                        with rounds(dve, 1, EFB, {b.raw: 6, b.hl: 6, b.raw_in: 6, b.hl_in: 6, b.T: 2, av: 1, aq: 2}):
                            split(2)
                            used(2)
                            lo_a()
                            split(2)
                            used(2)
                            hidden()
                            split(2)
                            used(2)
                        lo_a()
                        split(2 - AHEAD)
                        v = used(2)
                        for half in range(2):
                            po, free = O_in(v)
                            V.tensor_copy(oe[:, half * W:(half + 1) * W], po[:, :]).then_inc(free, 1)
                        for t in range(TT):
                            for half in range(2):
                                pt, free = T_in()
                                dst = yacc[:, t, half * W:(half + 1) * W]
                                V.scalar_tensor_tensor(dst, pt[:, :], gate16[:, t, bass.ds(e, 1)], dst, ALU.mult, ALU.add).then_inc(free, 1)
                    link(dve.drain())
                for t in range(TT):
                    for half in range(2):
                        c = slice(half * W, (half + 1) * W)
                        link(V.tensor_tensor(yacc[:, t, c], yacc[:, t, c], gw[:, c], ALU.mult))
                        link(V.tensor_tensor(x[:, t, c], x[:, t, c], yacc[:, t, c], ALU.add))
            link(normalise())
            dve.wait_ge(late_in, 16)
            for t in range(TT):
                ins = V.tensor_tensor(y[:, t, :], y[:, t, :], gw[:, :], ALU.mult)
            ins.then_inc(fin_ready, 1)


NAMES = ["x", "c", "ada_w", "ada_b", "norm_mix", "norm_ffn", "w_in", "cmp_k_pe", "cmp_k_w1", "cmp_k_w2", "cmp_v_pe",
         "cmp_v_w1", "cmp_v_w2", "fox_f_bias", "w_read_nsa", "w_read_ret", "w_read_fox", "w_out", "ffn_w1", "ffn_w3",
         "ffn_w2", "router_w", "moe_w1", "moe_w3", "moe_w2", "final_norm"]


def kernel(**inputs):
    import concourse.bacc as bacc
    from concourse.bass_utils import run_bass_kernel_spmd

    nc = bacc.Bacc("TRN2", target_bir_lowering=False, num_devices=1)
    arrays, aps = {}, {}
    for name in NAMES:
        v = np.ascontiguousarray(inputs[name])
        arrays[f"in_{name}"] = v
        aps[name] = nc.dram_tensor(f"in_{name}", v.shape, mybir.dt.from_np(v.dtype), kind="ExternalInput").ap()
    arrays["in_tables"] = tables()
    table = nc.dram_tensor("in_tables", (P, TABLE_W), F32, kind="ExternalInput").ap()
    out = nc.dram_tensor("out_0", (1, SEQ, D), F32, kind="ExternalOutput").ap()
    build(nc, aps, table, out)
    return run_bass_kernel_spmd(nc, [arrays], core_ids=[0]).results[0]["out_0"]
```

```python
from contextlib import ExitStack, contextmanager

import numpy as np
import concourse.bass as bass
from concourse import mybir

F32 = mybir.dt.float32
F32R = mybir.dt.float32r
I32 = mybir.dt.int32
BF16 = mybir.dt.bfloat16
ALU = mybir.AluOpType
ACT = mybir.ActivationFunctionType
AX_X = mybir.AxisListType.X

P = 128
D = 1024
KB = D // P
SEQ = 256
TT = SEQ // P
DEPTH = 2
HD = 64
EPS = 1e-6
NEG = -1e30
SCALE = HD ** -0.5
HG = 4
D_IN = 7456
C_NQ, C_NKC, C_NVC, C_NKS, C_NVS, C_NKW, C_NVW, C_NG = 0, 512, 640, 768, 896, 1024, 1152, 1280
C_RQ, C_RK, C_RV, C_RG = 1304, 1560, 1816, 2328
C_FQ, C_FK, C_FV, C_FF, C_MG = 2840, 3352, 3864, 4376, 4384

CMP_LEN, CMP_STRIDE, CMP_HID = 32, 16, 256
NCMP = (SEQ - CMP_LEN) // CMP_STRIDE + 1
FF = 2816
FFE = 3584
NE = 8
W = 512
CK = 4
CHUNK = CK * W
RAW = 6
HALF = CHUNK // 2
HL = 4
AHEAD = HL - 1
ADA = 6 * D // W
WBLK = 9
PROJ = WBLK * W
assert PROJ >= C_MG and WBLK % 3 == 0
FFB = FF // W
EFB = FFE // W
assert FF == FFB * W + W // 2 and FFE == EFB * W

FIRST = 4
BEHIND_ROUND = (0, 1, 1, 2, 1, 1)
BEHIND_LAST = (0, 1, 1, 1, 1, 0)
BEHIND_MERGE = (0, 1, 1)
BEHIND_DENSE = (0, 1, 1, 0, 1, 0, 0, 1, 1, 0, 1, 0)
IN_MERGE = ADA // 2
assert FFB % 2 and IN_MERGE == 6
_all = list(BEHIND_ROUND) * (WBLK // 3 - 1) + list(BEHIND_LAST) + [0] * 4 + list(BEHIND_MERGE) * 6 + [0] * 8 + list(BEHIND_DENSE) * (FFB // 2)
BEHIND = dict(enumerate(_all))
assert 2 * FIRST + sum(BEHIND.values()) == 2 * ADA * DEPTH

TABLES = {}
_at = 0
for _n, _w in (("ident", P), ("tri", P), ("ones", P), ("iota", P), ("mask", 2 * P), ("cmask", 2 * 2 * 4 * 16),
               ("cvalid", 2), ("rope", 2 * 2 * HD), ("decay", 4 * 2 * P), ("ties", NE * NE)):
    TABLES[_n] = (_at, _w)
    _at += _w
TABLE_W = _at

R_ADAB, R_NMIX, R_NFFN, R_PEK, R_PEV, R_C = 0, 48, 56, 64, 80, 96
ROWS = 104


def tables():
    f = np.float32
    t = np.zeros((P, TABLE_W), f)

    def put(name, a):
        at, w = TABLES[name]
        t[:, at:at + w] = np.asarray(a, f).reshape(P, w)

    i = np.arange(P)
    put("ident", np.eye(P))
    put("tri", i[:, None] <= i[None, :])
    put("ones", np.ones((P, P)))
    put("iota", np.broadcast_to(i, (P, P)))
    causal = np.where(i[None, :] <= i[:, None], 0.0, NEG)
    put("mask", np.concatenate([np.zeros((P, P)), causal], 1))
    tok = np.arange(SEQ).reshape(TT, P)
    end = np.arange(16) * CMP_STRIDE + CMP_LEN - 1
    open_ = (end[None, None, :] <= tok[:, :, None]) & (np.arange(16) < NCMP)
    cm = np.where(open_, 0.0, NEG).transpose(1, 0, 2)[:, :, None, :]
    cm = np.broadcast_to(cm, (P, TT, HG, 16))
    put("cmask", np.stack([cm, cm], 1))
    put("cvalid", open_.any(-1).T)
    inv = f(10000.0) ** (-np.arange(0, HD, 2, dtype=f) / f(HD))
    ang = np.arange(SEQ, dtype=f)[:, None] * inv[None, :]
    cos = np.concatenate([np.cos(ang)] * 2, 1)
    sin = np.concatenate([-np.sin(ang), np.sin(ang)], 1)
    put("rope", np.stack([cos.reshape(TT, P, HD), sin.reshape(TT, P, HD)], 0).transpose(2, 0, 1, 3))
    log_g = np.log(f(1.0) - f(2.0) ** (f(-5.0) - np.arange(4, dtype=f)))
    diff = (np.arange(2 * P)[None, :] - i[:, None]).astype(f)
    dec = np.where(diff[:, None, :] >= 0, np.exp(np.maximum(diff, 0)[:, None, :] * log_g[None, :, None]), 0.0)
    put("decay", dec * f(SCALE))
    put("ties", np.broadcast_to(np.tril(np.ones((NE, NE)), -1), (P, NE, NE)))
    return t


class Turn:

    def __init__(self, size=1, start=0):
        self.size, self.n, self.loops = size, start, []

    def take(self):
        self.n += 1
        return self.n - 1

    def done(self, v, times=1):
        out = (v + 1) * times
        for reg, per in self.loops:
            out = reg * (per * times) + out
        return out

    def slot(self, v):
        return v % self.size

    def before(self, v):
        out = v // self.size
        for reg, per in self.loops:
            out = reg * (per // self.size) + out
        return out


@contextmanager
def rounds(eng, first, end, turns):
    at = [t.n for t in turns]
    with eng.Fori(first, end) as reg:
        for t, per in turns.items():
            assert per % t.size == 0
            t.loops.append((reg - first if first else reg, per))
        yield reg
        for t, n in zip(turns, at):
            assert t.n == n + turns[t], (t.n - n, turns[t])
            t.loops.pop()
    if isinstance(end, int):
        for t, n in zip(turns, at):
            t.n = n + turns[t] * (end - first)


class Books:

    def __init__(self):
        self.raw, self.ada = Turn(RAW), Turn()
        self.hl, self.hl_in = Turn(HL), Turn(HL)
        self.end = 0
        self.A, self.T, self.O = Turn(4), Turn(2), Turn(2)
        self.Af, self.Of = Turn(), Turn()
        self.link = Turn()


CALLS = [("cmp", 0), ("sel", 0), ("win", 0), ("cmp", 1), ("sel", 1), ("win", 1), ("ret", 0), ("fox", 0), ("fox", 1)]
WHOLE = {5: 0, 6: 1, 8: 2}
S_COUNT = {"cmp": 1, "sel": 2, "win": 2, "ret": 1, "fox": 2}
P_COUNT = {"cmp": 1, "sel": 2, "win": 2, "ret": 0, "fox": 2}
S_SIGNALS = sum(S_COUNT[k] for k, _ in CALLS)
P_SIGNALS = sum(P_COUNT[k] for k, _ in CALLS)


def build(nc, a, table, out):
    ctx = ExitStack()
    with ctx:
        def sem(name):
            return ctx.enter_context(nc.semaphore(name))

        here = [(nc.sbuf_base + 63) // 64 * 64]

        def sb(name, shape, dt=F32, at=None):
            size = 4
            for s in shape[1:]:
                size *= s
            if dt == BF16:
                size //= 2
            off = here[0] if at is None else at
            t = nc.alloc_sbuf_tensor_at(name, shape, dt, offset=off)
            if at is None:
                here[0] += (size + 31) // 32 * 32
            return t

        raw = [sb(f"raw{i}", [P, CHUNK]) for i in range(RAW)]
        w_hi = [sb(f"w_hi{i}", [P, HALF], F32R) for i in range(HL)]
        w_lo = [sb(f"w_lo{i}", [P, HALF], F32R) for i in range(HL)]
        tab = sb("tab", [P, TABLE_W])
        x = sb("x", [P, TT, D])
        h_hi = sb("h_hi", [P, KB, SEQ], F32R)
        h_lo = sb("h_lo", [P, KB, SEQ], F32R)
        rows = [sb(f"rows{i}", [P, P]) for i in range(DEPTH)]
        cols = sb("cols", [P, DEPTH, P])
        csilu = sb("csilu", [P, KB])
        mod = sb("mod", [P, DEPTH, 48])
        small = sb("small", [P, 64])
        fbias = sb("fbias", [P, DEPTH, 8])
        w2c = sb("w2c", [P, DEPTH, 2, 2, HD])
        routw = sb("routw", [P, KB, NE])
        zeros = sb("zeros", [P, W], BF16)
        pool_mark = sb("pool_mark", [P, 4])
        gates3 = sb("gates3", [P, TT, 24])
        nrm = sb("nrm", [P, 16])
        flag = sb("flag", [P, 4], I32)
        oT_hi, oT_lo = [None] * 3, [None] * 3
        oT_hi[0] = sb("oTn_hi", [P, 4, SEQ], F32R)
        oT_lo[0] = sb("oTn_lo", [P, 4, SEQ], F32R)

        area = here[0]
        proj = sb("proj", [P, TT, PROJ])
        PR = PROJ * 4
        oT_hi[1] = sb("oTr_hi", [P, 4, SEQ], F32R, at=area)
        oT_lo[1] = sb("oTr_lo", [P, 4, SEQ], F32R, at=area + PR)
        oT_hi[2] = sb("oTf_hi", [P, 4, SEQ], F32R, at=area + C_RQ * 4 + 32)
        oT_lo[2] = sb("oTf_lo", [P, 4, SEQ], F32R, at=area + PR + C_RQ * 4 + 32)
        merged = [sb(f"merged{t}", [P, D], at=area + t * PR + C_FQ * 4) for t in range(TT)]
        work = here[0]
        qT = sb("qT", [P, HG, SEQ])
        kT = [sb(f"kT{i}", [P, HG, SEQ]) for i in range(2)]
        S = [sb(f"S{i}", [P, HG * 3 * P]) for i in range(2)]
        PT = sb("PT", [P, HG * 3 * P])
        o_sb = sb("o_sb", [P, TT, W])
        stat = sb("stat", [P, 96])
        fox_st = sb("fox_st", [P, 24])
        ret_st = sb("ret_st", [P, 20])
        o_part = sb("o_part", [P, HG * HD])
        end_work = here[0]
        acc = [sb(f"acc{i}", [P, W], at=work + 12288 + 2048 * i) for i in range(3)]
        y = sb("y", [P, TT, D], at=area + 4096)
        hf = sb("hf", [P, KB, SEQ], at=area + 12288)
        rope_t = sb("rope_t", [P, TT, 10, HD], at=work)
        kk = sb("kk", [P, 4, SEQ], at=work)
        win = sb("win", [P, 2, 16, 2, NCMP], at=work + 4096)
        win_hi = sb("win_hi", [P, 2, 16 * 30 + 98], F32R, at=work + 4096 + 4096)
        win_lo = sb("win_lo", [P, 2, 16 * 30 + 98], F32R, at=work + 4096 + 4096 + 4640)
        hid = sb("hid", [P, 2, CMP_HID], at=work + 17632)
        hidT = sb("hidT", [P, 4, 30], at=work + 19680)
        kcT = sb("kcT", [P, 32])
        vc = sb("vc", [P, 2, HD])
        q_aug = sb("q_aug", [P, TT, HG, HD + 2])
        k_aug = sb("k_aug", [P, TT, HG, HD + 2])
        cum = sb("cum", [P, TT, 8, 2])
        fox = sb("fox", [P, 4, TT * 8])
        assert here[0] <= nc.sbuf_usable_end
        gate = sb("gate", [P, TT, W], at=work)
        gw = sb("gw", [P, D], at=work + 24576)
        tmp = sb("tmp", [P, W], at=work + 8192)
        yacc = sb("yacc", [P, TT, D], at=area + 20480)
        a_sb = sb("a_sb", [P, TT, W], at=area + 28672)
        aT_hi = sb("aT_hi", [P, CK, SEQ], F32R, at=work)
        aT_lo = sb("aT_lo", [P, CK, SEQ], F32R, at=work + 4096)
        x_f = sb("x_f", [P, KB, P], at=work + 8192)
        x_hi = sb("x_hi", [P, KB, P], F32R, at=work + 12288)
        x_lo = sb("x_lo", [P, KB, P], F32R, at=work + 16384)
        oe = sb("oe", [P, D], at=area)
        sel = sb("sel", [P, TT, P], at=work + 20480)
        selT = sb("selT", [P, TT * P], at=work + 21504)
        rt = sb("rt", [P, TT, NE, NE], at=work + 22528)
        rt2 = sb("rt2", [P, NE, NE], at=work + 23040 + 640)
        rs = sb("rs", [P, 10, TT * NE], at=work + 23040)
        slot16 = sb("slot16", [P, TT, 2 * NE + 1])
        gate16 = sb("gate16", [P, TT, 2 * NE])
        assert work + 23040 + 10 * TT * NE * 4 <= end_work, (end_work - work)
        assert here[0] <= nc.sbuf_usable_end, (here[0], nc.sbuf_usable_end)

        def cst(name):
            at, w = TABLES[name]
            return tab[:, at:at + w]

        ident, tri, ones, iota = cst("ident"), cst("tri"), cst("ones"), cst("iota")
        mask = cst("mask")
        cmask = cst("cmask")[:, 0:TT * HG * 16].rearrange("p (t h n) -> p t h n", t=TT, h=HG)
        cvalid = cst("cvalid")
        rope = cst("rope").rearrange("p (s t d) -> p s t d", s=2, t=TT)
        decay = cst("decay").rearrange("p (h n) -> p h n", h=4)
        ties = cst("ties").rearrange("p (e j) -> p e j", e=NE)

        SMALL = 16 * (2 + DEPTH * 3 + 1)

        def bank(name):
            return ctx.enter_context(nc.psum_tensor(name, [P, W], F32))[:, :]
        pA = [bank(f"pA{i}") for i in range(4)]
        pT = [bank(f"pT{i}") for i in range(2)]
        pO = [bank(f"pO{i}") for i in range(2)]

        landed = [sem(f"landed{i}") for i in range(RAW)]
        hi_ready = sem("hi_ready")
        raw_done = sem("raw_done")
        half_used = sem("half_used")
        A_full = sem("A_full")
        T_full = sem("T_full")
        O_full = sem("O_full")
        A_free = [sem(f"A_free{i}") for i in range(4)]
        T_free = [sem(f"T_free{i}") for i in range(2)]
        O_free = [sem(f"O_free{i}") for i in range(2)]
        small_in = sem("small_in")
        rows_in = [sem(f"rows_in{i}") for i in range(DEPTH)]
        late_in = sem("late_in")
        cols_ready = sem("cols_ready")
        csilu_ready = sem("csilu_ready")
        consts = sem("consts")
        dve_link = sem("dve_link")
        act_link = sem("act_link")
        pool_link = sem("pool_link")
        ms_ready = sem("ms_ready")
        rt_ready = sem("rt_ready")
        y_ready = sem("y_ready")
        hf_ready = sem("hf_ready")
        h_hi_ready = sem("h_hi_ready")
        h_ready = sem("h_ready")
        proj_ready = sem("proj_ready")
        roped = sem("roped")
        kk_ready = sem("kk_ready")
        win_ready = sem("win_ready")
        win_hi_ready = sem("win_hi_ready")
        win_lo_ready = sem("win_lo_ready")
        hid_ready = sem("hid_ready")
        hidT_ready = sem("hidT_ready")
        kc_ready = sem("kc_ready")
        sig_ready = sem("sig_ready")
        z_ready = sem("z_ready")
        e_ready = sem("e_ready")
        ls_ready = sem("ls_ready")
        cum_ready = sem("cum_ready")
        aug_ready = sem("aug_ready")
        qk_ready = sem("qk_ready")
        s_ready = sem("s_ready")
        p_ready = sem("p_ready")
        pT_ready = sem("pT_ready")
        var_ready = sem("var_ready")
        dev_ready = sem("dev_ready")
        o_ready = sem("o_ready")
        oT_hi_ready = sem("oT_hi_ready")
        oT_ready = sem("oT_ready")
        g_ready = sem("g_ready")
        g_used = sem("g_used")
        merged_ready = sem("merged_ready")
        mT_hi_ready = sem("mT_hi_ready")
        mT_ready = sem("mT_ready")
        grow_ready = sem("grow_ready")
        g_free = sem("g_free")
        u_free = sem("u_free")
        silu_ready = sem("silu_ready")
        a_ready = sem("a_ready")
        aT_hi_ready = sem("aT_hi_ready")
        aT_ready = sem("aT_ready")
        log_ready = sem("log_ready")
        re_ready = sem("re_ready")
        sel_ready = sem("sel_ready")
        slots_ready = sem("slots_ready")
        selT_ready = sem("selT_ready")
        xf_ready = sem("xf_ready")
        x_hi_ready = sem("x_hi_ready")
        x_ready = sem("x_ready")
        oe_ready = sem("oe_ready")
        fin_ready = sem("fin_ready")
        stored = sem("stored")

        ctx.enter_context(nc.allow_non_contiguous_dma("small parameter loads"))
        block = ctx.enter_context(nc.Block())

        def chunk_rows(w, k0, c0, width=W, kb=CK):
            return w[bass.ds(k0, kb * P), bass.ds(c0, width)].rearrange("(k p) n -> p k n", p=P)

        @block.sync
        def _(sp):
            b = Books()

            def load(src, kb=CK):
                g = b.raw.take()
                slot = raw[b.raw.slot(g)]
                if g >= RAW or b.raw.loops:
                    sp.wait_ge(raw_done, b.raw.done(g - RAW, 2))
                sp.dma_start(slot[:, :].rearrange("p (k n) -> p k n", k=kb), src).then_inc(landed[b.raw.slot(g)], 16)

            def block8(w, c0):
                for k in range(KB // CK):
                    load(chunk_rows(w, k * CK * P, c0))

            sp.dma_start(tab[:, :], table).then_inc(small_in, 16)
            for l in range(DEPTH):
                for at, n, src in ((R_ADAB, 48, a["ada_b"][l].rearrange("(r p) -> r p", p=P)),
                                   (R_NMIX, 8, a["norm_mix"][l].rearrange("(r p) -> r p", p=P)),
                                   (R_NFFN, 8, a["norm_ffn"][l].rearrange("(r p) -> r p", p=P)),
                                   (R_PEK, 16, a["cmp_k_pe"][l].rearrange("(j s) d -> j (s d)", s=2)),
                                   (R_PEV, 16, a["cmp_v_pe"][l].rearrange("(j s) d -> j (s d)", s=2)),
                                   (R_C, 8, a["c"].rearrange("a (r p) -> (a r) p", p=P))):
                    sp.dma_start(rows[l][at:at + n, :], src).then_inc(rows_in[l], 16)
            sp.dma_start(x[:, :, :], a["x"][0].rearrange("(t p) d -> p t d", p=P)).then_inc(small_in, 16)
            for l in range(DEPTH):
                sp.dma_start(fbias[:, l, :], a["fox_f_bias"][l:l + 1, :].broadcast_to([P, 8])).then_inc(small_in, 16)
                for i, name in enumerate(("cmp_k_w2", "cmp_v_w2")):
                    sp.dma_start(w2c[:, l, i, :, :], a[name][l].rearrange("(k p) d -> p k d", p=P)).then_inc(small_in, 16)
            sp.dma_start(routw[:, :, :], a["router_w"][0].rearrange("(k p) e -> p k e", p=P)).then_inc(small_in, 16)

            def mixed(sources, behind, w, c0):
                n = 0
                for (src, *kb), m in zip(sources, behind):
                    load(src, *kb)
                    for _ in range(m):
                        load(chunk_rows(w, n % 2 * CK * P, c0 + n // 2 * W))
                        n += 1

            def in_round(l, r):
                return [(chunk_rows(a["w_in"][l], k * CK * P, r * (3 * W) + j * W),) for j in range(3) for k in range(2)]

            for j in range(FIRST):
                block8(a["ada_w"][0], j * W)
            for l in range(DEPTH):
                if l == 0:
                    last = WBLK // 3 - 1
                    with rounds(sp, 0, last, {b.raw: 12}) as r:
                        mixed(in_round(l, r), BEHIND_ROUND, a["ada_w"][0], FIRST * W + r * (3 * W))
                    mixed(in_round(l, last), BEHIND_LAST, a["ada_w"][0], (FIRST + 3 * last) * W)
                else:
                    with rounds(sp, 0, WBLK // 3, {b.raw: 6}) as r:
                        mixed(in_round(l, r), [0] * 6, None, 0)
                for name in ("cmp_k_w1", "cmp_v_w1"):
                    for half in range(2):
                        load(chunk_rows(a[name][l], half * 8 * P, 0, CMP_HID, 8), 8)
                for half in range(2):
                    for m, name in enumerate(("w_read_nsa", "w_read_ret", "w_read_fox")):
                        group = [(chunk_rows(a["w_in"][l], k * CK * P, C_MG + m * D + half * W),) for k in range(2)]
                        group.append((chunk_rows(a[name][l], 0, half * W),))
                        if l == 0:
                            mixed(group, BEHIND_MERGE, a["ada_w"][1], (3 * half + m) * W)
                        else:
                            mixed(group, [0] * 3, None, 0)
                for half in range(2):
                    block8(a["w_out"][l], half * W)
                if l % 2 == 0:
                    w1, w3, w2 = (a[n][l // 2] for n in ("ffn_w1", "ffn_w3", "ffn_w2"))
                    block8(w1, 0)
                    block8(w3, 0)
                    with rounds(sp, 0, FFB // 2, {b.raw: 18}) as r:
                        srcs = []
                        for f in (r * 2 + 1, r * 2 + 2):
                            srcs += [(chunk_rows(w, k * CK * P, f * W),) for w in (w1, w3) for k in range(2)]
                            srcs += [(chunk_rows(w2, f * W - W, half * W),) for half in range(2)]
                        mixed(srcs, BEHIND_DENSE, a["ada_w"][l + 1], IN_MERGE * W + r * (3 * W))
                    load(chunk_rows(w1, 0, FFB * W, W // 2, KB), KB)
                    load(chunk_rows(w3, 0, FFB * W, W // 2, KB), KB)
                    for half in range(2):
                        load(chunk_rows(w2, (FFB - 1) * W, half * W))
                    load(chunk_rows(w2, FFB * W, 0, D, 2), 2)
                else:
                    def experts():
                        with rounds(sp, 0, NE, {b.raw: EFB * 6}) as e:
                            w1, w3, w2 = (a[n][l // 2].rearrange("e k n -> (e k) n") for n in ("moe_w1", "moe_w3", "moe_w2"))

                            def up(f0):
                                for w in (w1, w3):
                                    for k in range(2):
                                        load(chunk_rows(w, e * D + k * CK * P, f0))

                            def down(f0):
                                for half in range(2):
                                    load(chunk_rows(w2, e * FFE + f0, half * W))
                            up(0)
                            with rounds(sp, 1, EFB, {b.raw: 6}) as f:
                                up(f * W)
                                down(f * W - W)
                            down((EFB - 1) * W)
                    experts()
                    sp.wait_ge(slots_ready, 1)
                    items = sp.value_load(flag[0:1, 0:1], min_val=NE, max_val=2 * NE)
                    with sp.If(items > NE):
                        experts()
            sp.wait_ge(ms_ready, 2 * DEPTH + 1)
            sp.dma_start(gw[:, :], a["final_norm"].unsqueeze(0).broadcast_to([P, D])).then_inc(late_in, 16)
            sp.wait_ge(fin_ready, 1)
            sp.dma_start(out[0].rearrange("(t p) d -> p t d", p=P), y[:, :, :]).then_inc(stored, 16)
            sp.wait_ge(stored, 16)

        marks = {}

        @block.tensor
        def _(pe):
            b = Books()

            def take(turn, free, banks):
                v = turn.take()
                if turn.loops or turn.before(v):
                    pe.wait_ge(free[turn.slot(v)], turn.before(v))
                return banks[turn.slot(v)]

            take_A = lambda: take(b.A, A_free, pA)
            take_T = lambda: take(b.T, T_free, pT)
            take_O = lambda: take(b.O, O_free, pO)

            def evacuated(turn, free, uses):
                for v in range(turn.n - min(uses, turn.size), turn.n):
                    pe.wait_ge(free[turn.slot(v)], turn.before(v) + 1)

            def mm3(dst, xh, xl, wh, wl, first, last):
                nc.tensor.matmul(dst, xl, wh, start=first, stop=False, skip_group_check=True)
                nc.tensor.matmul(dst, xh, wl, start=False, stop=False, skip_group_check=True)
                return nc.tensor.matmul(dst, xh, wh, start=False, stop=last, skip_group_check=True)

            def mm(dst, lhsT, rhs, first=True, last=True):
                return nc.tensor.matmul(dst, lhsT, rhs, start=first, stop=last, skip_group_check=True)

            def half_in(i):
                h = b.hl.take()
                g = b.raw.take() if i == 0 else b.raw.n - 1
                pe.wait_ge(raw_done, b.raw.done(g, 2) - (1 - i))
                for _ in range(i * BEHIND.get(h // 2, 0)):
                    b.raw.take()
                return w_hi[b.hl.slot(h)], w_lo[b.hl.slot(h)]

            def product(dsts, lhs, chunks, kb=CK, width=W, first=True, last=True):
                kh = kb // 2
                for c in range(2 * chunks):
                    wh, wl = half_in(c % 2)
                    for t, dst in enumerate(dsts):
                        for k in range(kh):
                            xh, xl = lhs(c * kh + k, t)
                            ins = mm3(dst, xh, xl, wh[:, k * width:(k + 1) * width], wl[:, k * width:(k + 1) * width],
                                      first and c + k == 0, last and c == 2 * chunks - 1 and k == kh - 1)
                    ins.then_inc(half_used, 1)

            def of(hi, lo):
                return lambda j, t: (hi[:, j, t * P:(t + 1) * P], lo[:, j, t * P:(t + 1) * P])

            def turned(blocks, width):
                pt = take_T()
                for i, src in enumerate(blocks):
                    n, m = src.shape[0], src.shape[1]
                    ins = nc.tensor.transpose(pt[0:m, i * width:i * width + n], src, ident[0:n, 0:n])
                ins.then_inc(T_full, 1)

            def turn8(src):
                for q in range(KB // 2):
                    turned([src(t, 2 * q + j) for j in range(2) for t in range(TT)], P)

            def gate_row(l, which):
                for half in range(2):
                    dst = take_A()
                    for k in range(4):
                        at = which * 8 + half * 4 + k
                        ins = mm(dst[:, k * P:(k + 1) * P], mod[:, l, at:at + 1].broadcast_to([P, P]), ident)
                    ins.then_inc(A_full, 1)

            def head(c0, h, t, w=HD):
                return proj[:, t, c0 + h * w:c0 + (h + 1) * w]

            def heads_T(c0, g, n):
                for p0 in range(0, n, 2):
                    turned([head(c0, g * HG + h, t) for h in range(p0, min(p0 + 2, n)) for t in range(TT)], P)

            pe.wait_ge(small_in, SMALL)
            for l in range(DEPTH):
                pe.wait_ge(rows_in[l], 6 * 16)
                turned([rows[l][0:ROWS, :]], P)
            def ada_sum(at, n):
                pe.wait_ge(raw_done, b.raw.done(b.raw.n - 1, 2))
                pt = take_T()
                for i in range(n):
                    for k in range(4):
                        ins = mm(pt[:, 4 * i + k:4 * i + k + 1], acc[(at + i) % 3][:, k * P:(k + 1) * P], ones[:, 0:1])
                ins.then_inc(T_full, 1)

            for j in range(FIRST):
                b.raw.take(), b.raw.take()
                ada_sum(j % 3, 1)

            def attention_scores(c, l):
                kind, g = CALLS[c]
                kt = kT[c % 2]
                if kind == "cmp":
                    heads_T(C_NQ, g, HG)
                    evacuated(b.T, T_free, 2)
                    dst = take_A()
                    for t in range(TT):
                        for h in range(HG):
                            at = (t * HG + h) * 16
                            ins = mm(dst[:, at:at + NCMP], qT[0:HD, h, t * P:(t + 1) * P], kcT[0:HD, g * NCMP:(g + 1) * NCMP])
                    ins.then_inc(A_full, 1)
                    return
                if kind in ("sel", "win"):
                    c0 = C_NKS if kind == "sel" else C_NKW
                    turned([head(c0, g, t) for t in range(TT)], P)
                    evacuated(b.T, T_free, 1)
                    kd, one = HD, True
                elif kind == "ret":
                    heads_T(C_RQ, 0, HG)
                    heads_T(C_RK, 0, HG)
                    evacuated(b.T, T_free, 2)
                    for p0 in range(0, HG, 2):
                        dst = take_A()
                        for h in range(p0, p0 + 2):
                            ins = mm(dst[:, (h - p0) * SEQ:(h - p0 + 1) * SEQ], kt[0:HD, h, 0:P], qT[0:HD, h, :])
                        ins.then_inc(A_full, 1)
                    dst = take_A()
                    for h in range(HG):
                        ins = mm(dst[:, h * P:(h + 1) * P], kt[0:HD, h, P:SEQ], qT[0:HD, h, P:SEQ])
                    ins.then_inc(A_full, 1)
                    return
                else:
                    pe.wait_ge(aug_ready, 2 * l + g + 1)
                    for aug in (q_aug, k_aug):
                        for p0 in range(0, HG, 2):
                            turned([aug[:, t, h, :] for h in range(p0, p0 + 2) for t in range(TT)], P)
                    marks[l, g] = b.T.n
                    evacuated(b.T, T_free, 2)
                    kd, one = HD + 2, False
                dst = take_A()
                for h in range(HG):
                    ins = mm(dst[:, h * P:(h + 1) * P], qT[0:kd, h, 0:P], kt[0:kd, 0 if one else h, 0:P])
                ins.then_inc(A_full, 1)
                for p0 in range(0, HG, 2):
                    dst = take_A()
                    for h in range(p0, p0 + 2):
                        ins = mm(dst[:, (h - p0) * SEQ:(h - p0 + 1) * SEQ], qT[0:kd, h, P:SEQ], kt[0:kd, 0 if one else h, :])
                    ins.then_inc(A_full, 1)

            def attention_values(c, l):
                kind, g = CALLS[c]
                s = S[c % 2]
                if kind == "ret":
                    n = l * len(CALLS)
                    pe.wait_ge(s_ready, S_SIGNALS * l + sum(S_COUNT[k] for k, _ in CALLS[:c + 1]))
                    for t in range(TT):
                        dst = take_O()
                        for h in range(HG):
                            for m in range(t + 1):
                                lhsT = s[:, h * SEQ + t * P:h * SEQ + (t + 1) * P] if m == 0 else s[:, 4 * SEQ + h * P:4 * SEQ + (h + 1) * P]
                                ins = mm(dst[:, h * P:(h + 1) * P], lhsT, proj[:, m, C_RV + h * P:C_RV + (h + 1) * P], m == 0, m == t)
                        ins.then_inc(O_full, 1)
                    return
                p_at = P_SIGNALS * l + sum(P_COUNT[k] for k, _ in CALLS[:c])
                if kind == "cmp":
                    pe.wait_ge(p_ready, p_at + 1)
                    for t in range(TT):
                        turned([s[:, (t * HG + h) * 16:(t * HG + h) * 16 + NCMP] for h in range(HG)], P)
                    evacuated(b.T, T_free, 2)
                    for t in range(TT):
                        dst = take_O()
                        for h in range(HG):
                            ins = mm(dst[:, h * HD:(h + 1) * HD], PT[0:NCMP, (t * HG + h) * P:(t * HG + h + 1) * P], vc[0:NCMP, g, :])
                        ins.then_inc(O_full, 1)
                    return
                v0 = {"sel": C_NVS + g * HD, "win": C_NVW + g * HD, "fox": C_FV + g * HG * HD}[kind]
                vs = HD if kind == "fox" else 0
                pe.wait_ge(p_ready, p_at + 1)
                turned([s[:, h * P:(h + 1) * P] for h in range(HG)], P)
                evacuated(b.T, T_free, 1)
                dst = take_O()
                for h in range(HG):
                    ins = mm(dst[:, h * HD:(h + 1) * HD], PT[:, h * P:(h + 1) * P], proj[:, 0, v0 + h * vs:v0 + h * vs + HD])
                ins.then_inc(O_full, 1)
                pe.wait_ge(p_ready, p_at + 2)
                for p0 in range(0, HG, 2):
                    turned([s[:, HG * P + h * SEQ + m * P:HG * P + h * SEQ + (m + 1) * P] for h in range(p0, p0 + 2) for m in range(2)], P)
                evacuated(b.T, T_free, 2)
                dst = take_O()
                for h in range(HG):
                    for m in range(2):
                        at = (HG + h * 2 + m) * P
                        ins = mm(dst[:, h * HD:(h + 1) * HD], PT[:, at:at + P], proj[:, m, v0 + h * vs:v0 + h * vs + HD], m == 0, m == 1)
                ins.then_inc(O_full, 1)

            n_gu, n_a, n_h = [0], [0], [0]

            for l in range(DEPTH):
                pe.wait_ge(y_ready, 2 * l + 1)
                turn8(lambda t, k: y[:, t, k * P:(k + 1) * P])
                n_h[0] += 4
                pe.wait_ge(h_ready, n_h[0])

                def in_round():
                    for j in range(3):
                        banks = [take_O(), take_O()] if j == 2 else [take_A(), take_A()]
                        product(banks, of(h_hi, h_lo), 2)
                if l == 0:
                    with rounds(pe, 0, WBLK // 3 - 1, {b.raw: 12, b.hl: 12, b.A: 4, b.O: 2, b.T: 2}):
                        in_round()
                        ada_sum(1, 1)
                        ada_sum(2, 2)
                    in_round()
                    ada_sum(1, 1)
                    ada_sum(2, 1)
                else:
                    with rounds(pe, 0, WBLK // 3, {b.raw: 6, b.hl: 12, b.A: 4, b.O: 2}):
                        in_round()
                pe.wait_ge(roped, l + 1)
                turned([proj[:, t, c0:c0 + 2 * HD] for c0 in (C_NKC, C_NVC) for t in range(TT)], P)
                pe.wait_ge(win_lo_ready, l + 1)
                for kv in range(2):
                    dst = take_A()
                    product([dst[:, 0:CMP_HID]], lambda j, t: (win_hi[:, kv, j * 30:j * 30 + P], win_lo[:, kv, j * 30:j * 30 + P]),
                            2, 8, CMP_HID)
                pe.wait_ge(hid_ready, 2 * l + 2)
                turned([hid[0:30, kv, k * P:(k + 1) * P] for kv in range(2) for k in range(2)], 32)
                evacuated(b.T, T_free, 1)
                dst = take_O()
                for k in range(2):
                    mm(dst[0:HD, 0:30], w2c[:, l, 0, k, :], hidT[:, k, :], k == 0, k == 1)
                for g in range(2):
                    for k in range(2):
                        ins = mm(dst[0:NCMP, HD + g * HD:HD + (g + 1) * HD], hidT[:, 2 + k, g * NCMP:(g + 1) * NCMP], w2c[:, l, 1, k, :], k == 0, k == 1)
                ins.then_inc(O_full, 1)
                pe.wait_ge(ls_ready, l + 1)
                dst = take_O()
                ls = fox[:, 3, :].rearrange("p (t h) -> p t h", t=TT)
                mm(dst[:, 0:8], tri, ls[:, 0, :])
                mm(dst[:, 8:16], ones, ls[:, 0, :], True, False)
                mm(dst[:, 8:16], tri, ls[:, 1, :], False, True).then_inc(O_full, 1)
                evacuated(b.O, O_free, 2)
                for c in range(len(CALLS) + 1):
                    if c < len(CALLS):
                        attention_scores(c, l)
                    if c:
                        attention_values(c - 1, l)
                        if c - 1 in WHOLE:
                            m = WHOLE[c - 1]
                            pe.wait_ge(o_ready, 3 * l + m + 1)
                            for q in range(2):
                                turned([o_sb[:, t, (2 * q + j) * P:(2 * q + j + 1) * P] for j in range(2) for t in range(TT)], P)
                for half in range(2):
                    for m in range(3):
                        product([take_A(), take_A()], of(h_hi, h_lo), 2)
                        if half == 0:
                            pe.wait_ge(oT_ready, 6 * l + 2 * m + 2)
                        product([take_A(), take_A()], of(oT_hi[m], oT_lo[m]), 1)
                        if l == 0:
                            ada_sum(m, 1)
                pe.wait_ge(merged_ready, l + 1)
                turn8(lambda t, k: merged[t][:, k * P:(k + 1) * P])
                gate_row(l, 2)
                n_h[0] += 4
                pe.wait_ge(h_ready, n_h[0])
                for half in range(2):
                    product([take_A(), take_A()], of(h_hi, h_lo), 2)
                pe.wait_ge(y_ready, 2 * l + 2)
                turn8(lambda t, k: y[:, t, k * P:(k + 1) * P])

                if l % 2 == 0:
                    n_h[0] += 4
                    pe.wait_ge(h_ready, n_h[0])
                    G, U, av = Turn(), Turn(), Turn()
                    evacuated(b.A, A_free, 4)

                    def gate_up(banks, turn, free, chunks, kb, width):
                        v = turn.take()
                        if turn.loops or v:
                            pe.wait_ge(free, turn.done(v - 1))
                        product([p[:, 0:width] for p in banks], of(h_hi, h_lo), chunks, kb, width)

                    def turn_a(nb):
                        v = av.take()
                        pe.wait_ge(a_ready, av.done(v))
                        for q in range(nb // 2):
                            turned([a_sb[:, t, (2 * q + j) * P:(2 * q + j + 1) * P] for j in range(2) for t in range(TT)], P)

                    def down(nb):
                        evacuated(b.T, T_free, nb // 2)
                        if nb == CK:
                            for half in range(2):
                                parts = [half_in(0), None]
                                for t in range(TT):
                                    dst = take_O()
                                    for k in range(CK):
                                        if t == 0 and k == CK // 2:
                                            parts[1] = half_in(1)
                                        wh, wl = parts[k // (CK // 2)]
                                        at = k % (CK // 2) * W
                                        xh, xl = of(aT_hi, aT_lo)(k, t)
                                        ins = mm3(dst, xh, xl, wh[:, at:at + W], wl[:, at:at + W], k == 0, k == CK - 1)
                                        if t == 1 and k % (CK // 2) == CK // 2 - 1:
                                            ins.then_inc(half_used, 1)
                                    if t == 0:
                                        ins.then_inc(O_full, 1)
                        else:
                            parts = [half_in(0), half_in(1)]
                            for half in range(2):
                                for t in range(TT):
                                    dst = take_O()
                                    for k, (wh, wl) in enumerate(parts):
                                        xh, xl = of(aT_hi, aT_lo)(k, t)
                                        ins = mm3(dst, xh, xl, wh[:, half * W:(half + 1) * W], wl[:, half * W:(half + 1) * W], k == 0, k == 1)
                                        if half + t == 2:
                                            ins.then_inc(half_used, 1)
                                    if half + t < 2:
                                        ins.then_inc(O_full, 1)
                    gate_up(pA[0:2], G, g_free, 2, CK, W)
                    gate_up(pA[2:4], U, u_free, 2, CK, W)
                    with rounds(pe, 0, FFB // 2, {b.raw: 18, b.hl: 24, b.T: 6, b.O: 8, G: 2, U: 2, av: 2}):
                        for _ in range(2):
                            gate_up(pA[0:2], G, g_free, 2, CK, W)
                            turn_a(CK)
                            gate_up(pA[2:4], U, u_free, 2, CK, W)
                            down(CK)
                        ada_sum(0, 2)
                        ada_sum(2, 1)
                    gate_up(pA[0:2], G, g_free, 1, KB, W // 2)
                    turn_a(CK)
                    gate_up(pA[2:4], U, u_free, 1, KB, W // 2)
                    down(CK)
                    turn_a(2)
                    down(2)
                    pe.wait_ge(g_free, G.n)
                    pe.wait_ge(u_free, U.n)
                    gate_row(l, 5)
                else:
                    pe.wait_ge(hf_ready, 4 * (2 * l + 2))
                    dst = take_A()
                    for t in range(TT):
                        for k in range(KB):
                            ins = mm(dst[:, t * NE:(t + 1) * NE], hf[:, k, t * P:(t + 1) * P], routw[:, k, :], k == 0, k == KB - 1)
                    ins.then_inc(A_full, 1)
                    pe.wait_ge(sel_ready, 1)
                    dst = take_A()
                    chosen = rs[:, 0, :].rearrange("p (t e) -> p t e", t=TT)
                    mm(dst[:, 0:NE], tri, chosen[:, 0, :])
                    mm(dst[:, NE:2 * NE], ones, chosen[:, 0, :], True, False)
                    mm(dst[:, NE:2 * NE], tri, chosen[:, 1, :], False, True)
                    mm(dst[:, 2 * NE:3 * NE], ones, chosen[:, 0, :], True, False)
                    mm(dst[:, 2 * NE:3 * NE], ones, chosen[:, 1, :], False, True).then_inc(A_full, 1)
                    gate_row(l, 5)
                    pe.wait_ge(slots_ready, 1)
                    items = pe.value_load(flag[0:1, 0:1], min_val=NE, max_val=2 * NE)
                    evacuated(b.A, A_free, 4)
                    G, U, av, xv = Turn(start=FFB + 1), Turn(start=FFB + 1), Turn(start=FFB + 1), Turn()

                    def gather():
                        for q in range(2):
                            pt = take_T()
                            for j in range(4):
                                k = 4 * q + j
                                for t in range(TT):
                                    ins = mm(pt[:, j * P:(j + 1) * P], y[:, t, k * P:(k + 1) * P], sel[:, t, :], t == 0, t == 1)
                            ins.then_inc(T_full, 1)
                    pe.wait_ge(sel_ready, 2)
                    gather()
                    with rounds(pe, 0, items, {b.raw: 42, b.hl: 84, b.T: 22, b.O: 2, G: EFB, U: EFB, av: EFB, xv: 1}):
                        v = xv.take()
                        for t in range(TT):
                            turned([sel[:, t, :]], P)
                        outs = [take_O(), take_O()]
                        for o in outs:
                            mm(o[:, :], zeros[:, 0:P], zeros[:, :], True, False)
                        pe.wait_ge(x_ready, xv.done(v, 2))

                        def gate_up(dst, turn, free):
                            v = turn.take()
                            pe.wait_ge(free, turn.done(v - 1))
                            product([dst], lambda j, t: (x_hi[:, j, :], x_lo[:, j, :]), 2)

                        def turn_a():
                            v = av.take()
                            pe.wait_ge(a_ready, av.done(v))
                            for q in range(2):
                                turned([a_sb[:, 0, (2 * q + j) * P:(2 * q + j + 1) * P] for j in range(2)], P)

                        def down(last=False):
                            evacuated(b.T, T_free, 2)
                            for half in range(2):
                                for i in range(2):
                                    wh, wl = half_in(i)
                                    for j in range(CK // 2):
                                        k = i * (CK // 2) + j
                                        ins = mm3(outs[half][:, :], aT_hi[:, k, 0:P], aT_lo[:, k, 0:P],
                                                  wh[:, j * W:(j + 1) * W], wl[:, j * W:(j + 1) * W], False, last and k == CK - 1)
                                    ins.then_inc(half_used, 1)
                        gate_up(pA[0], G, g_free)
                        gate_up(pA[2], U, u_free)
                        with rounds(pe, 1, EFB, {b.raw: 6, b.hl: 12, b.T: 2, G: 1, U: 1, av: 1}):
                            gate_up(pA[0], G, g_free)
                            turn_a()
                            gate_up(pA[2], U, u_free)
                            down()
                        pe.wait_ge(sel_ready, xv.done(v) + 2)
                        gather()
                        turn_a()
                        down(True)
                        evacuated(b.O, O_free, 2)
                        for t in range(TT):
                            for half in range(2):
                                dst = take_T()
                                mm(dst[:, :], selT[:, t * P:(t + 1) * P], oe[:, half * W:(half + 1) * W]).then_inc(T_full, 1)

        @block.gpsimd
        def _(pool):
            n_link = [0]

            def link(ins):
                n_link[0] += 1
                ins.then_inc(pool_link, 1)
                pool.wait_ge(pool_link, n_link[0])

            link(pool.memset(zeros[:, :], 0.0))
            pool.wait_ge(small_in, SMALL)
            for l in range(DEPTH):
                pool.wait_ge(proj_ready, l + 1)
                half = HD // 2
                for c0, nh in ((C_NKC, 2), (C_NQ, 8), (C_NKS, 2), (C_NKW, 2), (C_RQ, 8)):
                    for t in range(TT):
                        v = proj[:, t, c0:c0 + nh * HD].rearrange("p (h d) -> p h d", h=nh)
                        r = rope_t[:, t, 0:nh, :]
                        cos, sin = (rope[:, s, t, :].unsqueeze(1) for s in range(2))
                        pool.tensor_tensor(r[:, :, 0:half], v[:, :, half:HD], sin[:, :, 0:half].broadcast_to([P, nh, half]), ALU.mult)
                        link(pool.tensor_tensor(r[:, :, half:HD], v[:, :, 0:half], sin[:, :, half:HD].broadcast_to([P, nh, half]), ALU.mult))
                        link(pool.tensor_tensor(v, v, cos.broadcast_to([P, nh, HD]), ALU.mult))
                        link(pool.tensor_tensor(v, v, r, ALU.add))
                pool.drain().then_inc(roped, 1)
                pool.wait_ge(cum_ready, l + 1)
                for g in range(2):
                    if g or l:
                        pool.wait_ge(T_full, marks[l - 1 + g, 1 - g])
                    for aug, c0, own in ((q_aug, C_FQ, 0), (k_aug, C_FK, 1)):
                        src = proj[:, :, c0 + g * HG * HD:c0 + (g + 1) * HG * HD].rearrange("p t (h d) -> p t h d", h=HG)
                        for t in range(TT):
                            pool.tensor_copy(aug[:, t, :, 0:HD], src[:, t, :, :])
                            pool.tensor_copy(aug[:, t, :, HD + own:HD + own + 1], cum[:, t, g * HG:(g + 1) * HG, own:own + 1])
                            pool.memset(aug[:, t, :, HD + 1 - own:HD + 2 - own], 1.0)
                    pool.drain().then_inc(aug_ready, 1)

        @block.scalar
        def _(act):
            b = Books()
            link_n = [0]

            def link(ins):
                link_n[0] += 1
                ins.then_inc(act_link, 1)
                act.wait_ge(act_link, link_n[0])

            def copy(dst, src):
                return nc.scalar.activation(dst, src, ACT.Copy)

            def split_to(at):
                while b.hl_in.n < min(at, b.end):
                    h = b.hl_in.take()
                    i = h % 2
                    g = b.raw.take() if i == 0 else b.raw.n - 1
                    if i == 0:
                        act.wait_ge(landed[b.raw.slot(g)], (b.raw.before(g) + 1) * 16)
                    if h >= HL or b.hl_in.loops:
                        act.wait_ge(half_used, b.hl_in.done(h - HL))
                    copy(w_hi[b.hl_in.slot(h)][:, :], raw[b.raw.slot(g)][:, i * HALF:(i + 1) * HALF]).then_inc(hi_ready, 1)
                    for _ in range(i * BEHIND.get(h // 2, 0)):
                        b.raw.take()

            def segment(chunks):
                b.end = b.hl.n + 2 * chunks
                split_to(b.hl.n + AHEAD)

            def ahead():
                n = b.end - b.hl_in.n + AHEAD
                b.end += AHEAD
                split_to(b.hl_in.n + n)

            def use(n):
                split_to(b.hl.n + 2 * n + AHEAD)
                for _ in range(n):
                    b.hl.take()
                    v = b.hl.take()
                return v

            def T_in():
                v = b.T.take()
                act.wait_ge(T_full, b.T.done(v))
                return pT[b.T.slot(v)], T_free[b.T.slot(v)]

            def T_copy(dst_of):
                pt, free = T_in()
                copy(*dst_of(pt)).then_inc(free, 1)

            def skip(turn, n):
                for _ in range(n):
                    turn.take()

            act.wait_ge(cols_ready, 1)
            nc.scalar.activation(csilu[:, :], cols[:, 0, R_C:R_C + 8], ACT.Silu).then_inc(csilu_ready, 1)
            skip(b.T, DEPTH + FIRST)
            skip(b.raw, 2 * FIRST)
            n_norm, n_hf, n_m, n_dev = [0], [0], [0], [0]

            def root():
                n_norm[0] += 1
                act.wait_ge(ms_ready, n_norm[0])
                nc.scalar.activation(nrm[:, 2:4], nrm[:, 0:2], ACT.Sqrt).then_inc(rt_ready, 1)

            def hi_columns():
                for q in range(4):
                    b.T.take()
                    n_hf[0] += 1
                    act.wait_ge(hf_ready, n_hf[0])
                    copy(h_hi[:, 2 * q:2 * q + 2, :], hf[:, 2 * q:2 * q + 2, :]).then_inc(h_hi_ready, 1)

            def evacuate_qk(c, l):
                kind, g = CALLS[c]
                kt = kT[c % 2]
                pair = lambda dst, p0, kd: T_copy(lambda pt: (dst[0:kd, p0:p0 + 2, :], pt[0:kd, :].rearrange("p (h n) -> p h n", h=2)))
                if kind == "cmp":
                    pair(qT, 0, HD)
                    pair(qT, 2, HD)
                    skip(b.A, 1)
                elif kind in ("sel", "win"):
                    T_copy(lambda pt: (kt[0:HD, 0, :], pt[0:HD, 0:SEQ]))
                    skip(b.A, 3)
                else:
                    kd = HD if kind == "ret" else HD + 2
                    for dst in (qT, kt):
                        pair(dst, 0, kd)
                        pair(dst, 2, kd)
                    skip(b.A, 3)

            def exponentials(c, l):
                kind, g = CALLS[c]
                s, st = S[c % 2], stat[:, (c % 2) * 40:(c % 2) * 40 + 40]
                s_at = S_SIGNALS * l + sum(S_COUNT[k] for k, _ in CALLS[:c])
                if kind == "ret":
                    return
                if kind == "cmp":
                    act.wait_ge(s_ready, s_at + 1)
                    nc.scalar.activation(s[:, 0:P], s[:, 0:P], ACT.Exp, scale=SCALE).then_inc(p_ready, 1)
                    return
                for t in range(TT):
                    act.wait_ge(s_ready, s_at + t + 1)
                    for h in range(HG):
                        v = s[:, h * P:(h + 1) * P] if t == 0 else s[:, HG * P + h * SEQ:HG * P + (h + 1) * SEQ]
                        ins = nc.scalar.activation(v, v, ACT.Exp, bias=st[:, 8 + t * HG + h:9 + t * HG + h], scale=SCALE,
                                                   accum_out=st[:, 16 + t * HG + h:17 + t * HG + h])
                    ins.then_inc(p_ready, 1)

            def evacuate_p(c):
                kind, g = CALLS[c]
                if kind == "ret":
                    for t in range(TT):
                        skip(b.O, 1)
                        n_dev[0] += 1
                        act.wait_ge(var_ready, n_dev[0])
                        nc.scalar.activation(ret_st[:, 12:16], ret_st[:, 8:12], ACT.Sqrt).then_inc(dev_ready, 1)
                elif kind == "cmp":
                    for t in range(TT):
                        T_copy(lambda pt: (PT[0:NCMP, t * 4 * P:(t + 1) * 4 * P], pt[0:NCMP, :]))
                    skip(b.O, 2)
                else:
                    for i in range(3):
                        T_copy(lambda pt: (PT[:, i * 4 * P:(i + 1) * 4 * P], pt[:, :]))
                    skip(b.O, 2)

            for l in range(DEPTH):
                root()
                hi_columns()
                segment(2 * WBLK + 4)

                def in_round(ada):
                    for j in range(3):
                        use(2)
                    skip(b.A, 4)
                    skip(b.O, 2)
                    skip(b.T, 2 * ada)
                if l == 0:
                    with rounds(act, 0, WBLK // 3 - 1, {b.raw: 12, b.hl: 12, b.hl_in: 12, b.A: 4, b.O: 2, b.T: 2}):
                        in_round(True)
                    in_round(True)
                else:
                    with rounds(act, 0, WBLK // 3, {b.raw: 6, b.hl: 12, b.hl_in: 12, b.A: 4, b.O: 2}):
                        in_round(False)
                pt, free = T_in()
                for i in range(4):
                    kv, g = divmod(i, 2)
                    src = pt[g * HD:(g + 1) * HD, kv * SEQ:(kv + 1) * SEQ]
                    copy(kk[0:HD, i, :], src)
                    ins = copy(kk[HD:P, i, 0:SEQ - 1], src[:, 1:SEQ])
                ins.then_inc(free, 1)
                act.wait_ge(win_ready, l + 1)
                copy(win_hi[:, :, 0:480], win[:, :, :, :, :].rearrange("p v j g n -> p v (j g n)")).then_inc(win_hi_ready, 1)
                for kv in range(2):
                    v = use(2)
                    av = b.A.take()
                    act.wait_ge(half_used, b.hl.done(v))
                    nc.scalar.activation(hid[0:30, kv, :], pA[b.A.slot(av)][0:30, 0:CMP_HID], ACT.Silu).then_inc(hid_ready, 1)
                    act.drain().then_inc(A_free[b.A.slot(av)], 1)
                pt, free = T_in()
                copy(hidT[:, :, :], pt[:, 0:P].rearrange("p (i n) -> p i n", i=4)[:, :, 0:30]).then_inc(free, 1)
                skip(b.O, 2)
                act.wait_ge(proj_ready, l + 1)
                rg = proj[:, :, C_RG:C_RG + W]
                nc.scalar.activation(rg, rg, ACT.Silu)
                nc.scalar.activation(gates3[:, :, :], proj[:, :, C_NG:C_NG + 24], ACT.Sigmoid).then_inc(sig_ready, 1)
                act.wait_ge(z_ready, l + 1)
                link(nc.scalar.activation(fox[:, 1, :], fox[:, 1, :], ACT.Exp))
                nc.scalar.activation(fox[:, 2, :], fox[:, 1, :], ACT.Ln, bias=1.0).then_inc(e_ready, 1)
                for c in range(len(CALLS) + 1):
                    if c < len(CALLS):
                        evacuate_qk(c, l)
                        exponentials(c, l)
                    if c:
                        evacuate_p(c - 1)
                        if c - 1 in WHOLE:
                            m = WHOLE[c - 1]
                            for q in range(2):
                                pt, free = T_in()
                                copy(oT_hi[m][:, 2 * q:2 * q + 2, :], pt[:, :].rearrange("p (k n) -> p k n", k=2)).then_inc(oT_hi_ready, 1)
                segment(3 * 3 * 2 + 4)
                for half in range(2):
                    for m in range(3):
                        v = use(2)
                        act.wait_ge(half_used, b.hl.done(v))
                        if n_m[0]:
                            act.wait_ge(g_used, n_m[0])
                        n_m[0] += 1
                        for t in range(TT):
                            av = b.A.take()
                            ins = nc.scalar.activation(gate[:, t, :], pA[b.A.slot(av)][:, :], ACT.Sigmoid)
                            ins.then_inc(A_free[b.A.slot(av)], 1)
                        skip(b.A, 2)
                        use(1)
                        skip(b.T, l == 0)
                for q in range(4):
                    pt, free = T_in()
                    copy(h_hi[:, 2 * q:2 * q + 2, :], pt[:, :].rearrange("p (k n) -> p k n", k=2)).then_inc(h_hi_ready, 1)
                skip(b.A, 2)
                use(4)
                skip(b.A, 4)
                root()
                if l % 2 == 0:
                    hi_columns()
                    segment(6 * FFB + 3)
                    G, av, bv = Turn(), Turn(), Turn()

                    def silu(width=W):
                        v = G.take()
                        act.wait_ge(half_used, b.hl.done(b.hl.n - 1))
                        for t in range(TT):
                            ins = nc.scalar.activation(a_sb[:, t, 0:width], pA[t][:, 0:width], ACT.Silu)
                        ins.then_inc(g_free, 1)

                    def hi_a(n):
                        for q in range(n):
                            pt, free = T_in()
                            copy(aT_hi[:, 2 * q:2 * q + 2, :], pt[:, :].rearrange("p (k n) -> p k n", k=2)).then_inc(aT_hi_ready, 1)
                    use(2)
                    silu()
                    use(2)
                    with rounds(act, 0, FFB // 2, {b.raw: 18, b.hl: 24, b.hl_in: 24, b.T: 6, b.O: 8, G: 2}):
                        for _ in range(2):
                            use(2)
                            hi_a(2)
                            silu()
                            use(2)
                            use(2)
                            skip(b.O, 4)
                        skip(b.T, 2)
                    use(1)
                    hi_a(2)
                    silu(W // 2)
                    use(1)
                    use(2)
                    skip(b.O, 4)
                    hi_a(1)
                    use(1)
                    skip(b.O, 4)
                    skip(b.A, 2)
                else:
                    b.T.take(), b.T.take(), b.T.take(), b.T.take()
                    act.wait_ge(log_ready, 1)
                    nc.scalar.activation(rs[:, 2, :], rs[:, 2, :], ACT.Exp).then_inc(re_ready, 1)
                    act.wait_ge(slots_ready, 1)
                    items = act.value_load(flag[0:1, 0:1], min_val=NE, max_val=2 * NE)
                    G, xv = Turn(start=FFB + 1), Turn()

                    def hi_x(at):
                        for q in range(2):
                            act.wait_ge(xf_ready, at + q + 1)
                            copy(x_hi[:, 4 * q:4 * q + 4, :], x_f[:, 4 * q:4 * q + 4, :]).then_inc(x_hi_ready, 1)
                    segment(6 * EFB)
                    skip(b.T, 2)
                    hi_x(0)
                    with rounds(act, 0, items, {b.raw: 42, b.hl: 84, b.hl_in: 84, b.T: 22, b.O: 2, G: EFB, xv: 1}) as e:
                        v = xv.take()
                        for t in range(TT):
                            T_copy(lambda pt: (selT[:, t * P:(t + 1) * P], pt[:, 0:P]))

                        def silu():
                            G.take()
                            act.wait_ge(half_used, b.hl.done(b.hl.n - 1))
                            nc.scalar.activation(a_sb[:, 0, :], pA[0][:, :], ACT.Silu).then_inc(g_free, 1)

                        def hi_a():
                            for q in range(2):
                                pt, free = T_in()
                                copy(aT_hi[:, 2 * q:2 * q + 2, 0:P], pt[:, 0:SEQ].rearrange("p (k n) -> p k n", k=2)).then_inc(aT_hi_ready, 1)
                        use(2)
                        silu()
                        use(2)
                        with rounds(act, 1, EFB, {b.raw: 6, b.hl: 12, b.hl_in: 12, b.T: 2, G: 1}):
                            use(2)
                            hi_a()
                            silu()
                            use(4)
                        skip(b.T, 2)
                        hi_a()
                        hi_x(xv.done(v, 2))
                        u = use(2)
                        with act.If(e < items - 1):
                            ahead()
                        act.wait_ge(half_used, b.hl.done(u))
                        copy(oe[:, 0:W], pO[b.O.slot(b.O.take())][:, :]).then_inc(O_free[0], 1)
                        skip(b.O, 1)
                        skip(b.T, 4)
            root()

        @block.vector
        def _(dve):
            b = Books()
            V = nc.vector

            def link(ins):
                v = b.link.take()
                ins.then_inc(dve_link, 1)
                dve.wait_ge(dve_link, b.link.done(v))

            def split_to(at):
                while b.hl_in.n < min(at, b.end):
                    h = b.hl_in.take()
                    i = h % 2
                    g = b.raw.take() if i == 0 else b.raw.n - 1
                    dve.wait_ge(hi_ready, b.hl_in.done(h))
                    s, m = b.raw.slot(g), b.hl_in.slot(h)
                    V.tensor_tensor(w_lo[m][:, :], raw[s][:, i * HALF:(i + 1) * HALF], w_hi[m][:, :].bitcast(F32), ALU.subtract).then_inc(raw_done, 1)
                    for _ in range(i * BEHIND.get(h // 2, 0)):
                        ada_chunk()

            def ada_chunk():
                n, c = divmod(b.ada.take(), 2)
                g = b.raw.take()
                s = raw[b.raw.slot(g)]
                dst = acc[n % 3]
                dve.wait_ge(landed[b.raw.slot(g)], (b.raw.before(g) + 1) * 16)
                for k in range(CK):
                    src, sc = s[:, k * W:(k + 1) * W], csilu[:, c * CK + k:c * CK + k + 1]
                    if c + k == 0:
                        ins = V.tensor_scalar(dst[:, :], src, sc, None, ALU.mult)
                    else:
                        ins = V.scalar_tensor_tensor(dst[:, :], src, sc, dst[:, :], ALU.mult, ALU.add)
                    if k % 2 == 1:
                        ins.then_inc(raw_done, 1)
                        dve.wait_ge(raw_done, b.raw.done(g, 2) - (1 - k // 2))
                    else:
                        link(ins)

            def ada_columns(l, at, n):
                pt, free = T_in()
                V.tensor_tensor(mod[:, l, bass.ds(at, 4 * n)], pt[:, 0:4 * n], cols[:, l, bass.ds(at + R_ADAB, 4 * n)], ALU.add).then_inc(free, 1)

            def ada_scale(l, at, w):
                link(dve.drain())
                link(V.scalar_tensor_tensor(mod[:, l, at:at + 8], mod[:, l, at:at + 8], 1.0, cols[:, l, w:w + 8], ALU.add, ALU.mult))

            def segment(chunks):
                b.end = b.hl.n + 2 * chunks
                split_to(b.hl.n + AHEAD)

            def ahead():
                n = b.end - b.hl_in.n + AHEAD
                b.end += AHEAD
                split_to(b.hl_in.n + n)

            def use(n):
                split_to(b.hl.n + 2 * n + AHEAD)
                for _ in range(n):
                    b.hl.take()
                    v = b.hl.take()
                return v

            def T_in():
                v = b.T.take()
                dve.wait_ge(T_full, b.T.done(v))
                return pT[b.T.slot(v)], T_free[b.T.slot(v)]

            def A_in(chunk=None):
                v = b.A.take()
                if chunk is None:
                    dve.wait_ge(A_full, b.Af.done(b.Af.take()))
                else:
                    dve.wait_ge(half_used, b.hl.done(chunk))
                return pA[b.A.slot(v)], A_free[b.A.slot(v)]

            def O_in(chunk=None):
                v = b.O.take()
                if chunk is None:
                    dve.wait_ge(O_full, b.Of.done(b.Of.take()))
                else:
                    dve.wait_ge(half_used, b.hl.done(chunk))
                return pO[b.O.slot(v)], O_free[b.O.slot(v)]

            def skip(turn, n):
                for _ in range(n):
                    turn.take()

            def bc(v, shape):
                return v.broadcast_to(shape)

            for l in range(DEPTH):
                pt, free = T_in()
                V.tensor_copy(cols[:, l, 0:ROWS], pt[:, 0:ROWS]).then_inc(cols_ready, 1)
                dve.drain().then_inc(free, 1)

            n_rt, n_hi, n_aT, n_go = [0], [0], [0], [0]

            def normalise():
                for t in range(TT):
                    link(V.tensor_tensor_reduce(y[:, t, :], x[:, t, :], x[:, t, :], 1.0, 0.0, ALU.mult, ALU.add, nrm[:, 6 + t:7 + t]))
                V.tensor_scalar(nrm[:, 0:2], nrm[:, 6:8], 1.0 / D, EPS, ALU.mult, ALU.add).then_inc(ms_ready, 1)
                n_rt[0] += 1
                dve.wait_ge(rt_ready, n_rt[0])
                link(V.reciprocal(nrm[:, 4:6], nrm[:, 2:4]))
                for t in range(TT):
                    ins = V.tensor_scalar(y[:, t, :], x[:, t, :], nrm[:, 4 + t:5 + t], None, ALU.mult)
                return ins

            def modulate(l, which, both):
                sc, sh = (which * 24 + 8, which * 24)
                for q in range(4):
                    pt, free = T_in()
                    for j in range(2):
                        k = 2 * q + j
                        ins = V.tensor_scalar(hf[:, k, :], pt[:, j * SEQ:(j + 1) * SEQ], mod[:, l, sc + k:sc + k + 1],
                                              mod[:, l, sh + k:sh + k + 1], ALU.mult, ALU.add)
                        if j == 0:
                            pass
                    ins.then_inc(hf_ready, 1)
                    dve.drain().then_inc(free, 1)
                    if both:
                        n_hi[0] += 1
                        dve.wait_ge(h_hi_ready, n_hi[0])
                        V.tensor_tensor(h_lo[:, 2 * q:2 * q + 2, :], hf[:, 2 * q:2 * q + 2, :],
                                        h_hi[:, 2 * q:2 * q + 2, :].bitcast(F32), ALU.subtract).then_inc(h_ready, 1)

            def scores(c, l):
                kind, g = CALLS[c]
                s, st = S[c % 2], stat[:, (c % 2) * 40:(c % 2) * 40 + 40]
                skip(b.T, {"cmp": 2, "sel": 1, "win": 1, "ret": 4, "fox": 4}[kind])
                if kind == "ret":
                    for p0 in range(0, HG, 2):
                        pa, free = A_in()
                        V.tensor_tensor(s[:, p0 * SEQ:(p0 + 2) * SEQ], pa[:, :], decay[:, p0:p0 + 2, :].rearrange("p h n -> p (h n)"), ALU.mult).then_inc(free, 1)
                    pa, free = A_in()
                    link(V.tensor_tensor(s[:, 4 * SEQ:4 * SEQ + 4 * P].rearrange("p (h n) -> p h n", h=HG),
                                         pa[:, :].rearrange("p (h n) -> p h n", h=HG), decay[:, :, 0:P], ALU.mult))
                    dve.drain().then_inc(free, 1)
                    dve.drain().then_inc(s_ready, 1)
                    return
                if kind == "cmp":
                    pa, free = A_in()
                    sv = s[:, 0:P].rearrange("p (r n) -> p r n", n=16)[:, :, 0:NCMP]
                    cm = cmask.rearrange("p t h n -> p (t h) n")[:, :, 0:NCMP]
                    link(V.memset(s[:, 0:P], 0.0))
                    V.tensor_tensor(sv, pa[:, 0:P].rearrange("p (r n) -> p r n", n=16)[:, :, 0:NCMP], cm, ALU.add).then_inc(free, 1)
                    v = b.A.n - 1
                    dve.wait_ge(free, b.A.before(v) + 1)
                    link(V.tensor_reduce(st[:, 0:8], sv, AX_X, ALU.max))
                    V.tensor_tensor(sv, sv, bc(st[:, 0:8].unsqueeze(2), [P, 8, NCMP]), ALU.subtract).then_inc(s_ready, 1)
                    return
                for t in range(TT):
                    w = (t + 1) * P
                    for i in range(t + 1):
                        nh = HG // (t + 1)
                        pa, free = A_in()
                        at = HG * P * t + i * nh * w
                        dst = s[:, at:at + nh * w].rearrange("p (h n) -> p h n", h=nh)
                        mk = mask[:, 2 * P - w:2 * P].unsqueeze(1)
                        V.tensor_tensor(dst, pa[:, 0:nh * w].rearrange("p (h n) -> p h n", h=nh), bc(mk, [P, nh, w]), ALU.add).then_inc(free, 1)
                        v = b.A.n - 1
                        dve.wait_ge(free, b.A.before(v) + 1)
                    sv = s[:, HG * P * t:HG * P * t + HG * w].rearrange("p (h n) -> p h n", h=HG)
                    link(V.tensor_reduce(st[:, t * HG:(t + 1) * HG], sv, AX_X, ALU.max))
                    V.tensor_scalar(st[:, 8 + t * HG:8 + (t + 1) * HG], st[:, t * HG:(t + 1) * HG], -SCALE, None, ALU.mult).then_inc(s_ready, 1)

            def values(c, l):
                kind, g = CALLS[c]
                st = stat[:, (c % 2) * 40:(c % 2) * 40 + 40]
                s = S[c % 2]
                skip(b.T, {"cmp": 2, "sel": 3, "win": 3, "ret": 0, "fox": 3}[kind])
                if kind == "ret":
                    for t in range(TT):
                        po, free = O_in()
                        for h in range(HG):
                            link(V.bn_stats(fox_st[:, h * 6:(h + 1) * 6], po[:, h * P:(h + 1) * P]))
                            link(V.bn_aggr(ret_st[:, h * 2:h * 2 + 2], fox_st[:, h * 6:(h + 1) * 6]))
                        mv = ret_st[:, 0:8].rearrange("p (h s) -> p h s", s=2)
                        V.tensor_scalar(ret_st[:, 8:12], mv[:, :, 1], EPS, None, ALU.add).then_inc(var_ready, 1)
                        dve.wait_ge(dev_ready, TT * l + t + 1)
                        link(V.reciprocal(ret_st[:, 16:20], ret_st[:, 12:16]))
                        for h in range(HG):
                            link(V.tensor_scalar(o_sb[:, t, h * P:(h + 1) * P], po[:, h * P:(h + 1) * P], ret_st[:, 2 * h:2 * h + 1],
                                                 ret_st[:, 16 + h:17 + h], ALU.subtract, ALU.mult))
                        dve.drain().then_inc(free, 1)
                        link(V.tensor_tensor(o_sb[:, t, :], o_sb[:, t, :], proj[:, t, C_RG:C_RG + W], ALU.mult))
                    dve.drain().then_inc(o_ready, 1)
                    return
                p_at = P_SIGNALS * l + sum(P_COUNT[k] for k, _ in CALLS[:c])
                if kind == "cmp":
                    dve.wait_ge(p_ready, p_at + 1)
                    sv = s[:, 0:P].rearrange("p (r n) -> p r n", n=16)[:, :, 0:NCMP]
                    link(V.tensor_reduce(st[:, 16:24], sv, AX_X, ALU.add))
                else:
                    dve.wait_ge(p_ready, p_at + 2)
                link(V.reciprocal(st[:, 24:32], st[:, 16:24]))
                coef = st[:, 24:32]
                if kind != "fox":
                    coef = st[:, 32:40]
                    branch = {"cmp": 0, "sel": 1, "win": 2}[kind]
                    cv = coef.rearrange("p (t h) -> p t h", t=TT)
                    link(V.tensor_tensor(cv, st[:, 24:32].rearrange("p (t h) -> p t h", t=TT),
                                         gates3[:, :, branch * 8 + g * HG:branch * 8 + (g + 1) * HG], ALU.mult))
                    if kind == "cmp":
                        link(V.tensor_tensor(cv, cv, bc(cvalid.unsqueeze(2), [P, TT, HG]), ALU.mult))
                for t in range(TT):
                    po, free = O_in()
                    src = po[:, 0:HG * HD].rearrange("p (h d) -> p h d", h=HG)
                    dst = o_sb[:, t, g * HG * HD:(g + 1) * HG * HD].rearrange("p (h d) -> p h d", h=HG)
                    cf = bc(coef[:, t * HG:(t + 1) * HG].unsqueeze(2), [P, HG, HD])
                    if kind in ("cmp", "fox"):
                        V.tensor_tensor(dst, src, cf, ALU.mult).then_inc(free, 1)
                        dve.wait_ge(free, b.O.before(b.O.n - 1) + 1)
                    else:
                        part = o_part[:, :].rearrange("p (h d) -> p h d", h=HG)
                        V.tensor_tensor(part, src, cf, ALU.mult).then_inc(free, 1)
                        dve.wait_ge(free, b.O.before(b.O.n - 1) + 1)
                        link(V.tensor_tensor(dst, dst, part, ALU.add))
                if c in WHOLE:
                    dve.drain().then_inc(o_ready, 1)

            dve.wait_ge(small_in, SMALL)
            dve.wait_ge(csilu_ready, 1)
            dve.wait_ge(cols_ready, DEPTH)
            for l in range(DEPTH):
                normalise().then_inc(y_ready, 1)
                if l == 0:
                    for j in range(FIRST):
                        ada_chunk()
                        ada_chunk()
                        if j:
                            ada_columns(0, 4 * (j - 1), 1)
                    ada_columns(0, 4 * (FIRST - 1), 1)
                    ada_scale(0, 8, R_NMIX)
                modulate(l, 0, True)
                segment(2 * WBLK + 4)

                def in_round(r):
                    for j in range(3):
                        v = use(2)
                        for t in range(TT):
                            src, free = O_in(v) if j == 2 else A_in(v)
                            V.tensor_copy(proj[:, t, bass.ds(r * (3 * W) + j * W, W)], src[:, :]).then_inc(free, 1)
                if l == 0:
                    last = WBLK // 3 - 1
                    with rounds(dve, 0, last, {b.raw: 12, b.hl: 12, b.hl_in: 12, b.A: 4, b.O: 2, b.T: 2, b.ada: 6, b.link: 12}) as r:
                        in_round(r)
                        ada_columns(0, r * 12 + 4 * FIRST, 1)
                        ada_columns(0, r * 12 + 4 * FIRST + 4, 2)
                    in_round(last)
                    ada_columns(0, last * 12 + 4 * FIRST, 1)
                    ada_columns(0, last * 12 + 4 * FIRST + 4, 1)
                    ada_scale(0, 32, R_NFFN)
                else:
                    with rounds(dve, 0, WBLK // 3, {b.raw: 6, b.hl: 12, b.hl_in: 12, b.A: 4, b.O: 2}) as r:
                        in_round(r)
                dve.drain().then_inc(proj_ready, 1)
                z = fox[:, 0, :].rearrange("p (t h) -> p t h", t=TT)
                dve.wait_ge(proj_ready, l + 1)
                link(V.tensor_tensor(z, proj[:, :, C_FF:C_FF + 8], bc(fbias[:, l, :].unsqueeze(1), [P, TT, 8]), ALU.add))
                link(V.tensor_scalar(fox[:, 1, :], fox[:, 0, :], -1.0, None, ALU.mult))
                V.tensor_tensor(fox[:, 1, :], fox[:, 1, :], fox[:, 0, :], ALU.min).then_inc(z_ready, 1)
                b.T.take()
                dve.wait_ge(T_free[b.T.slot(b.T.n - 1)], b.T.before(b.T.n - 1) + 1)
                V.memset(win_hi[:, :, 480:578].bitcast(F32), 0.0)
                V.memset(win_lo[:, :, 480:578].bitcast(F32), 0.0)
                for kv in range(2):
                    for g in range(2):
                        for jh in range(2):
                            v = kk[:, 2 * kv + g, :].rearrange("p (m j s) -> p s j m", j=8, s=2)[:, 0, :, jh:jh + NCMP]
                            pe_c = cols[:, l, R_PEK + 16 * kv + 8 * jh:R_PEK + 16 * kv + 8 * jh + 8].unsqueeze(2)
                            ins = V.tensor_tensor(win[:, kv, 8 * jh:8 * jh + 8, g, :], v, bc(pe_c, [P, 8, NCMP]), ALU.add)
                ins.then_inc(win_ready, 1)
                dve.wait_ge(win_hi_ready, l + 1)
                V.tensor_tensor(win_lo[:, :, 0:480], win[:, :, :, :, :].rearrange("p v j g n -> p v (j g n)"),
                                win_hi[:, :, 0:480].bitcast(F32), ALU.subtract).then_inc(win_lo_ready, 1)
                use(4)
                skip(b.A, 2)
                b.T.take()
                dve.wait_ge(e_ready, l + 1)
                V.scalar_tensor_tensor(fox[:, 3, :], fox[:, 0, :], 0.0, fox[:, 2, :], ALU.min, ALU.subtract).then_inc(ls_ready, 1)
                po, free = O_in()
                V.tensor_copy(kcT[0:HD, 0:30], po[0:HD, 0:30])
                V.tensor_copy(vc[0:NCMP, :, :], po[0:NCMP, HD:3 * HD].rearrange("p (g d) -> p g d", g=2)).then_inc(free, 1)
                po, free = O_in()
                cs = po[:, 0:16].rearrange("p (t h) -> p t h", t=TT)
                V.tensor_scalar(cum[:, :, :, 0], cs, 1.0 / SCALE, None, ALU.mult)
                link(V.tensor_scalar(cum[:, :, :, 1], cs, -1.0 / SCALE, None, ALU.mult))
                dve.drain().then_inc(free, 1)
                dve.drain().then_inc(cum_ready, 1)
                dve.wait_ge(sig_ready, l + 1)
                for c in range(len(CALLS) + 1):
                    if c < len(CALLS):
                        scores(c, l)
                    if c:
                        values(c - 1, l)
                        if c - 1 in WHOLE:
                            m = WHOLE[c - 1]
                            for q in range(2):
                                pt, free = T_in()
                                dve.wait_ge(oT_hi_ready, 6 * l + 2 * m + q + 1)
                                V.tensor_tensor(oT_lo[m][:, 2 * q:2 * q + 2, :], pt[:, :].rearrange("p (k n) -> p k n", k=2),
                                                oT_hi[m][:, 2 * q:2 * q + 2, :].bitcast(F32), ALU.subtract).then_inc(oT_ready, 1)
                                dve.drain().then_inc(free, 1)
                segment(3 * 3 * 2 + 4)
                for half in range(2):
                    for m in range(3):
                        v = use(2)
                        skip(b.A, 2)
                        v = use(1)
                        n_go[0] += 1
                        for t in range(TT):
                            pa, free = A_in(v)
                            if t == 0:
                                dve.wait_ge(A_free[b.A.slot(b.A.n - 2)], b.A.before(b.A.n - 2) + 1)
                            dst = merged[t][:, half * W:(half + 1) * W]
                            if m == 0:
                                V.tensor_tensor(dst, pa[:, :], gate[:, t, :], ALU.mult).then_inc(free, 1)
                            else:
                                V.tensor_tensor(tmp[:, :], pa[:, :], gate[:, t, :], ALU.mult).then_inc(free, 1)
                                dve.wait_ge(free, b.A.before(b.A.n - 1) + 1)
                                link(V.tensor_tensor(dst, dst, tmp[:, :], ALU.add))
                        dve.drain().then_inc(g_used, 1)
                        if l == 0:
                            ada_columns(1, 4 * (3 * half + m), 1)
                dve.drain().then_inc(merged_ready, 1)
                for q in range(4):
                    pt, free = T_in()
                    n_hi[0] += 1
                    dve.wait_ge(h_hi_ready, n_hi[0])
                    V.tensor_tensor(h_lo[:, 2 * q:2 * q + 2, :], pt[:, :].rearrange("p (k n) -> p k n", k=2),
                                    h_hi[:, 2 * q:2 * q + 2, :].bitcast(F32), ALU.subtract).then_inc(h_ready, 1)
                    dve.drain().then_inc(free, 1)

                def gate_rows():
                    for half in range(2):
                        pa, free = A_in()
                        V.tensor_copy(gw[:, half * W:(half + 1) * W], pa[:, :]).then_inc(free, 1)
                        dve.wait_ge(free, b.A.before(b.A.n - 1) + 1)
                gate_rows()
                for half in range(2):
                    v = use(2)
                    for t in range(TT):
                        pa, free = A_in(v)
                        V.tensor_tensor(tmp[:, :], pa[:, :], gw[:, half * W:(half + 1) * W], ALU.mult).then_inc(free, 1)
                        dve.wait_ge(free, b.A.before(b.A.n - 1) + 1)
                        link(V.tensor_tensor(x[:, t, half * W:(half + 1) * W], x[:, t, half * W:(half + 1) * W], tmp[:, :], ALU.add))
                normalise().then_inc(y_ready, 1)
                if l % 2 == 0:
                    modulate(l, 1, True)
                    link(V.memset(yacc[:, :, :], 0.0))
                    segment(6 * FFB + 3)
                    av, aq = Turn(), Turn()

                    def hidden(width=W):
                        v = av.take()
                        dve.wait_ge(g_free, av.done(v))
                        dve.wait_ge(half_used, b.hl.done(b.hl.n - 1))
                        for t in range(TT):
                            ins = V.tensor_tensor(a_sb[:, t, 0:width], a_sb[:, t, 0:width], pA[2 + t][:, 0:width], ALU.mult)
                        ins.then_inc(a_ready, 1)
                        dve.drain().then_inc(u_free, 1)

                    def lo_a(n):
                        for q in range(n):
                            pt, free = T_in()
                            v = aq.take()
                            dve.wait_ge(aT_hi_ready, aq.done(v))
                            V.tensor_tensor(aT_lo[:, 2 * q:2 * q + 2, :], pt[:, :].rearrange("p (k n) -> p k n", k=2),
                                            aT_hi[:, 2 * q:2 * q + 2, :].bitcast(F32), ALU.subtract).then_inc(free, 1)

                    def add_down(t, half, chunk=None):
                        po, free = O_in(chunk)
                        dst = yacc[:, t, half * W:(half + 1) * W]
                        V.tensor_tensor(dst, dst, po[:, :], ALU.add).then_inc(free, 1)

                    def down():
                        for half in range(2):
                            v = use(1)
                            add_down(0, half)
                            add_down(1, half, v)
                    use(2)
                    use(2)
                    hidden()
                    with rounds(dve, 0, FFB // 2, {b.raw: 18, b.hl: 24, b.hl_in: 24, b.T: 6, b.O: 8, b.Of: 4, av: 2, aq: 4, b.ada: 6, b.link: 12}) as r:
                        for _ in range(2):
                            use(2)
                            lo_a(2)
                            use(2)
                            hidden()
                            down()
                        ada_columns(l + 1, r * 12 + 4 * IN_MERGE, 2)
                        ada_columns(l + 1, r * 12 + 4 * IN_MERGE + 8, 1)
                    ada_scale(l + 1, 8, R_NMIX)
                    ada_scale(l + 1, 32, R_NFFN)
                    use(1)
                    lo_a(2)
                    use(1)
                    hidden(W // 2)
                    down()
                    lo_a(1)
                    v = use(1)
                    for i in range(4):
                        add_down(i % 2, i // 2, v if i == 3 else None)
                    dve.wait_ge(O_free[0], b.O.n // 2)
                    dve.wait_ge(O_free[1], b.O.n // 2)
                    gate_rows()
                else:
                    modulate(l, 1, False)
                    pa, free = A_in()
                    r = lambda i: rs[:, i, :]
                    te = lambda i: rs[:, i, :].rearrange("p (t e) -> p t e", t=TT)
                    V.tensor_copy(r(1), pa[:, 0:TT * NE]).then_inc(free, 1)
                    dve.wait_ge(free, b.A.before(b.A.n - 1) + 1)
                    link(V.tensor_reduce(r(3)[:, 0:TT], te(1), AX_X, ALU.max))
                    V.tensor_tensor(te(2), te(1), bc(r(3)[:, 0:TT].unsqueeze(2), [P, TT, NE]), ALU.subtract).then_inc(log_ready, 1)
                    for t in range(TT):
                        other = bc(te(1)[:, t, :].unsqueeze(1), [P, NE, NE])
                        own = bc(te(1)[:, t, :].unsqueeze(2), [P, NE, NE])
                        link(V.tensor_tensor(rt[:, t, :, :], other, own, ALU.is_equal))
                        link(V.tensor_tensor(rt[:, t, :, :], rt[:, t, :, :], ties, ALU.mult))
                        link(V.tensor_tensor(rt2[:, :, :], other, own, ALU.is_gt))
                        link(V.tensor_tensor(rt[:, t, :, :], rt[:, t, :, :], rt2[:, :, :], ALU.add))
                    link(V.tensor_reduce(te(4), rt[:, :, :, :], AX_X, ALU.add))
                    V.tensor_scalar(r(0), r(4), 2.0, None, ALU.is_lt).then_inc(sel_ready, 1)
                    dve.wait_ge(sel_ready, 1)
                    dve.wait_ge(re_ready, 1)
                    link(V.tensor_tensor(r(5), r(2), r(0), ALU.mult))
                    link(V.tensor_reduce(r(6)[:, 0:TT], te(5), AX_X, ALU.add))
                    link(V.reciprocal(r(7)[:, 0:TT], r(6)[:, 0:TT]))
                    for i in range(2):
                        link(V.tensor_tensor(gate16[:, :, i * NE:(i + 1) * NE], te(5), bc(r(7)[:, 0:TT].unsqueeze(2), [P, TT, NE]), ALU.mult))
                    pa, free = A_in()
                    link(V.tensor_tensor(te(8), pa[:, 0:2 * NE].rearrange("p (t e) -> p t e", t=TT), te(0), ALU.mult))
                    link(V.tensor_scalar(slot16[:, :, 0:NE], te(8), -1.0, None, ALU.add))
                    link(V.tensor_scalar(slot16[:, :, NE:2 * NE], te(8), -1.0 - P, None, ALU.add))
                    link(V.tensor_reduce(r(9)[:, 0:1], pa[:, 2 * NE:3 * NE], AX_X, ALU.max))
                    dve.drain().then_inc(free, 1)
                    link(V.tensor_scalar(r(9)[:, 1:2], r(9)[:, 0:1], float(P), float(NE), ALU.is_gt, ALU.mult))
                    link(V.tensor_scalar(flag[:, 0:1], r(9)[:, 1:2], float(NE), None, ALU.add))
                    gate_rows()
                    link(V.memset(slot16[:, :, 2 * NE:], -1.0))
                    link(V.memset(yacc[:, :, :], 0.0))
                    dve.drain().then_inc(slots_ready, 1)
                    items = dve.value_load(flag[0:1, 0:1], min_val=NE, max_val=2 * NE)
                    av, aq, xv = Turn(start=FFB + 1), Turn(start=2 * FFB + 1), Turn()

                    def one_hot(e):
                        for t in range(TT):
                            ins = V.tensor_scalar(sel[:, t, :], iota, slot16[:, t, bass.ds(e, 1)], None, ALU.is_equal)
                        ins.then_inc(sel_ready, 1)

                    def gathered():
                        for q in range(2):
                            pt, free = T_in()
                            for j in range(4):
                                k = 4 * q + j
                                ins = V.tensor_scalar(x_f[:, k, :], pt[:, j * P:(j + 1) * P], mod[:, l, 32 + k:33 + k],
                                                      mod[:, l, 24 + k:25 + k], ALU.mult, ALU.add)
                            ins.then_inc(xf_ready, 1)
                            dve.drain().then_inc(free, 1)

                    def lo_x(at):
                        for q in range(2):
                            dve.wait_ge(x_hi_ready, at + q + 1)
                            V.tensor_tensor(x_lo[:, 4 * q:4 * q + 4, :], x_f[:, 4 * q:4 * q + 4, :],
                                            x_hi[:, 4 * q:4 * q + 4, :].bitcast(F32), ALU.subtract).then_inc(x_ready, 1)
                    one_hot(0)
                    segment(6 * EFB)
                    gathered()
                    lo_x(0)
                    with rounds(dve, 0, items, {b.raw: 42, b.hl: 84, b.hl_in: 84, b.T: 22, b.O: 2, av: EFB, aq: 2 * EFB, xv: 1}) as e:
                        xe = xv.take()
                        skip(b.T, 2)

                        def hidden():
                            v = av.take()
                            dve.wait_ge(g_free, av.done(v))
                            dve.wait_ge(half_used, b.hl.done(b.hl.n - 1))
                            V.tensor_tensor(a_sb[:, 0, :], a_sb[:, 0, :], pA[2][:, :], ALU.mult).then_inc(a_ready, 1)
                            dve.drain().then_inc(u_free, 1)

                        def lo_a():
                            for q in range(2):
                                pt, free = T_in()
                                v = aq.take()
                                dve.wait_ge(aT_hi_ready, aq.done(v))
                                V.tensor_tensor(aT_lo[:, 2 * q:2 * q + 2, 0:P], pt[:, 0:SEQ].rearrange("p (k n) -> p k n", k=2),
                                                aT_hi[:, 2 * q:2 * q + 2, 0:P].bitcast(F32), ALU.subtract).then_inc(free, 1)
                        use(4)
                        hidden()
                        dve.wait_ge(T_full, b.T.done(b.T.n - 1))
                        one_hot(e + 1)
                        with rounds(dve, 1, EFB, {b.raw: 6, b.hl: 12, b.hl_in: 12, b.T: 2, av: 1, aq: 2}):
                            use(2)
                            lo_a()
                            use(2)
                            hidden()
                            use(2)
                        gathered()
                        lo_a()
                        lo_x(xv.done(xe, 2))
                        v = use(2)
                        with dve.If(e < items - 1):
                            ahead()
                        b.O.take()
                        po, free = O_in(v)
                        V.tensor_copy(oe[:, W:2 * W], po[:, :]).then_inc(free, 1)
                        for t in range(TT):
                            for half in range(2):
                                pt, free = T_in()
                                dst = yacc[:, t, half * W:(half + 1) * W]
                                V.scalar_tensor_tensor(dst, pt[:, :], gate16[:, t, bass.ds(e, 1)], dst, ALU.mult, ALU.add).then_inc(free, 1)
                    link(dve.drain())
                for t in range(TT):
                    for half in range(2):
                        c = slice(half * W, (half + 1) * W)
                        link(V.tensor_tensor(yacc[:, t, c], yacc[:, t, c], gw[:, c], ALU.mult))
                        link(V.tensor_tensor(x[:, t, c], x[:, t, c], yacc[:, t, c], ALU.add))
            link(normalise())
            dve.wait_ge(late_in, 16)
            for t in range(TT):
                ins = V.tensor_tensor(y[:, t, :], y[:, t, :], gw[:, :], ALU.mult)
            ins.then_inc(fin_ready, 1)


NAMES = ["x", "c", "ada_w", "ada_b", "norm_mix", "norm_ffn", "w_in", "cmp_k_pe", "cmp_k_w1", "cmp_k_w2", "cmp_v_pe",
         "cmp_v_w1", "cmp_v_w2", "fox_f_bias", "w_read_nsa", "w_read_ret", "w_read_fox", "w_out", "ffn_w1", "ffn_w3",
         "ffn_w2", "router_w", "moe_w1", "moe_w3", "moe_w2", "final_norm"]


def kernel(**inputs):
    import concourse.bacc as bacc
    from concourse.bass_utils import run_bass_kernel_spmd

    nc = bacc.Bacc("TRN2", target_bir_lowering=False, num_devices=1)
    arrays, aps = {}, {}
    for name in NAMES:
        v = np.ascontiguousarray(inputs[name])
        arrays[f"in_{name}"] = v
        aps[name] = nc.dram_tensor(f"in_{name}", v.shape, mybir.dt.from_np(v.dtype), kind="ExternalInput").ap()
    arrays["in_tables"] = tables()
    table = nc.dram_tensor("in_tables", (P, TABLE_W), F32, kind="ExternalInput").ap()
    out = nc.dram_tensor("out_0", (1, SEQ, D), F32, kind="ExternalOutput").ap()
    build(nc, aps, table, out)
    return run_bass_kernel_spmd(nc, [arrays], core_ids=[0]).results[0]["out_0"]
```

```python
from contextlib import ExitStack, contextmanager

import numpy as np
import concourse.bass as bass
from concourse import mybir

F32 = mybir.dt.float32
F32R = mybir.dt.float32r
I32 = mybir.dt.int32
BF16 = mybir.dt.bfloat16
ALU = mybir.AluOpType
ACT = mybir.ActivationFunctionType
AX_X = mybir.AxisListType.X

P = 128
D = 1024
KB = D // P
SEQ = 256
TT = SEQ // P
DEPTH = 2
HD = 64
EPS = 1e-6
NEG = -1e30
SCALE = HD ** -0.5
HG = 4
C_NQ, C_NKC, C_NVC, C_NKS, C_NVS, C_NKW, C_NVW, C_NG = 0, 512, 640, 768, 896, 1024, 1152, 1280
C_RQ, C_RK, C_RV, C_RG = 1304, 1560, 1816, 2328
C_FQ, C_FK, C_FV, C_FF, C_MG = 2840, 3352, 3864, 4376, 4384

CMP_LEN, CMP_STRIDE, CMP_HID = 32, 16, 256
NCMP = (SEQ - CMP_LEN) // CMP_STRIDE + 1
FF = 2816
FFE = 3584
NE = 8
W = 512
CK = 4
CHUNK = CK * W
RAW = 6
HALF = CHUNK // 2
HL = 4
AHEAD = HL - 1
ADA = 6 * D // W
WBLK = 9
PROJ = WBLK * W
assert PROJ >= C_MG and WBLK % 3 == 0
FFB = FF // W
EFB = FFE // W
assert FF == FFB * W + W // 2 and FFE == EFB * W

TABLES = {}
_at = 0
for _n, _w in (("ident", P), ("tri", P), ("ones", P), ("iota", P), ("mask", 2 * P), ("cmask", TT * HG * 16),
               ("cvalid", 2), ("rope", 2 * 2 * HD), ("decay", 4 * 2 * P), ("ties", NE * NE)):
    TABLES[_n] = (_at, _w)
    _at += _w
TABLE_W = _at

R_ADAB, R_NMIX, R_NFFN, R_PEK, R_PEV, R_C = 0, 48, 56, 64, 80, 96
ROWS = 104


def tables():
    f = np.float32
    t = np.zeros((P, TABLE_W), f)

    def put(name, a):
        at, w = TABLES[name]
        t[:, at:at + w] = np.asarray(a, f).reshape(P, w)

    i = np.arange(P)
    put("ident", np.eye(P))
    put("tri", i[:, None] <= i[None, :])
    put("ones", np.ones((P, P)))
    put("iota", np.broadcast_to(i, (P, P)))
    causal = np.where(i[None, :] <= i[:, None], 0.0, NEG)
    put("mask", np.concatenate([np.zeros((P, P)), causal], 1))
    tok = np.arange(SEQ).reshape(TT, P)
    end = np.arange(16) * CMP_STRIDE + CMP_LEN - 1
    open_ = (end[None, None, :] <= tok[:, :, None]) & (np.arange(16) < NCMP)
    cm = np.where(open_, 0.0, NEG).transpose(1, 0, 2)[:, :, None, :]
    cm = np.broadcast_to(cm, (P, TT, HG, 16))
    put("cmask", cm)
    put("cvalid", open_.any(-1).T)
    inv = f(10000.0) ** (-np.arange(0, HD, 2, dtype=f) / f(HD))
    ang = np.arange(SEQ, dtype=f)[:, None] * inv[None, :]
    cos = np.concatenate([np.cos(ang)] * 2, 1)
    sin = np.concatenate([-np.sin(ang), np.sin(ang)], 1)
    put("rope", np.stack([cos.reshape(TT, P, HD), sin.reshape(TT, P, HD)], 0).transpose(2, 0, 1, 3))
    log_g = np.log(f(1.0) - f(2.0) ** (f(-5.0) - np.arange(4, dtype=f)))
    diff = (np.arange(2 * P)[None, :] - i[:, None]).astype(f)
    dec = np.where(diff[:, None, :] >= 0, np.exp(np.maximum(diff, 0)[:, None, :] * log_g[None, :, None]), 0.0)
    put("decay", dec * f(SCALE))
    put("ties", np.broadcast_to(np.tril(np.ones((NE, NE)), -1), (P, NE, NE)))
    return t


class Turn:

    def __init__(self, size=1, start=0):
        self.size, self.n, self.loops = size, start, []

    def take(self):
        self.n += 1
        return self.n - 1

    def done(self, v, times=1):
        out = (v + 1) * times
        for reg, per in self.loops:
            out = reg * (per * times) + out
        return out

    def slot(self, v):
        return v % self.size

    def before(self, v):
        out = v // self.size
        for reg, per in self.loops:
            out = reg * (per // self.size) + out
        return out


@contextmanager
def rounds(eng, first, end, turns):
    at = [t.n for t in turns]
    with eng.Fori(first, end) as reg:
        for t, per in turns.items():
            assert per % t.size == 0
            t.loops.append((reg - first if first else reg, per))
        yield reg
        for t, n in zip(turns, at):
            assert t.n == n + turns[t], (t.n - n, turns[t])
            t.loops.pop()
    if isinstance(end, int):
        for t, n in zip(turns, at):
            t.n = n + turns[t] * (end - first)


class Books:

    def __init__(self):
        self.raw, self.ada = Turn(RAW), Turn()
        self.hl, self.hl_in = Turn(HL), Turn(HL)
        self.end = 0
        self.A, self.T, self.O = Turn(4), Turn(2), Turn(2)
        self.Af, self.Of = Turn(), Turn()
        self.link = Turn()


CALLS = [("cmp", 0), ("sel", 0), ("win", 0), ("cmp", 1), ("sel", 1), ("win", 1), ("ret", 0), ("fox", 0), ("fox", 1)]
WHOLE = {5: 0, 6: 1, 8: 2}
STEPS = [s.split() for s in
         "w 0|w 1|w 2|k 0|w 3|k 1|w 8|k 2|a 0|w 4|a 1|b 0|f 0|w 5|a 2|b 1|w 6|"
         "a 3|b 2|w 7|a 4|b 3|a 5|b 4|a 6|b 5|o 0|a 7|b 6|m 0 0|o 1|a 8|b 7|m 0 1|m 1 0|b 8|m 1 1|o 2|m 2 0|m 2 1".split("|")]
STEPS = [(s[0], *map(int, s[1:])) for s in STEPS]
ORDER = [s[1] for s in STEPS if s[0] == "w"]
assert sorted(ORDER) == list(range(WBLK))


def blocks_by(c0, c1):
    return max(ORDER.index(j) for j in range(c0 // W, (c1 - 1) // W + 1)) + 1


FIRST = 4
IN_MIX = 14
BEHIND_MIX = [0] + [2] * 6 + [1] * 14 + [2]
BEHIND_DENSE = (0, 1, 1, 0, 1, 0, 0, 1, 1, 0, 1, 0)
DENSE_ADA = FIRST + IN_MIX - ADA
assert FFB % 2 and sum(BEHIND_MIX) == 2 * IN_MIX and len(BEHIND_MIX) == 2 * WBLK + 4
assert FIRST + IN_MIX + FFB // 2 * 3 == DEPTH * ADA
MIX_CHUNKS = 2 * WBLK + 4 + 3 * 3 * 2 + 4
DENSE_CHUNKS = 6 * FFB + 3
BEHIND = dict(enumerate(BEHIND_MIX + [0] * (3 * 3 * 2 + 4 + 4) + list(BEHIND_DENSE) * (FFB // 2)))


def ada_buffer(n):
    return n % 4 if n < FIRST + IN_MIX else (n - FIRST - IN_MIX) % 3


def ada_blocks(first, last):
    count = lambda c: FIRST + sum(BEHIND[i] for i in range(c)) // 2
    return range(count(first), count(last)) if last <= len(BEHIND_MIX) else range(0)


S_COUNT = {"cmp": 1, "sel": 2, "win": 2, "ret": 1, "fox": 2}
P_COUNT = {"cmp": 1, "sel": 2, "win": 2, "ret": 0, "fox": 2}
S_SIGNALS = sum(S_COUNT[k] for k, _ in CALLS)
P_SIGNALS = sum(P_COUNT[k] for k, _ in CALLS)


def build(nc, a, table, out):
    ctx = ExitStack()
    with ctx:
        def sem(name):
            return ctx.enter_context(nc.semaphore(name))

        here = [(nc.sbuf_base + 63) // 64 * 64]

        def sb(name, shape, dt=F32, at=None):
            size = 4
            for s in shape[1:]:
                size *= s
            if dt == BF16:
                size //= 2
            off = here[0] if at is None else at
            t = nc.alloc_sbuf_tensor_at(name, shape, dt, offset=off)
            if at is None:
                here[0] += (size + 31) // 32 * 32
            return t

        raw = [sb(f"raw{i}", [P, CHUNK]) for i in range(RAW)]
        w_hi = [sb(f"w_hi{i}", [P, HALF], F32R) for i in range(HL)]
        w_lo = [sb(f"w_lo{i}", [P, HALF], F32R) for i in range(HL)]
        tab = sb("tab", [P, TABLE_W])
        x = sb("x", [P, TT, D])
        h_hi = sb("h_hi", [P, KB, SEQ], F32R)
        h_lo = sb("h_lo", [P, KB, SEQ], F32R)
        rows = [sb(f"rows{i}", [P, P]) for i in range(DEPTH)]
        cols = sb("cols", [P, DEPTH, P])
        csilu = sb("csilu", [P, KB])
        mod = sb("mod", [P, DEPTH, 48])
        fbias = sb("fbias", [P, DEPTH, 8])
        w2c = sb("w2c", [P, DEPTH, 2, 2, HD])
        routw = sb("routw", [P, KB, NE])
        zeros = sb("zeros", [P, W], BF16)
        gates3 = sb("gates3", [P, TT, 24])
        nrm = sb("nrm", [P, 16])
        flag = sb("flag", [P, 4], I32)
        oT_hi, oT_lo = [None] * 3, [None] * 3
        rope_t = sb("rope_t", [P, 8, HD])
        tmp = sb("tmp", [P, W])
        acc = [sb(f"acc{i}", [P, W], at=(here[0] + 31) // 32 * 32 + 2048 * i) for i in range(4)]
        oT_hi[0] = sb("oTn_hi", [P, 4, SEQ], F32R)
        oT_lo[0] = sb("oTn_lo", [P, 4, SEQ], F32R)

        area = here[0]
        proj = sb("proj", [P, TT, PROJ])
        PR = PROJ * 4
        oT_hi[1] = sb("oTr_hi", [P, 4, SEQ], F32R, at=area + C_RQ * 4)
        oT_lo[1] = sb("oTr_lo", [P, 4, SEQ], F32R, at=area + PR + C_RQ * 4)
        gate = [sb(f"gate{t}", [P, W], at=area + t * PR + C_RQ * 4 + 4096) for t in range(TT)]
        assert C_RQ * 4 + 4096 + 4 * W <= C_FQ * 4 and 4 * D <= C_RQ * 4
        oT_hi[2] = sb("oTf_hi", [P, 4, SEQ], F32R, at=area + C_FQ * 4)
        oT_lo[2] = sb("oTf_lo", [P, 4, SEQ], F32R, at=area + PR + C_FQ * 4)
        merged = [sb(f"merged{t}", [P, D], at=area + t * PR) for t in range(TT)]
        work = here[0]
        qT = sb("qT", [P, HG, SEQ])
        kT = [sb(f"kT{i}", [P, HG, SEQ]) for i in range(2)]
        S = [sb(f"S{i}", [P, HG * 3 * P]) for i in range(2)]
        PT = sb("PT", [P, HG * 3 * P])
        o_sb = sb("o_sb", [P, TT, W])
        stat = sb("stat", [P, 96])
        fox_st = sb("fox_st", [P, 24])
        ret_st = sb("ret_st", [P, 20])
        o_part = sb("o_part", [P, HG * HD])
        end_work = here[0]
        y = sb("y", [P, TT, D], at=area + 4096)
        hf = sb("hf", [P, KB, SEQ], at=area + 12288)
        kk = sb("kk", [P, 4, SEQ], at=work)
        win = sb("win", [P, 2, 16, 2, NCMP], at=work + 4096)
        win_hi = sb("win_hi", [P, 2, 16 * 30 + 98], F32R, at=work + 4096 + 4096)
        win_lo = sb("win_lo", [P, 2, 16 * 30 + 98], F32R, at=work + 4096 + 4096 + 4640)
        hid = sb("hid", [P, 2, CMP_HID], at=work + 17632)
        hidT = sb("hidT", [P, 4, 30], at=work + 19680)
        kcT = sb("kcT", [P, 32])
        vc = sb("vc", [P, 2, HD])
        q_aug = sb("q_aug", [P, TT, HG, HD + 2])
        k_aug = sb("k_aug", [P, TT, HG, HD + 2])
        cum = sb("cum", [P, TT, 8, 2])
        fox = sb("fox", [P, 4, TT * 8])
        assert here[0] <= nc.sbuf_usable_end
        gw = sb("gw", [P, D], at=work + 24576)
        yacc = sb("yacc", [P, TT, D], at=area + 20480)
        a_sb = sb("a_sb", [P, TT, W], at=area + 28672)
        aT_hi = sb("aT_hi", [P, CK, SEQ], F32R, at=work)
        aT_lo = sb("aT_lo", [P, CK, SEQ], F32R, at=work + 4096)
        x_f = sb("x_f", [P, KB, P], at=work + 8192)
        x_hi = sb("x_hi", [P, KB, P], F32R, at=work + 12288)
        x_lo = sb("x_lo", [P, KB, P], F32R, at=work + 16384)
        oe = sb("oe", [P, D], at=area)
        final_w = sb("final_w", [P, D], at=area + 12288)
        sel = sb("sel", [P, TT, P], at=work + 20480)
        selT = sb("selT", [P, TT * P], at=work + 21504)
        rt = sb("rt", [P, TT, NE, NE], at=work + 22528)
        rt2 = sb("rt2", [P, NE, NE], at=work + 23040 + 640)
        rs = sb("rs", [P, 10, TT * NE], at=work + 23040)
        slot16 = sb("slot16", [P, TT, 2 * NE + 1])
        gate16 = sb("gate16", [P, TT, 2 * NE])
        assert work + 23040 + 10 * TT * NE * 4 <= end_work, (end_work - work)
        assert here[0] <= nc.sbuf_usable_end, (here[0], nc.sbuf_usable_end)

        def cst(name):
            at, w = TABLES[name]
            return tab[:, at:at + w]

        ident, tri, ones, iota = cst("ident"), cst("tri"), cst("ones"), cst("iota")
        mask = cst("mask")
        cmask = cst("cmask").rearrange("p (t h n) -> p t h n", t=TT, h=HG)
        cvalid = cst("cvalid")
        rope = cst("rope").rearrange("p (s t d) -> p s t d", s=2, t=TT)
        decay = cst("decay").rearrange("p (h n) -> p h n", h=4)
        ties = cst("ties").rearrange("p (e j) -> p e j", e=NE)

        SMALL = 16 * (DEPTH * 3 + 1)

        def bank(name):
            return ctx.enter_context(nc.psum_tensor(name, [P, W], F32))[:, :]
        pA = [bank(f"pA{i}") for i in range(4)]
        pT = [bank(f"pT{i}") for i in range(2)]
        pO = [bank(f"pO{i}") for i in range(2)]

        landed = [sem(f"landed{i}") for i in range(RAW)]
        hi_ready = sem("hi_ready")
        raw_done = sem("raw_done")
        half_used = sem("half_used")
        A_full = sem("A_full")
        T_full = sem("T_full")
        O_full = sem("O_full")
        A_free = [sem(f"A_free{i}") for i in range(4)]
        T_free = [sem(f"T_free{i}") for i in range(2)]
        O_free = [sem(f"O_free{i}") for i in range(2)]
        tab_in = sem("tab_in")
        x_in = sem("x_in")
        small_in = sem("small_in")
        rows_in = [sem(f"rows_in{i}") for i in range(DEPTH)]
        final_in = sem("final_in")
        cols_ready = sem("cols_ready")
        csilu_ready = sem("csilu_ready")
        dve_link = sem("dve_link")
        act_link = sem("act_link")
        pool_link = sem("pool_link")
        ms_ready = sem("ms_ready")
        rt_ready = sem("rt_ready")
        y_ready = sem("y_ready")
        hf_ready = sem("hf_ready")
        h_hi_ready = sem("h_hi_ready")
        h_ready = sem("h_ready")
        proj_ready = sem("proj_ready")
        roped = sem("roped")
        win_ready = sem("win_ready")
        win_hi_ready = sem("win_hi_ready")
        win_lo_ready = sem("win_lo_ready")
        hid_ready = sem("hid_ready")
        sig_ready = sem("sig_ready")
        z_ready = sem("z_ready")
        e_ready = sem("e_ready")
        ls_ready = sem("ls_ready")
        cum_ready = sem("cum_ready")
        aug_ready = sem("aug_ready")
        s_ready = sem("s_ready")
        p_ready = sem("p_ready")
        var_ready = sem("var_ready")
        dev_ready = sem("dev_ready")
        o_ready = sem("o_ready")
        oT_hi_ready = sem("oT_hi_ready")
        oT_ready = sem("oT_ready")
        g_used = sem("g_used")
        merged_ready = sem("merged_ready")
        g_free = sem("g_free")
        u_free = sem("u_free")
        a_ready = sem("a_ready")
        aT_hi_ready = sem("aT_hi_ready")
        log_ready = sem("log_ready")
        re_ready = sem("re_ready")
        sel_ready = sem("sel_ready")
        slots_ready = sem("slots_ready")
        xf_ready = sem("xf_ready")
        x_hi_ready = sem("x_hi_ready")
        x_ready = sem("x_ready")
        fin_ready = sem("fin_ready")
        stored = sem("stored")

        ctx.enter_context(nc.allow_non_contiguous_dma("small parameter loads"))
        block = ctx.enter_context(nc.Block())

        def chunk_rows(w, k0, c0, width=W, kb=CK):
            return w[bass.ds(k0, kb * P), bass.ds(c0, width)].rearrange("(k p) n -> p k n", p=P)

        @block.sync
        def _(sp):
            b = Books()

            def load(src, kb=CK):
                g = b.raw.take()
                slot = raw[b.raw.slot(g)]
                if g >= RAW or b.raw.loops:
                    sp.wait_ge(raw_done, b.raw.done(g - RAW, 2))
                sp.dma_start(slot[:, :].rearrange("p (k n) -> p k n", k=kb), src).then_inc(landed[b.raw.slot(g)], 16)

            def block8(w, c0):
                for k in range(KB // CK):
                    load(chunk_rows(w, k * CK * P, c0))

            sp.dma_start(tab[:, :], table).then_inc(tab_in, 16)
            for l in range(DEPTH):
                for at, n, src in ((R_ADAB, 48, a["ada_b"][l].rearrange("(r p) -> r p", p=P)),
                                   (R_NMIX, 8, a["norm_mix"][l].rearrange("(r p) -> r p", p=P)),
                                   (R_NFFN, 8, a["norm_ffn"][l].rearrange("(r p) -> r p", p=P)),
                                   (R_PEK, 16, a["cmp_k_pe"][l].rearrange("(j s) d -> j (s d)", s=2)),
                                   (R_PEV, 16, a["cmp_v_pe"][l].rearrange("(j s) d -> j (s d)", s=2)),
                                   (R_C, 8, a["c"].rearrange("a (r p) -> (a r) p", p=P))):
                    sp.dma_start(rows[l][at:at + n, :], src).then_inc(rows_in[l], 16)

            def mixed(sources, ada_chunk):
                n = 0
                for src, *kb in sources:
                    load(src, *kb)
                    for _ in range(BEHIND.get(b.hl.n, 0)):
                        load(ada_chunk(n))
                        n += 1
                    b.hl.take()
                return n

            def ada_source(n):
                l, at = divmod(n, 2 * ADA)
                return chunk_rows(a["ada_w"][l], at % 2 * CK * P, at // 2 * W)

            def block8_sources(w, c0):
                return [(chunk_rows(w, k * CK * P, c0),) for k in range(2)]

            sp.dma_start(x[:, :, :], a["x"][0].rearrange("(t p) d -> p t d", p=P)).then_inc(x_in, 16)
            for j in range(FIRST - 1):
                block8(a["ada_w"][0], j * W)
            for l in range(DEPTH):
                sp.dma_start(fbias[:, l, :], a["fox_f_bias"][l:l + 1, :].broadcast_to([P, 8])).then_inc(small_in, 16)
                for i, name in enumerate(("cmp_k_w2", "cmp_v_w2")):
                    sp.dma_start(w2c[:, l, i, :, :], a[name][l].rearrange("(k p) d -> p k d", p=P)).then_inc(small_in, 16)
            sp.dma_start(routw[:, :, :], a["router_w"][0].rearrange("(k p) e -> p k e", p=P)).then_inc(small_in, 16)
            block8(a["ada_w"][0], (FIRST - 1) * W)
            n_ada = 2 * FIRST
            for l in range(DEPTH):
                for kind, *which in STEPS:
                    if kind == "w":
                        srcs = block8_sources(a["w_in"][l], which[0] * W)
                    elif (kind, which) == ("k", [1]):
                        srcs = [(chunk_rows(a[name][l], half * 8 * P, 0, CMP_HID, 8), 8)
                                for name in ("cmp_k_w1", "cmp_v_w1") for half in range(2)]
                    elif kind == "m":
                        m, half = which
                        srcs = block8_sources(a["w_in"][l], C_MG + m * D + half * W)
                        srcs.append((chunk_rows(a[("w_read_nsa", "w_read_ret", "w_read_fox")[m]][l], 0, half * W),))
                    else:
                        continue
                    n_ada += mixed(srcs, lambda i: ada_source(n_ada + i))
                for half in range(2):
                    block8(a["w_out"][l], half * W)
                b.hl.n += 4 + 4
                if l % 2 == 0:
                    w1, w3, w2 = (a[n][l // 2] for n in ("ffn_w1", "ffn_w3", "ffn_w2"))
                    block8(w1, 0)
                    block8(w3, 0)
                    with rounds(sp, 0, FFB // 2, {b.raw: 18, b.hl: 12}) as r:
                        srcs = []
                        for f in (r * 2 + 1, r * 2 + 2):
                            srcs += block8_sources(w1, f * W) + block8_sources(w3, f * W)
                            srcs += [(chunk_rows(w2, f * W - W, half * W),) for half in range(2)]
                        mixed(srcs, lambda i: chunk_rows(a["ada_w"][l + 1], i % 2 * CK * P, DENSE_ADA * W + r * (3 * W) + i // 2 * W))
                    load(chunk_rows(w1, 0, FFB * W, W // 2, KB), KB)
                    load(chunk_rows(w3, 0, FFB * W, W // 2, KB), KB)
                    for half in range(2):
                        load(chunk_rows(w2, (FFB - 1) * W, half * W))
                    load(chunk_rows(w2, FFB * W, 0, D, 2), 2)
                else:
                    def experts():
                        with rounds(sp, 0, NE, {b.raw: EFB * 6}) as e:
                            w1, w3, w2 = (a[n][l // 2].rearrange("e k n -> (e k) n") for n in ("moe_w1", "moe_w3", "moe_w2"))

                            def up(f0):
                                for w in (w1, w3):
                                    for k in range(2):
                                        load(chunk_rows(w, e * D + k * CK * P, f0))

                            def down(f0):
                                for half in range(2):
                                    load(chunk_rows(w2, e * FFE + f0, half * W))
                            up(0)
                            with rounds(sp, 1, EFB, {b.raw: 6}) as f:
                                up(f * W)
                                down(f * W - W)
                            down((EFB - 1) * W)
                    experts()
                    sp.wait_ge(slots_ready, 1)
                    sp.dma_start(final_w[:, :], a["final_norm"].unsqueeze(0).broadcast_to([P, D])).then_inc(final_in, 16)
                    items = sp.value_load(flag[0:1, 0:1], min_val=NE, max_val=2 * NE)
                    with sp.If(items > NE):
                        experts()
            for t in range(TT):
                sp.wait_ge(fin_ready, t + 1)
                sp.dma_start(out[0, t * P:(t + 1) * P, :], y[:, t, :]).then_inc(stored, 16)
            sp.wait_ge(stored, TT * 16)

        marks = {}

        @block.tensor
        def _(pe):
            b = Books()

            def take(turn, free, banks):
                v = turn.take()
                if turn.loops or turn.before(v):
                    pe.wait_ge(free[turn.slot(v)], turn.before(v))
                return banks[turn.slot(v)]

            take_A = lambda: take(b.A, A_free, pA)
            take_T = lambda: take(b.T, T_free, pT)
            take_O = lambda: take(b.O, O_free, pO)

            def evacuated(turn, free, uses):
                for v in range(turn.n - min(uses, turn.size), turn.n):
                    pe.wait_ge(free[turn.slot(v)], turn.before(v) + 1)

            def mm3(dst, xh, xl, wh, wl, first, last):
                nc.tensor.matmul(dst, xl, wh, start=first, stop=False, skip_group_check=True)
                nc.tensor.matmul(dst, xh, wl, start=False, stop=False, skip_group_check=True)
                return nc.tensor.matmul(dst, xh, wh, start=False, stop=last, skip_group_check=True)

            def mm(dst, lhsT, rhs, first=True, last=True):
                return nc.tensor.matmul(dst, lhsT, rhs, start=first, stop=last, skip_group_check=True)

            def half_in(i):
                h = b.hl.take()
                g = b.raw.take() if i == 0 else b.raw.n - 1
                pe.wait_ge(raw_done, b.raw.done(g, 2) - (1 - i))
                for _ in range(i * BEHIND.get(h // 2, 0)):
                    b.raw.take()
                return w_hi[b.hl.slot(h)], w_lo[b.hl.slot(h)]

            def product(dsts, lhs, chunks, kb=CK, width=W, first=True, last=True):
                kh = kb // 2
                for c in range(2 * chunks):
                    wh, wl = half_in(c % 2)
                    for t, dst in enumerate(dsts):
                        for k in range(kh):
                            xh, xl = lhs(c * kh + k, t)
                            ins = mm3(dst, xh, xl, wh[:, k * width:(k + 1) * width], wl[:, k * width:(k + 1) * width],
                                      first and c + k == 0, last and c == 2 * chunks - 1 and k == kh - 1)
                    ins.then_inc(half_used, 1)

            def of_h(count):
                seen = [-1]

                def lhs(j, t):
                    if j // 2 > seen[0]:
                        seen[0] = j // 2
                        pe.wait_ge(h_ready, count + j // 2)
                    return of(h_hi, h_lo)(j, t)
                return lhs

            def of(hi, lo):
                return lambda j, t: (hi[:, j, t * P:(t + 1) * P], lo[:, j, t * P:(t + 1) * P])

            def turned(blocks, width):
                pt = take_T()
                for i, src in enumerate(blocks):
                    n, m = src.shape[0], src.shape[1]
                    ins = nc.tensor.transpose(pt[0:m, i * width:i * width + n], src, ident[0:n, 0:n])
                ins.then_inc(T_full, 1)

            def turn8(src):
                for q in range(KB // 2):
                    turned([src(t, 2 * q + j) for j in range(2) for t in range(TT)], P)

            def gate_row(l, which):
                for half in range(2):
                    dst = take_A()
                    for k in range(4):
                        at = which * 8 + half * 4 + k
                        ins = mm(dst[:, k * P:(k + 1) * P], mod[:, l, at:at + 1].broadcast_to([P, P]), ident)
                    ins.then_inc(A_full, 1)

            def ada_ended(first):
                for n in ada_blocks(first, b.hl.n // 2):
                    ada_sum(n)

            def head(c0, h, t, w=HD):
                return proj[:, t, c0 + h * w:c0 + (h + 1) * w]

            def heads_T(c0, g, n):
                for p0 in range(0, n, 2):
                    turned([head(c0, g * HG + h, t) for h in range(p0, min(p0 + 2, n)) for t in range(TT)], P)

            pe.wait_ge(tab_in, 16)
            for l in range(DEPTH):
                pe.wait_ge(rows_in[l], 6 * 16)
                turned([rows[l][0:ROWS, :]], P)
            def ada_sum(*which):
                pe.wait_ge(raw_done, b.raw.done(b.raw.n - 1, 2))
                pt = take_T()
                for i, n in enumerate(which):
                    for k in range(4):
                        ins = mm(pt[:, 4 * i + k:4 * i + k + 1], acc[ada_buffer(n)][:, k * P:(k + 1) * P], ones[:, 0:1])
                ins.then_inc(T_full, 1)

            for j in range(FIRST):
                for _ in range(2):
                    b.raw.take()
                ada_sum(j)

            def attention_scores(c, l):
                kind, g = CALLS[c]
                kt = kT[c % 2]
                if kind == "cmp":
                    if g == 0:
                        pe.wait_ge(roped, 3 * l + 2)
                    heads_T(C_NQ, g, HG)
                    evacuated(b.T, T_free, 2)
                    dst = take_A()
                    for t in range(TT):
                        for h in range(HG):
                            at = (t * HG + h) * 16
                            ins = mm(dst[:, at:at + NCMP], qT[0:HD, h, t * P:(t + 1) * P], kcT[0:HD, g * NCMP:(g + 1) * NCMP])
                    ins.then_inc(A_full, 1)
                    return
                if kind in ("sel", "win"):
                    c0 = C_NKS if kind == "sel" else C_NKW
                    turned([head(c0, g, t) for t in range(TT)], P)
                    evacuated(b.T, T_free, 1)
                    kd, one = HD, True
                elif kind == "ret":
                    pe.wait_ge(roped, 3 * l + 3)
                    heads_T(C_RQ, 0, HG)
                    heads_T(C_RK, 0, HG)
                    evacuated(b.T, T_free, 2)
                    for p0 in range(0, HG, 2):
                        dst = take_A()
                        for h in range(p0, p0 + 2):
                            ins = mm(dst[:, (h - p0) * SEQ:(h - p0 + 1) * SEQ], kt[0:HD, h, 0:P], qT[0:HD, h, :])
                        ins.then_inc(A_full, 1)
                    dst = take_A()
                    for h in range(HG):
                        ins = mm(dst[:, h * P:(h + 1) * P], kt[0:HD, h, P:SEQ], qT[0:HD, h, P:SEQ])
                    ins.then_inc(A_full, 1)
                    return
                else:
                    pe.wait_ge(aug_ready, 2 * l + g + 1)
                    for aug in (q_aug, k_aug):
                        for p0 in range(0, HG, 2):
                            turned([aug[:, t, h, :] for h in range(p0, p0 + 2) for t in range(TT)], P)
                    marks[l, g] = b.T.n
                    evacuated(b.T, T_free, 2)
                    kd, one = HD + 2, False
                dst = take_A()
                for h in range(HG):
                    ins = mm(dst[:, h * P:(h + 1) * P], qT[0:kd, h, 0:P], kt[0:kd, 0 if one else h, 0:P])
                ins.then_inc(A_full, 1)
                for p0 in range(0, HG, 2):
                    dst = take_A()
                    for h in range(p0, p0 + 2):
                        ins = mm(dst[:, (h - p0) * SEQ:(h - p0 + 1) * SEQ], qT[0:kd, h, P:SEQ], kt[0:kd, 0 if one else h, :])
                    ins.then_inc(A_full, 1)

            def attention_values(c, l):
                kind, g = CALLS[c]
                s = S[c % 2]
                if kind == "ret":
                    pe.wait_ge(s_ready, S_SIGNALS * l + sum(S_COUNT[k] for k, _ in CALLS[:c + 1]))
                    for t in range(TT):
                        dst = take_O()
                        for h in range(HG):
                            for m in range(t + 1):
                                lhsT = s[:, h * SEQ + t * P:h * SEQ + (t + 1) * P] if m == 0 else s[:, 4 * SEQ + h * P:4 * SEQ + (h + 1) * P]
                                ins = mm(dst[:, h * P:(h + 1) * P], lhsT, proj[:, m, C_RV + h * P:C_RV + (h + 1) * P], m == 0, m == t)
                        ins.then_inc(O_full, 1)
                    return
                p_at = P_SIGNALS * l + sum(P_COUNT[k] for k, _ in CALLS[:c])
                if kind == "cmp":
                    pe.wait_ge(p_ready, p_at + 1)
                    for t in range(TT):
                        turned([s[:, (t * HG + h) * 16:(t * HG + h) * 16 + NCMP] for h in range(HG)], P)
                    evacuated(b.T, T_free, 2)
                    for t in range(TT):
                        dst = take_O()
                        for h in range(HG):
                            ins = mm(dst[:, h * HD:(h + 1) * HD], PT[0:NCMP, (t * HG + h) * P:(t * HG + h + 1) * P], vc[0:NCMP, g, :])
                        ins.then_inc(O_full, 1)
                    return
                v0 = {"sel": C_NVS + g * HD, "win": C_NVW + g * HD, "fox": C_FV + g * HG * HD}[kind]
                vs = HD if kind == "fox" else 0
                pe.wait_ge(p_ready, p_at + 1)
                turned([s[:, h * P:(h + 1) * P] for h in range(HG)], P)
                evacuated(b.T, T_free, 1)
                dst = take_O()
                for h in range(HG):
                    ins = mm(dst[:, h * HD:(h + 1) * HD], PT[:, h * P:(h + 1) * P], proj[:, 0, v0 + h * vs:v0 + h * vs + HD])
                ins.then_inc(O_full, 1)
                pe.wait_ge(p_ready, p_at + 2)
                for p0 in range(0, HG, 2):
                    turned([s[:, HG * P + h * SEQ + m * P:HG * P + h * SEQ + (m + 1) * P] for h in range(p0, p0 + 2) for m in range(2)], P)
                evacuated(b.T, T_free, 2)
                dst = take_O()
                for h in range(HG):
                    for m in range(2):
                        at = (HG + h * 2 + m) * P
                        ins = mm(dst[:, h * HD:(h + 1) * HD], PT[:, at:at + P], proj[:, m, v0 + h * vs:v0 + h * vs + HD], m == 0, m == 1)
                ins.then_inc(O_full, 1)

            def compression(part, l):
                if part == 0:
                    pe.wait_ge(roped, 3 * l + 1)
                    turned([proj[:, t, c0:c0 + 2 * HD] for c0 in (C_NKC, C_NVC) for t in range(TT)], P)
                elif part == 1:
                    pe.wait_ge(win_lo_ready, l + 1)
                    for kv in range(2):
                        dst = take_A()
                        product([dst[:, 0:CMP_HID]], lambda j, t: (win_hi[:, kv, j * 30:j * 30 + P], win_lo[:, kv, j * 30:j * 30 + P]),
                                2, 8, CMP_HID)
                else:
                    pe.wait_ge(small_in, SMALL)
                    pe.wait_ge(hid_ready, 2 * l + 2)
                    turned([hid[0:30, kv, k * P:(k + 1) * P] for kv in range(2) for k in range(2)], 32)
                    evacuated(b.T, T_free, 1)
                    dst = take_O()
                    for k in range(2):
                        mm(dst[0:HD, 0:30], w2c[:, l, 0, k, :], hidT[:, k, :], k == 0, k == 1)
                    for g in range(2):
                        for k in range(2):
                            ins = mm(dst[0:NCMP, HD + g * HD:HD + (g + 1) * HD], hidT[:, 2 + k, g * NCMP:(g + 1) * NCMP], w2c[:, l, 1, k, :], k == 0, k == 1)
                    ins.then_inc(O_full, 1)
                    evacuated(b.O, O_free, 1)

            n_h = [0]

            for l in range(DEPTH):
                pe.wait_ge(y_ready, 2 * l + 1)
                turn8(lambda t, k: y[:, t, k * P:(k + 1) * P])
                n_h[0] += 4
                for kind, *which in STEPS:
                    at = b.hl.n // 2
                    if kind == "w":
                        product([take_A(), take_A()], of(h_hi, h_lo) if which[0] != ORDER[0] else of_h(n_h[0] - 3), 2)
                    elif kind == "k":
                        compression(which[0], l)
                    elif kind == "f":
                        pe.wait_ge(ls_ready, l + 1)
                        dst = take_O()
                        ls = fox[:, 3, :].rearrange("p (t h) -> p t h", t=TT)
                        mm(dst[:, 0:8], tri, ls[:, 0, :])
                        mm(dst[:, 8:16], ones, ls[:, 0, :], True, False)
                        mm(dst[:, 8:16], tri, ls[:, 1, :], False, True).then_inc(O_full, 1)
                    elif kind == "a":
                        attention_scores(which[0], l)
                    elif kind == "b":
                        attention_values(which[0], l)
                    elif kind == "o":
                        pe.wait_ge(o_ready, 3 * l + which[0] + 1)
                        for q in range(2):
                            turned([o_sb[:, t, (2 * q + j) * P:(2 * q + j + 1) * P] for j in range(2) for t in range(TT)], P)
                    else:
                        m, half = which
                        product([take_A(), take_A()], of(h_hi, h_lo), 2)
                        pe.wait_ge(oT_ready, 6 * l + 2 * m + 2)
                        product([take_A(), take_A()], of(oT_hi[m], oT_lo[m]), 1)
                    ada_ended(at)
                pe.wait_ge(merged_ready, l + 1)
                turn8(lambda t, k: merged[t][:, k * P:(k + 1) * P])
                gate_row(l, 2)
                n_h[0] += 4
                for half in range(2):
                    product([take_A(), take_A()], of(h_hi, h_lo) if half else of_h(n_h[0] - 3), 2)
                gate_row(l, 5)
                pe.wait_ge(y_ready, 2 * l + 2)
                turn8(lambda t, k: y[:, t, k * P:(k + 1) * P])

                if l % 2 == 0:
                    n_h[0] += 4
                    G, U, av = Turn(), Turn(), Turn()
                    evacuated(b.A, A_free, 4)

                    def gate_up(banks, turn, free, chunks, kb, width, lhs=of(h_hi, h_lo)):
                        v = turn.take()
                        if turn.loops or v:
                            pe.wait_ge(free, turn.done(v - 1))
                        product([p[:, 0:width] for p in banks], lhs, chunks, kb, width)

                    def turn_a(nb):
                        v = av.take()
                        pe.wait_ge(a_ready, av.done(v))
                        for q in range(nb // 2):
                            turned([a_sb[:, t, (2 * q + j) * P:(2 * q + j + 1) * P] for j in range(2) for t in range(TT)], P)

                    def down(nb):
                        evacuated(b.T, T_free, nb // 2)
                        if nb == CK:
                            for half in range(2):
                                parts = [half_in(0), None]
                                for t in range(TT):
                                    dst = take_O()
                                    for k in range(CK):
                                        if t == 0 and k == CK // 2:
                                            parts[1] = half_in(1)
                                        wh, wl = parts[k // (CK // 2)]
                                        at = k % (CK // 2) * W
                                        xh, xl = of(aT_hi, aT_lo)(k, t)
                                        ins = mm3(dst, xh, xl, wh[:, at:at + W], wl[:, at:at + W], k == 0, k == CK - 1)
                                        if t == 1 and k % (CK // 2) == CK // 2 - 1:
                                            ins.then_inc(half_used, 1)
                                    if t == 0:
                                        ins.then_inc(O_full, 1)
                        else:
                            parts = [half_in(0), half_in(1)]
                            for half in range(2):
                                for t in range(TT):
                                    dst = take_O()
                                    for k, (wh, wl) in enumerate(parts):
                                        xh, xl = of(aT_hi, aT_lo)(k, t)
                                        ins = mm3(dst, xh, xl, wh[:, half * W:(half + 1) * W], wl[:, half * W:(half + 1) * W], k == 0, k == 1)
                                        if half + t == 2:
                                            ins.then_inc(half_used, 1)
                                    if half + t < 2:
                                        ins.then_inc(O_full, 1)
                    gate_up(pA[0:2], G, g_free, 2, CK, W, of_h(n_h[0] - 3))
                    gate_up(pA[2:4], U, u_free, 2, CK, W)
                    with rounds(pe, 0, FFB // 2, {b.raw: 18, b.hl: 24, b.T: 6, b.O: 8, G: 2, U: 2, av: 2}):
                        for _ in range(2):
                            gate_up(pA[0:2], G, g_free, 2, CK, W)
                            turn_a(CK)
                            gate_up(pA[2:4], U, u_free, 2, CK, W)
                            down(CK)
                        n = FIRST + IN_MIX
                        ada_sum(n, n + 1)
                        ada_sum(n + 2)
                    gate_up(pA[0:2], G, g_free, 1, KB, W // 2)
                    turn_a(CK)
                    gate_up(pA[2:4], U, u_free, 1, KB, W // 2)
                    down(CK)
                    turn_a(2)
                    down(2)
                    pe.wait_ge(g_free, G.n)
                    pe.wait_ge(u_free, U.n)
                else:
                    pe.wait_ge(hf_ready, 4 * (2 * l + 2))
                    dst = take_A()
                    for t in range(TT):
                        for k in range(KB):
                            ins = mm(dst[:, t * NE:(t + 1) * NE], hf[:, k, t * P:(t + 1) * P], routw[:, k, :], k == 0, k == KB - 1)
                    ins.then_inc(A_full, 1)
                    pe.wait_ge(sel_ready, 1)
                    dst = take_A()
                    chosen = rs[:, 0, :].rearrange("p (t e) -> p t e", t=TT)
                    mm(dst[:, 0:NE], tri, chosen[:, 0, :])
                    mm(dst[:, NE:2 * NE], ones, chosen[:, 0, :], True, False)
                    mm(dst[:, NE:2 * NE], tri, chosen[:, 1, :], False, True)
                    mm(dst[:, 2 * NE:3 * NE], ones, chosen[:, 0, :], True, False)
                    mm(dst[:, 2 * NE:3 * NE], ones, chosen[:, 1, :], False, True).then_inc(A_full, 1)
                    pe.wait_ge(slots_ready, 1)
                    items = pe.value_load(flag[0:1, 0:1], min_val=NE, max_val=2 * NE)
                    evacuated(b.A, A_free, 4)
                    G, U, av, xv = Turn(start=FFB + 1), Turn(start=FFB + 1), Turn(start=FFB + 1), Turn()

                    def gather():
                        for q in range(2):
                            pt = take_T()
                            for j in range(4):
                                k = 4 * q + j
                                for t in range(TT):
                                    ins = mm(pt[:, j * P:(j + 1) * P], y[:, t, k * P:(k + 1) * P], sel[:, t, :], t == 0, t == 1)
                            ins.then_inc(T_full, 1)
                    pe.wait_ge(sel_ready, 2)
                    gather()
                    with rounds(pe, 0, items, {b.raw: 42, b.hl: 84, b.T: 22, b.O: 2, G: EFB, U: EFB, av: EFB, xv: 1}):
                        v = xv.take()
                        for t in range(TT):
                            turned([sel[:, t, :]], P)
                        outs = [take_O(), take_O()]
                        for o in outs:
                            mm(o[:, :], zeros[:, 0:P], zeros[:, :], True, False)
                        pe.wait_ge(x_ready, xv.done(v, 2))

                        def gate_up(dst, turn, free):
                            v = turn.take()
                            pe.wait_ge(free, turn.done(v - 1))
                            product([dst], lambda j, t: (x_hi[:, j, :], x_lo[:, j, :]), 2)

                        def turn_a():
                            v = av.take()
                            pe.wait_ge(a_ready, av.done(v))
                            for q in range(2):
                                turned([a_sb[:, 0, (2 * q + j) * P:(2 * q + j + 1) * P] for j in range(2)], P)

                        def down(last=False):
                            evacuated(b.T, T_free, 2)
                            for half in range(2):
                                for i in range(2):
                                    wh, wl = half_in(i)
                                    for j in range(CK // 2):
                                        k = i * (CK // 2) + j
                                        ins = mm3(outs[half][:, :], aT_hi[:, k, 0:P], aT_lo[:, k, 0:P],
                                                  wh[:, j * W:(j + 1) * W], wl[:, j * W:(j + 1) * W], False, last and k == CK - 1)
                                    ins.then_inc(half_used, 1)
                        gate_up(pA[0], G, g_free)
                        gate_up(pA[2], U, u_free)
                        with rounds(pe, 1, EFB, {b.raw: 6, b.hl: 12, b.T: 2, G: 1, U: 1, av: 1}):
                            gate_up(pA[0], G, g_free)
                            turn_a()
                            gate_up(pA[2], U, u_free)
                            down()
                        pe.wait_ge(sel_ready, xv.done(v) + 2)
                        gather()
                        turn_a()
                        down(True)
                        evacuated(b.O, O_free, 2)
                        for t in range(TT):
                            for half in range(2):
                                dst = take_T()
                                mm(dst[:, :], selT[:, t * P:(t + 1) * P], oe[:, half * W:(half + 1) * W]).then_inc(T_full, 1)

        @block.gpsimd
        def _(pool):
            n_link = [0]

            def link(ins):
                n_link[0] += 1
                ins.then_inc(pool_link, 1)
                pool.wait_ge(pool_link, n_link[0])

            link(pool.memset(zeros[:, :], 0.0))
            pool.wait_ge(tab_in, 16)
            for l in range(DEPTH):
                half = HD // 2
                for part in (((C_NKC, 2),), ((C_NQ, 8), (C_NKS, 2), (C_NKW, 2)), ((C_RQ, 8),)):
                    for c0, nh in part:
                        pool.wait_ge(proj_ready, WBLK * l + blocks_by(c0, c0 + nh * HD))
                        for t in range(TT):
                            v = proj[:, t, c0:c0 + nh * HD].rearrange("p (h d) -> p h d", h=nh)
                            r = rope_t[:, 0:nh, :]
                            cos, sin = (rope[:, s, t, :].unsqueeze(1) for s in range(2))
                            pool.tensor_tensor(r[:, :, 0:half], v[:, :, half:HD], sin[:, :, 0:half].broadcast_to([P, nh, half]), ALU.mult)
                            link(pool.tensor_tensor(r[:, :, half:HD], v[:, :, 0:half], sin[:, :, half:HD].broadcast_to([P, nh, half]), ALU.mult))
                            link(pool.tensor_tensor(v, v, cos.broadcast_to([P, nh, HD]), ALU.mult))
                            link(pool.tensor_tensor(v, v, r, ALU.add))
                    pool.drain().then_inc(roped, 1)
                pool.wait_ge(cum_ready, l + 1)
                pool.wait_ge(proj_ready, WBLK * l + blocks_by(C_FQ, C_FF))
                for g in range(2):
                    if g or l:
                        pool.wait_ge(T_full, marks[l - 1 + g, 1 - g])
                    for aug, c0, own in ((q_aug, C_FQ, 0), (k_aug, C_FK, 1)):
                        src = proj[:, :, c0 + g * HG * HD:c0 + (g + 1) * HG * HD].rearrange("p t (h d) -> p t h d", h=HG)
                        for t in range(TT):
                            pool.tensor_copy(aug[:, t, :, 0:HD], src[:, t, :, :])
                            pool.tensor_copy(aug[:, t, :, HD + own:HD + own + 1], cum[:, t, g * HG:(g + 1) * HG, own:own + 1])
                            pool.memset(aug[:, t, :, HD + 1 - own:HD + 2 - own], 1.0)
                    pool.drain().then_inc(aug_ready, 1)

        @block.scalar
        def _(act):
            b = Books()
            link_n = [0]

            def link(ins):
                link_n[0] += 1
                ins.then_inc(act_link, 1)
                act.wait_ge(act_link, link_n[0])

            def copy(dst, src):
                return nc.scalar.activation(dst, src, ACT.Copy)

            def split_to(at):
                while b.hl_in.n < min(at, b.end):
                    h = b.hl_in.take()
                    i = h % 2
                    g = b.raw.take() if i == 0 else b.raw.n - 1
                    if i == 0:
                        act.wait_ge(landed[b.raw.slot(g)], (b.raw.before(g) + 1) * 16)
                    if h >= HL or b.hl_in.loops:
                        act.wait_ge(half_used, b.hl_in.done(h - HL))
                    copy(w_hi[b.hl_in.slot(h)][:, :], raw[b.raw.slot(g)][:, i * HALF:(i + 1) * HALF]).then_inc(hi_ready, 1)
                    for _ in range(i * BEHIND.get(h // 2, 0)):
                        b.raw.take()

            def start_splits():
                b.end = 2 * (DEPTH * MIX_CHUNKS + DENSE_CHUNKS + 6 * EFB)
                split_to(AHEAD)

            def ahead():
                n = b.end - b.hl_in.n + AHEAD
                b.end += AHEAD
                split_to(b.hl_in.n + n)

            def use(n, halves=AHEAD):
                split_to(b.hl.n + 2 * n + halves)
                for _ in range(n):
                    b.hl.take()
                    v = b.hl.take()
                return v

            def T_in():
                v = b.T.take()
                act.wait_ge(T_full, b.T.done(v))
                return pT[b.T.slot(v)], T_free[b.T.slot(v)]

            def T_copy(dst_of):
                pt, free = T_in()
                copy(*dst_of(pt)).then_inc(free, 1)

            def skip(turn, n):
                for _ in range(n):
                    turn.take()

            act.wait_ge(cols_ready, 1)
            nc.scalar.activation(csilu[:, :], cols[:, 0, R_C:R_C + 8], ACT.Silu).then_inc(csilu_ready, 1)
            skip(b.T, DEPTH + FIRST)
            skip(b.raw, 2 * FIRST)
            n_norm, n_hf, n_m, n_dev = [0], [0], [0], [0]

            def root():
                n_norm[0] += 1
                act.wait_ge(ms_ready, n_norm[0])
                nc.scalar.activation(nrm[:, 2:4], nrm[:, 0:2], ACT.Sqrt).then_inc(rt_ready, 1)

            def hi_columns():
                for q in range(4):
                    b.T.take()
                    n_hf[0] += 1
                    act.wait_ge(hf_ready, n_hf[0])
                    copy(h_hi[:, 2 * q:2 * q + 2, :], hf[:, 2 * q:2 * q + 2, :]).then_inc(h_hi_ready, 1)

            def evacuate_qk(c, l):
                kind, g = CALLS[c]
                kt = kT[c % 2]
                pair = lambda dst, p0, kd: T_copy(lambda pt: (dst[0:kd, p0:p0 + 2, :], pt[0:kd, :].rearrange("p (h n) -> p h n", h=2)))
                if kind == "cmp":
                    pair(qT, 0, HD)
                    pair(qT, 2, HD)
                    skip(b.A, 1)
                elif kind in ("sel", "win"):
                    T_copy(lambda pt: (kt[0:HD, 0, :], pt[0:HD, 0:SEQ]))
                    skip(b.A, 3)
                else:
                    kd = HD if kind == "ret" else HD + 2
                    for dst in (qT, kt):
                        pair(dst, 0, kd)
                        pair(dst, 2, kd)
                    skip(b.A, 3)

            def exponentials(c, l):
                kind, g = CALLS[c]
                s, st = S[c % 2], stat[:, (c % 2) * 40:(c % 2) * 40 + 40]
                s_at = S_SIGNALS * l + sum(S_COUNT[k] for k, _ in CALLS[:c])
                if kind == "ret":
                    return
                if kind == "cmp":
                    act.wait_ge(s_ready, s_at + 1)
                    nc.scalar.activation(s[:, 0:P], s[:, 0:P], ACT.Exp, scale=SCALE).then_inc(p_ready, 1)
                    return
                for t in range(TT):
                    act.wait_ge(s_ready, s_at + t + 1)
                    for h in range(HG):
                        v = s[:, h * P:(h + 1) * P] if t == 0 else s[:, HG * P + h * SEQ:HG * P + (h + 1) * SEQ]
                        ins = nc.scalar.activation(v, v, ACT.Exp, bias=st[:, 8 + t * HG + h:9 + t * HG + h], scale=SCALE,
                                                   accum_out=st[:, 16 + t * HG + h:17 + t * HG + h])
                    ins.then_inc(p_ready, 1)

            def evacuate_p(c):
                kind, g = CALLS[c]
                if kind == "ret":
                    for t in range(TT):
                        skip(b.O, 1)
                        n_dev[0] += 1
                        act.wait_ge(var_ready, n_dev[0])
                        nc.scalar.activation(ret_st[:, 12:16], ret_st[:, 8:12], ACT.Sqrt).then_inc(dev_ready, 1)
                elif kind == "cmp":
                    for t in range(TT):
                        T_copy(lambda pt: (PT[0:NCMP, t * 4 * P:(t + 1) * 4 * P], pt[0:NCMP, :]))
                    skip(b.O, 2)
                else:
                    for i in range(3):
                        T_copy(lambda pt: (PT[:, i * 4 * P:(i + 1) * 4 * P], pt[:, :]))
                    skip(b.O, 2)

            def compression(part, l):
                if part == 0:
                    pt, free = T_in()
                    for i in range(4):
                        kv, g = divmod(i, 2)
                        src = pt[g * HD:(g + 1) * HD, kv * SEQ:(kv + 1) * SEQ]
                        copy(kk[0:HD, i, :], src)
                        ins = copy(kk[HD:P, i, 0:SEQ - 1], src[:, 1:SEQ])
                    ins.then_inc(free, 1)
                    act.wait_ge(win_ready, l + 1)
                    copy(win_hi[:, :, 0:480], win[:, :, :, :, :].rearrange("p v j g n -> p v (j g n)")).then_inc(win_hi_ready, 1)
                elif part == 1:
                    for kv in range(2):
                        v = use(2)
                        av = b.A.take()
                        act.wait_ge(half_used, b.hl.done(v))
                        nc.scalar.activation(hid[0:30, kv, :], pA[b.A.slot(av)][0:30, 0:CMP_HID], ACT.Silu).then_inc(hid_ready, 1)
                        act.drain().then_inc(A_free[b.A.slot(av)], 1)
                else:
                    pt, free = T_in()
                    copy(hidT[:, :, :], pt[:, 0:P].rearrange("p (i n) -> p i n", i=4)[:, :, 0:30]).then_inc(free, 1)
                    skip(b.O, 1)

            for l in range(DEPTH):
                root()
                hi_columns()
                if l == 0:
                    start_splits()
                for at_step, (kind, *which) in enumerate(STEPS):
                    at = b.hl.n // 2
                    if kind == "w":
                        use(2)
                        skip(b.A, 2)
                        if which[0] == 2:
                            act.wait_ge(proj_ready, WBLK * l + blocks_by(C_NG, C_RQ))
                            nc.scalar.activation(gates3[:, :, :], proj[:, :, C_NG:C_NG + 24], ACT.Sigmoid).then_inc(sig_ready, 1)
                    elif kind == "k":
                        compression(which[0], l)
                    elif kind == "f":
                        act.wait_ge(z_ready, l + 1)
                        link(nc.scalar.activation(fox[:, 1, :], fox[:, 1, :], ACT.Exp))
                        nc.scalar.activation(fox[:, 2, :], fox[:, 1, :], ACT.Ln, bias=1.0).then_inc(e_ready, 1)
                        skip(b.O, 1)
                    elif kind == "a":
                        c = which[0]
                        if CALLS[c][0] == "ret":
                            act.wait_ge(proj_ready, WBLK * l + blocks_by(C_RG, C_FQ))
                            rg = proj[:, :, C_RG:C_RG + W]
                            nc.scalar.activation(rg, rg, ACT.Silu).then_inc(sig_ready, 1)
                        evacuate_qk(c, l)
                        if c == 0 or ("b", c - 1) in STEPS[:at_step]:
                            exponentials(c, l)
                    elif kind == "b":
                        c = which[0]
                        evacuate_p(c)
                        if ("a", c + 1) in STEPS[:at_step]:
                            exponentials(c + 1, l)
                    elif kind == "o":
                        m = which[0]
                        for q in range(2):
                            pt, free = T_in()
                            copy(oT_hi[m][:, 2 * q:2 * q + 2, :], pt[:, :].rearrange("p (k n) -> p k n", k=2)).then_inc(oT_hi_ready, 1)
                    else:
                        v = use(2)
                        act.wait_ge(half_used, b.hl.done(v))
                        if n_m[0]:
                            act.wait_ge(g_used, n_m[0])
                        n_m[0] += 1
                        for t in range(TT):
                            av = b.A.take()
                            ins = nc.scalar.activation(gate[t][:, :], pA[b.A.slot(av)][:, :], ACT.Sigmoid)
                            ins.then_inc(A_free[b.A.slot(av)], 1)
                        skip(b.A, 2)
                        use(1)
                    skip(b.T, len(ada_blocks(at, b.hl.n // 2)))
                for q in range(4):
                    pt, free = T_in()
                    copy(h_hi[:, 2 * q:2 * q + 2, :], pt[:, :].rearrange("p (k n) -> p k n", k=2)).then_inc(h_hi_ready, 1)
                skip(b.A, 2)
                use(4)
                skip(b.A, 4)
                root()
                if l % 2 == 0:
                    hi_columns()
                    G = Turn()

                    def silu(width=W):
                        v = G.take()
                        act.wait_ge(half_used, b.hl.done(b.hl.n - 1))
                        for t in range(TT):
                            ins = nc.scalar.activation(a_sb[:, t, 0:width], pA[t][:, 0:width], ACT.Silu)
                        ins.then_inc(g_free, 1)

                    def hi_a(n):
                        for q in range(n):
                            pt, free = T_in()
                            copy(aT_hi[:, 2 * q:2 * q + 2, :], pt[:, :].rearrange("p (k n) -> p k n", k=2)).then_inc(aT_hi_ready, 1)
                    use(2)
                    silu()
                    use(2)
                    with rounds(act, 0, FFB // 2, {b.raw: 18, b.hl: 24, b.hl_in: 24, b.T: 6, b.O: 8, G: 2}):
                        for _ in range(2):
                            use(2)
                            hi_a(2)
                            silu()
                            use(2)
                            use(2)
                            skip(b.O, 4)
                        skip(b.T, 2)
                    use(1)
                    hi_a(2)
                    silu(W // 2)
                    use(1)
                    use(2)
                    skip(b.O, 4)
                    hi_a(1)
                    use(1, 1)
                    skip(b.O, 4)
                    skip(b.A, 2)
                else:
                    skip(b.T, 4)
                    act.wait_ge(log_ready, 1)
                    nc.scalar.activation(rs[:, 2, :], rs[:, 2, :], ACT.Exp).then_inc(re_ready, 1)
                    act.wait_ge(slots_ready, 1)
                    items = act.value_load(flag[0:1, 0:1], min_val=NE, max_val=2 * NE)
                    G, xv = Turn(start=FFB + 1), Turn()

                    def hi_x(at):
                        for q in range(2):
                            act.wait_ge(xf_ready, at + q + 1)
                            copy(x_hi[:, 4 * q:4 * q + 4, :], x_f[:, 4 * q:4 * q + 4, :]).then_inc(x_hi_ready, 1)
                    skip(b.T, 2)
                    hi_x(0)
                    with rounds(act, 0, items, {b.raw: 42, b.hl: 84, b.hl_in: 84, b.T: 22, b.O: 2, G: EFB, xv: 1}) as e:
                        v = xv.take()
                        for t in range(TT):
                            T_copy(lambda pt: (selT[:, t * P:(t + 1) * P], pt[:, 0:P]))

                        def silu():
                            G.take()
                            act.wait_ge(half_used, b.hl.done(b.hl.n - 1))
                            nc.scalar.activation(a_sb[:, 0, :], pA[0][:, :], ACT.Silu).then_inc(g_free, 1)

                        def hi_a():
                            for q in range(2):
                                pt, free = T_in()
                                copy(aT_hi[:, 2 * q:2 * q + 2, 0:P], pt[:, 0:SEQ].rearrange("p (k n) -> p k n", k=2)).then_inc(aT_hi_ready, 1)
                        use(2)
                        silu()
                        use(2)
                        with rounds(act, 1, EFB, {b.raw: 6, b.hl: 12, b.hl_in: 12, b.T: 2, G: 1}):
                            use(2)
                            hi_a()
                            silu()
                            use(4)
                        skip(b.T, 2)
                        hi_a()
                        hi_x(xv.done(v, 2))
                        u = use(2)
                        with act.If(e < items - 1):
                            ahead()
                        act.wait_ge(half_used, b.hl.done(u))
                        copy(oe[:, 0:W], pO[b.O.slot(b.O.take())][:, :]).then_inc(O_free[0], 1)
                        skip(b.O, 1)
                        skip(b.T, 4)
            root()

        @block.vector
        def _(dve):
            b = Books()
            V = nc.vector

            def link(ins):
                v = b.link.take()
                ins.then_inc(dve_link, 1)
                dve.wait_ge(dve_link, b.link.done(v))

            def split_to(at):
                while b.hl_in.n < min(at, b.end):
                    h = b.hl_in.take()
                    i = h % 2
                    g = b.raw.take() if i == 0 else b.raw.n - 1
                    dve.wait_ge(hi_ready, b.hl_in.done(h))
                    s, m = b.raw.slot(g), b.hl_in.slot(h)
                    V.tensor_tensor(w_lo[m][:, :], raw[s][:, i * HALF:(i + 1) * HALF], w_hi[m][:, :].bitcast(F32), ALU.subtract).then_inc(raw_done, 1)
                    for _ in range(i * BEHIND.get(h // 2, 0)):
                        ada_chunk()

            def ada_chunk():
                n, c = divmod(b.ada.take(), 2)
                g = b.raw.take()
                s = raw[b.raw.slot(g)]
                dst = acc[ada_buffer(n)]
                dve.wait_ge(landed[b.raw.slot(g)], (b.raw.before(g) + 1) * 16)
                for k in range(CK):
                    src, sc = s[:, k * W:(k + 1) * W], csilu[:, c * CK + k:c * CK + k + 1]
                    if c + k == 0:
                        ins = V.tensor_scalar(dst[:, :], src, sc, None, ALU.mult)
                    else:
                        ins = V.scalar_tensor_tensor(dst[:, :], src, sc, dst[:, :], ALU.mult, ALU.add)
                    if k % 2 == 1:
                        ins.then_inc(raw_done, 1)
                        dve.wait_ge(raw_done, b.raw.done(g, 2) - (1 - k // 2))
                    else:
                        link(ins)

            def ada_columns(l, at, n):
                pt, free = T_in()
                V.tensor_tensor(mod[:, l, bass.ds(at, 4 * n)], pt[:, 0:4 * n], cols[:, l, bass.ds(at + R_ADAB, 4 * n)], ALU.add).then_inc(free, 1)

            def ada_scale(l, at, w):
                link(dve.drain())
                link(V.scalar_tensor_tensor(mod[:, l, at:at + 8], mod[:, l, at:at + 8], 1.0, cols[:, l, w:w + 8], ALU.add, ALU.mult))

            def start_splits():
                b.end = 2 * (DEPTH * MIX_CHUNKS + DENSE_CHUNKS + 6 * EFB)
                split_to(AHEAD)

            def ahead():
                n = b.end - b.hl_in.n + AHEAD
                b.end += AHEAD
                split_to(b.hl_in.n + n)

            def use(n, halves=AHEAD):
                split_to(b.hl.n + 2 * n + halves)
                for _ in range(n):
                    b.hl.take()
                    v = b.hl.take()
                return v

            def T_in():
                v = b.T.take()
                dve.wait_ge(T_full, b.T.done(v))
                return pT[b.T.slot(v)], T_free[b.T.slot(v)]

            def A_in(chunk=None):
                v = b.A.take()
                if chunk is None:
                    dve.wait_ge(A_full, b.Af.done(b.Af.take()))
                else:
                    dve.wait_ge(half_used, b.hl.done(chunk))
                return pA[b.A.slot(v)], A_free[b.A.slot(v)]

            def O_in(chunk=None):
                v = b.O.take()
                if chunk is None:
                    dve.wait_ge(O_full, b.Of.done(b.Of.take()))
                else:
                    dve.wait_ge(half_used, b.hl.done(chunk))
                return pO[b.O.slot(v)], O_free[b.O.slot(v)]

            def skip(turn, n):
                for _ in range(n):
                    turn.take()

            def bc(v, shape):
                return v.broadcast_to(shape)

            for l in range(DEPTH):
                pt, free = T_in()
                V.tensor_copy(cols[:, l, 0:ROWS], pt[:, 0:ROWS]).then_inc(cols_ready, 1)
                dve.drain().then_inc(free, 1)

            n_rt, n_hi = [0], [0]

            def normalise(meanwhile=lambda: None, final=False):
                for t in range(TT):
                    link(V.tensor_tensor_reduce(y[:, t, :], x[:, t, :], x[:, t, :], 1.0, 0.0, ALU.mult, ALU.add, nrm[:, 6 + t:7 + t]))
                V.tensor_scalar(nrm[:, 0:2], nrm[:, 6:8], 1.0 / D, EPS, ALU.mult, ALU.add).then_inc(ms_ready, 1)
                n_rt[0] += 1
                meanwhile()
                dve.wait_ge(rt_ready, n_rt[0])
                link(V.reciprocal(nrm[:, 4:6], nrm[:, 2:4]))
                for t in range(TT):
                    if final:
                        ins = V.scalar_tensor_tensor(y[:, t, :], x[:, t, :], nrm[:, 4 + t:5 + t], final_w[:, :], ALU.mult, ALU.mult).then_inc(fin_ready, 1)
                    else:
                        ins = V.tensor_scalar(y[:, t, :], x[:, t, :], nrm[:, 4 + t:5 + t], None, ALU.mult)
                return ins

            def modulate(l, which, both):
                sc, sh = (which * 24 + 8, which * 24)
                for q in range(4):
                    pt, free = T_in()
                    for j in range(2):
                        k = 2 * q + j
                        ins = V.tensor_scalar(hf[:, k, :], pt[:, j * SEQ:(j + 1) * SEQ], mod[:, l, sc + k:sc + k + 1],
                                              mod[:, l, sh + k:sh + k + 1], ALU.mult, ALU.add)
                    ins.then_inc(hf_ready, 1)
                    dve.drain().then_inc(free, 1)
                    if both:
                        n_hi[0] += 1
                        dve.wait_ge(h_hi_ready, n_hi[0])
                        V.tensor_tensor(h_lo[:, 2 * q:2 * q + 2, :], hf[:, 2 * q:2 * q + 2, :],
                                        h_hi[:, 2 * q:2 * q + 2, :].bitcast(F32), ALU.subtract).then_inc(h_ready, 1)

            def scores(c, l):
                kind, g = CALLS[c]
                s, st = S[c % 2], stat[:, (c % 2) * 40:(c % 2) * 40 + 40]
                skip(b.T, {"cmp": 2, "sel": 1, "win": 1, "ret": 4, "fox": 4}[kind])
                if kind == "ret":
                    for p0 in range(0, HG, 2):
                        pa, free = A_in()
                        V.tensor_tensor(s[:, p0 * SEQ:(p0 + 2) * SEQ], pa[:, :], decay[:, p0:p0 + 2, :].rearrange("p h n -> p (h n)"), ALU.mult).then_inc(free, 1)
                    pa, free = A_in()
                    link(V.tensor_tensor(s[:, 4 * SEQ:4 * SEQ + 4 * P].rearrange("p (h n) -> p h n", h=HG),
                                         pa[:, :].rearrange("p (h n) -> p h n", h=HG), decay[:, :, 0:P], ALU.mult))
                    dve.drain().then_inc(free, 1)
                    dve.drain().then_inc(s_ready, 1)
                    return
                if kind == "cmp":
                    pa, free = A_in()
                    sv = s[:, 0:P].rearrange("p (r n) -> p r n", n=16)[:, :, 0:NCMP]
                    cm = cmask.rearrange("p t h n -> p (t h) n")[:, :, 0:NCMP]
                    link(V.memset(s[:, 0:P], 0.0))
                    V.tensor_tensor(sv, pa[:, 0:P].rearrange("p (r n) -> p r n", n=16)[:, :, 0:NCMP], cm, ALU.add).then_inc(free, 1)
                    v = b.A.n - 1
                    dve.wait_ge(free, b.A.before(v) + 1)
                    link(V.tensor_reduce(st[:, 0:8], sv, AX_X, ALU.max))
                    V.tensor_tensor(sv, sv, bc(st[:, 0:8].unsqueeze(2), [P, 8, NCMP]), ALU.subtract).then_inc(s_ready, 1)
                    return
                for t in range(TT):
                    w = (t + 1) * P
                    for i in range(t + 1):
                        nh = HG // (t + 1)
                        pa, free = A_in()
                        at = HG * P * t + i * nh * w
                        dst = s[:, at:at + nh * w].rearrange("p (h n) -> p h n", h=nh)
                        mk = mask[:, 2 * P - w:2 * P].unsqueeze(1)
                        V.tensor_tensor(dst, pa[:, 0:nh * w].rearrange("p (h n) -> p h n", h=nh), bc(mk, [P, nh, w]), ALU.add).then_inc(free, 1)
                        v = b.A.n - 1
                        dve.wait_ge(free, b.A.before(v) + 1)
                    sv = s[:, HG * P * t:HG * P * t + HG * w].rearrange("p (h n) -> p h n", h=HG)
                    link(V.tensor_reduce(st[:, t * HG:(t + 1) * HG], sv, AX_X, ALU.max))
                    V.tensor_scalar(st[:, 8 + t * HG:8 + (t + 1) * HG], st[:, t * HG:(t + 1) * HG], -SCALE, None, ALU.mult).then_inc(s_ready, 1)

            def compression(part, l):
                if part == 0:
                    b.T.take()
                    dve.wait_ge(T_free[b.T.slot(b.T.n - 1)], b.T.before(b.T.n - 1) + 1)
                    V.memset(win_hi[:, :, 480:578].bitcast(F32), 0.0)
                    V.memset(win_lo[:, :, 480:578].bitcast(F32), 0.0)
                    for kv in range(2):
                        for g in range(2):
                            for jh in range(2):
                                v = kk[:, 2 * kv + g, :].rearrange("p (m j s) -> p s j m", j=8, s=2)[:, 0, :, jh:jh + NCMP]
                                pe_c = cols[:, l, R_PEK + 16 * kv + 8 * jh:R_PEK + 16 * kv + 8 * jh + 8].unsqueeze(2)
                                ins = V.tensor_tensor(win[:, kv, 8 * jh:8 * jh + 8, g, :], v, bc(pe_c, [P, 8, NCMP]), ALU.add)
                    ins.then_inc(win_ready, 1)
                    dve.wait_ge(win_hi_ready, l + 1)
                    V.tensor_tensor(win_lo[:, :, 0:480], win[:, :, :, :, :].rearrange("p v j g n -> p v (j g n)"),
                                    win_hi[:, :, 0:480].bitcast(F32), ALU.subtract).then_inc(win_lo_ready, 1)
                elif part == 1:
                    use(4)
                    skip(b.A, 2)
                else:
                    b.T.take()
                    po, free = O_in()
                    V.tensor_copy(kcT[0:HD, 0:30], po[0:HD, 0:30])
                    V.tensor_copy(vc[0:NCMP, :, :], po[0:NCMP, HD:3 * HD].rearrange("p (g d) -> p g d", g=2)).then_inc(free, 1)

            def forget_gates(l):
                z = fox[:, 0, :].rearrange("p (t h) -> p t h", t=TT)
                dve.wait_ge(small_in, SMALL)
                dve.wait_ge(proj_ready, WBLK * l + blocks_by(C_FF, C_MG))
                link(V.tensor_tensor(z, proj[:, :, C_FF:C_FF + 8], bc(fbias[:, l, :].unsqueeze(1), [P, TT, 8]), ALU.add))
                link(V.tensor_scalar(fox[:, 1, :], fox[:, 0, :], -1.0, None, ALU.mult))
                V.tensor_tensor(fox[:, 1, :], fox[:, 1, :], fox[:, 0, :], ALU.min).then_inc(z_ready, 1)
                dve.wait_ge(e_ready, l + 1)
                V.scalar_tensor_tensor(fox[:, 3, :], fox[:, 0, :], 0.0, fox[:, 2, :], ALU.min, ALU.subtract).then_inc(ls_ready, 1)
                po, free = O_in()
                cs = po[:, 0:16].rearrange("p (t h) -> p t h", t=TT)
                V.tensor_scalar(cum[:, :, :, 0], cs, 1.0 / SCALE, None, ALU.mult)
                link(V.tensor_scalar(cum[:, :, :, 1], cs, -1.0 / SCALE, None, ALU.mult))
                dve.drain().then_inc(free, 1)
                dve.drain().then_inc(cum_ready, 1)

            def merge(m, half):
                use(2)
                skip(b.A, 2)
                v = use(1)
                for t in range(TT):
                    pa, free = A_in(v)
                    if t == 0:
                        dve.wait_ge(A_free[b.A.slot(b.A.n - 2)], b.A.before(b.A.n - 2) + 1)
                    dst = merged[t][:, half * W:(half + 1) * W]
                    if m == 0:
                        V.tensor_tensor(dst, pa[:, :], gate[t][:, :], ALU.mult).then_inc(free, 1)
                    else:
                        V.tensor_tensor(tmp[:, :], pa[:, :], gate[t][:, :], ALU.mult).then_inc(free, 1)
                        dve.wait_ge(free, b.A.before(b.A.n - 1) + 1)
                        link(V.tensor_tensor(dst, dst, tmp[:, :], ALU.add))
                dve.drain().then_inc(g_used, 1)

            def values(c, l):
                kind, g = CALLS[c]
                st = stat[:, (c % 2) * 40:(c % 2) * 40 + 40]
                s = S[c % 2]
                skip(b.T, {"cmp": 2, "sel": 3, "win": 3, "ret": 0, "fox": 3}[kind])
                if kind == "ret":
                    for t in range(TT):
                        po, free = O_in()
                        for h in range(HG):
                            link(V.bn_stats(fox_st[:, h * 6:(h + 1) * 6], po[:, h * P:(h + 1) * P]))
                            link(V.bn_aggr(ret_st[:, h * 2:h * 2 + 2], fox_st[:, h * 6:(h + 1) * 6]))
                        mv = ret_st[:, 0:8].rearrange("p (h s) -> p h s", s=2)
                        V.tensor_scalar(ret_st[:, 8:12], mv[:, :, 1], EPS, None, ALU.add).then_inc(var_ready, 1)
                        dve.wait_ge(dev_ready, TT * l + t + 1)
                        link(V.reciprocal(ret_st[:, 16:20], ret_st[:, 12:16]))
                        for h in range(HG):
                            link(V.tensor_scalar(o_sb[:, t, h * P:(h + 1) * P], po[:, h * P:(h + 1) * P], ret_st[:, 2 * h:2 * h + 1],
                                                 ret_st[:, 16 + h:17 + h], ALU.subtract, ALU.mult))
                        dve.drain().then_inc(free, 1)
                        link(V.tensor_tensor(o_sb[:, t, :], o_sb[:, t, :], proj[:, t, C_RG:C_RG + W], ALU.mult))
                    dve.drain().then_inc(o_ready, 1)
                    return
                p_at = P_SIGNALS * l + sum(P_COUNT[k] for k, _ in CALLS[:c])
                if kind == "cmp":
                    dve.wait_ge(p_ready, p_at + 1)
                    sv = s[:, 0:P].rearrange("p (r n) -> p r n", n=16)[:, :, 0:NCMP]
                    link(V.tensor_reduce(st[:, 16:24], sv, AX_X, ALU.add))
                else:
                    dve.wait_ge(p_ready, p_at + 2)
                link(V.reciprocal(st[:, 24:32], st[:, 16:24]))
                coef = st[:, 24:32]
                if kind != "fox":
                    coef = st[:, 32:40]
                    branch = {"cmp": 0, "sel": 1, "win": 2}[kind]
                    cv = coef.rearrange("p (t h) -> p t h", t=TT)
                    link(V.tensor_tensor(cv, st[:, 24:32].rearrange("p (t h) -> p t h", t=TT),
                                         gates3[:, :, branch * 8 + g * HG:branch * 8 + (g + 1) * HG], ALU.mult))
                    if kind == "cmp":
                        link(V.tensor_tensor(cv, cv, bc(cvalid.unsqueeze(2), [P, TT, HG]), ALU.mult))
                for t in range(TT):
                    po, free = O_in()
                    src = po[:, 0:HG * HD].rearrange("p (h d) -> p h d", h=HG)
                    dst = o_sb[:, t, g * HG * HD:(g + 1) * HG * HD].rearrange("p (h d) -> p h d", h=HG)
                    cf = bc(coef[:, t * HG:(t + 1) * HG].unsqueeze(2), [P, HG, HD])
                    if kind in ("cmp", "fox"):
                        V.tensor_tensor(dst, src, cf, ALU.mult).then_inc(free, 1)
                        dve.wait_ge(free, b.O.before(b.O.n - 1) + 1)
                    else:
                        part = o_part[:, :].rearrange("p (h d) -> p h d", h=HG)
                        V.tensor_tensor(part, src, cf, ALU.mult).then_inc(free, 1)
                        dve.wait_ge(free, b.O.before(b.O.n - 1) + 1)
                        link(V.tensor_tensor(dst, dst, part, ALU.add))
                if c in WHOLE:
                    dve.drain().then_inc(o_ready, 1)

            dve.wait_ge(x_in, 16)
            dve.wait_ge(tab_in, 16)
            dve.wait_ge(csilu_ready, 1)
            dve.wait_ge(cols_ready, DEPTH)
            for l in range(DEPTH):
                normalise().then_inc(y_ready, 1)
                if l == 0:
                    for j in range(FIRST):
                        ada_chunk()
                        ada_chunk()
                        if j:
                            ada_columns(0, 4 * (j - 1), 1)
                    ada_columns(0, 4 * (FIRST - 1), 1)
                    ada_scale(0, 8, R_NMIX)
                modulate(l, 0, True)
                if l == 0:
                    start_splits()
                for kind, *which in STEPS:
                    at = b.hl.n // 2
                    if kind == "w":
                        v = use(2)
                        for t in range(TT):
                            src, free = A_in(v)
                            V.tensor_copy(proj[:, t, which[0] * W:(which[0] + 1) * W], src[:, :]).then_inc(free, 1)
                        dve.drain().then_inc(proj_ready, 1)
                    elif kind == "k":
                        compression(which[0], l)
                    elif kind == "f":
                        forget_gates(l)
                    elif kind == "a":
                        scores(which[0], l)
                    elif kind == "b":
                        c = which[0]
                        if c == 0:
                            dve.wait_ge(sig_ready, 2 * l + 1)
                        if CALLS[c][0] == "ret":
                            dve.wait_ge(sig_ready, 2 * l + 2)
                        values(c, l)
                    elif kind == "o":
                        m = which[0]
                        for q in range(2):
                            pt, free = T_in()
                            dve.wait_ge(oT_hi_ready, 6 * l + 2 * m + q + 1)
                            V.tensor_tensor(oT_lo[m][:, 2 * q:2 * q + 2, :], pt[:, :].rearrange("p (k n) -> p k n", k=2),
                                            oT_hi[m][:, 2 * q:2 * q + 2, :].bitcast(F32), ALU.subtract).then_inc(oT_ready, 1)
                            dve.drain().then_inc(free, 1)
                    else:
                        merge(*which)
                    for n in ada_blocks(at, b.hl.n // 2):
                        ada_columns(n // ADA, n % ADA * 4, 1)
                if l == 0:
                    ada_scale(0, 32, R_NFFN)
                dve.drain().then_inc(merged_ready, 1)
                for q in range(4):
                    pt, free = T_in()
                    n_hi[0] += 1
                    dve.wait_ge(h_hi_ready, n_hi[0])
                    V.tensor_tensor(h_lo[:, 2 * q:2 * q + 2, :], pt[:, :].rearrange("p (k n) -> p k n", k=2),
                                    h_hi[:, 2 * q:2 * q + 2, :].bitcast(F32), ALU.subtract).then_inc(h_ready, 1)
                    dve.drain().then_inc(free, 1)

                def gate_rows():
                    for half in range(2):
                        pa, free = A_in()
                        V.tensor_copy(gw[:, half * W:(half + 1) * W], pa[:, :]).then_inc(free, 1)
                        dve.wait_ge(free, b.A.before(b.A.n - 1) + 1)
                gate_rows()
                link(V.memset(yacc[:, :, :], 0.0))
                for half in range(2):
                    v = use(2)
                    for t in range(TT):
                        pa, free = A_in(v)
                        V.tensor_tensor(tmp[:, :], pa[:, :], gw[:, half * W:(half + 1) * W], ALU.mult).then_inc(free, 1)
                        dve.wait_ge(free, b.A.before(b.A.n - 1) + 1)
                        link(V.tensor_tensor(x[:, t, half * W:(half + 1) * W], x[:, t, half * W:(half + 1) * W], tmp[:, :], ALU.add))
                normalise(gate_rows).then_inc(y_ready, 1)
                if l % 2 == 0:
                    modulate(l, 1, True)
                    av, aq = Turn(), Turn()

                    def hidden(width=W):
                        v = av.take()
                        dve.wait_ge(g_free, av.done(v))
                        dve.wait_ge(half_used, b.hl.done(b.hl.n - 1))
                        for t in range(TT):
                            ins = V.tensor_tensor(a_sb[:, t, 0:width], a_sb[:, t, 0:width], pA[2 + t][:, 0:width], ALU.mult)
                        ins.then_inc(a_ready, 1)
                        dve.drain().then_inc(u_free, 1)

                    def lo_a(n):
                        for q in range(n):
                            pt, free = T_in()
                            v = aq.take()
                            dve.wait_ge(aT_hi_ready, aq.done(v))
                            V.tensor_tensor(aT_lo[:, 2 * q:2 * q + 2, :], pt[:, :].rearrange("p (k n) -> p k n", k=2),
                                            aT_hi[:, 2 * q:2 * q + 2, :].bitcast(F32), ALU.subtract).then_inc(free, 1)

                    def add_down(t, half, chunk=None):
                        po, free = O_in(chunk)
                        dst = yacc[:, t, half * W:(half + 1) * W]
                        V.tensor_tensor(dst, dst, po[:, :], ALU.add).then_inc(free, 1)

                    def down():
                        for half in range(2):
                            v = use(1)
                            add_down(0, half)
                            add_down(1, half, v)
                    use(2)
                    use(2)
                    hidden()
                    with rounds(dve, 0, FFB // 2, {b.raw: 18, b.hl: 24, b.hl_in: 24, b.T: 6, b.O: 8, b.Of: 4, av: 2, aq: 4, b.ada: 6, b.link: 12}) as r:
                        for _ in range(2):
                            use(2)
                            lo_a(2)
                            use(2)
                            hidden()
                            down()
                        ada_columns(l + 1, r * 12 + 4 * DENSE_ADA, 2)
                        ada_columns(l + 1, r * 12 + 4 * DENSE_ADA + 8, 1)
                    ada_scale(l + 1, 8, R_NMIX)
                    ada_scale(l + 1, 32, R_NFFN)
                    use(1)
                    lo_a(2)
                    use(1)
                    hidden(W // 2)
                    down()
                    lo_a(1)
                    v = use(1, 1)
                    for i in range(4):
                        add_down(i % 2, i // 2, v if i == 3 else None)
                    dve.wait_ge(O_free[0], b.O.n // 2)
                    dve.wait_ge(O_free[1], b.O.n // 2)
                else:
                    modulate(l, 1, False)
                    pa, free = A_in()
                    r = lambda i: rs[:, i, :]
                    te = lambda i: rs[:, i, :].rearrange("p (t e) -> p t e", t=TT)
                    V.tensor_copy(r(1), pa[:, 0:TT * NE]).then_inc(free, 1)
                    dve.wait_ge(free, b.A.before(b.A.n - 1) + 1)
                    link(V.tensor_reduce(r(3)[:, 0:TT], te(1), AX_X, ALU.max))
                    V.tensor_tensor(te(2), te(1), bc(r(3)[:, 0:TT].unsqueeze(2), [P, TT, NE]), ALU.subtract).then_inc(log_ready, 1)
                    for t in range(TT):
                        other = bc(te(1)[:, t, :].unsqueeze(1), [P, NE, NE])
                        own = bc(te(1)[:, t, :].unsqueeze(2), [P, NE, NE])
                        link(V.tensor_tensor(rt[:, t, :, :], other, own, ALU.is_equal))
                        link(V.tensor_tensor(rt[:, t, :, :], rt[:, t, :, :], ties, ALU.mult))
                        link(V.tensor_tensor(rt2[:, :, :], other, own, ALU.is_gt))
                        link(V.tensor_tensor(rt[:, t, :, :], rt[:, t, :, :], rt2[:, :, :], ALU.add))
                    link(V.tensor_reduce(te(4), rt[:, :, :, :], AX_X, ALU.add))
                    V.tensor_scalar(r(0), r(4), 2.0, None, ALU.is_lt).then_inc(sel_ready, 1)
                    dve.wait_ge(sel_ready, 1)
                    dve.wait_ge(re_ready, 1)
                    link(V.tensor_tensor(r(5), r(2), r(0), ALU.mult))
                    link(V.tensor_reduce(r(6)[:, 0:TT], te(5), AX_X, ALU.add))
                    link(V.reciprocal(r(7)[:, 0:TT], r(6)[:, 0:TT]))
                    for i in range(2):
                        link(V.tensor_tensor(gate16[:, :, i * NE:(i + 1) * NE], te(5), bc(r(7)[:, 0:TT].unsqueeze(2), [P, TT, NE]), ALU.mult))
                    pa, free = A_in()
                    link(V.tensor_tensor(te(8), pa[:, 0:2 * NE].rearrange("p (t e) -> p t e", t=TT), te(0), ALU.mult))
                    link(V.tensor_scalar(slot16[:, :, 0:NE], te(8), -1.0, None, ALU.add))
                    link(V.tensor_scalar(slot16[:, :, NE:2 * NE], te(8), -1.0 - P, None, ALU.add))
                    link(V.tensor_reduce(r(9)[:, 0:1], pa[:, 2 * NE:3 * NE], AX_X, ALU.max))
                    dve.drain().then_inc(free, 1)
                    link(V.tensor_scalar(r(9)[:, 1:2], r(9)[:, 0:1], float(P), float(NE), ALU.is_gt, ALU.mult))
                    link(V.tensor_scalar(flag[:, 0:1], r(9)[:, 1:2], float(NE), None, ALU.add))
                    link(V.memset(slot16[:, :, 2 * NE:], -1.0))
                    dve.drain().then_inc(slots_ready, 1)
                    items = dve.value_load(flag[0:1, 0:1], min_val=NE, max_val=2 * NE)
                    av, aq, xv = Turn(start=FFB + 1), Turn(start=2 * FFB + 1), Turn()

                    def one_hot(e):
                        for t in range(TT):
                            ins = V.tensor_scalar(sel[:, t, :], iota, slot16[:, t, bass.ds(e, 1)], None, ALU.is_equal)
                        ins.then_inc(sel_ready, 1)

                    def gathered():
                        for q in range(2):
                            pt, free = T_in()
                            for j in range(4):
                                k = 4 * q + j
                                ins = V.tensor_scalar(x_f[:, k, :], pt[:, j * P:(j + 1) * P], mod[:, l, 32 + k:33 + k],
                                                      mod[:, l, 24 + k:25 + k], ALU.mult, ALU.add)
                            ins.then_inc(xf_ready, 1)
                            dve.drain().then_inc(free, 1)

                    def lo_x(at):
                        for q in range(2):
                            dve.wait_ge(x_hi_ready, at + q + 1)
                            V.tensor_tensor(x_lo[:, 4 * q:4 * q + 4, :], x_f[:, 4 * q:4 * q + 4, :],
                                            x_hi[:, 4 * q:4 * q + 4, :].bitcast(F32), ALU.subtract).then_inc(x_ready, 1)
                    one_hot(0)
                    gathered()
                    lo_x(0)
                    with rounds(dve, 0, items, {b.raw: 42, b.hl: 84, b.hl_in: 84, b.T: 22, b.O: 2, av: EFB, aq: 2 * EFB, xv: 1}) as e:
                        xe = xv.take()
                        skip(b.T, 2)

                        def hidden():
                            v = av.take()
                            dve.wait_ge(g_free, av.done(v))
                            dve.wait_ge(half_used, b.hl.done(b.hl.n - 1))
                            V.tensor_tensor(a_sb[:, 0, :], a_sb[:, 0, :], pA[2][:, :], ALU.mult).then_inc(a_ready, 1)
                            dve.drain().then_inc(u_free, 1)

                        def lo_a():
                            for q in range(2):
                                pt, free = T_in()
                                v = aq.take()
                                dve.wait_ge(aT_hi_ready, aq.done(v))
                                V.tensor_tensor(aT_lo[:, 2 * q:2 * q + 2, 0:P], pt[:, 0:SEQ].rearrange("p (k n) -> p k n", k=2),
                                                aT_hi[:, 2 * q:2 * q + 2, 0:P].bitcast(F32), ALU.subtract).then_inc(free, 1)
                        use(4)
                        hidden()
                        dve.wait_ge(T_full, b.T.done(b.T.n - 1))
                        one_hot(e + 1)
                        with rounds(dve, 1, EFB, {b.raw: 6, b.hl: 12, b.hl_in: 12, b.T: 2, av: 1, aq: 2}):
                            use(2)
                            lo_a()
                            use(2)
                            hidden()
                            use(2)
                        gathered()
                        lo_a()
                        lo_x(xv.done(xe, 2))
                        v = use(2)
                        with dve.If(e < items - 1):
                            ahead()
                        b.O.take()
                        po, free = O_in(v)
                        V.tensor_copy(oe[:, W:2 * W], po[:, :]).then_inc(free, 1)
                        for t in range(TT):
                            for half in range(2):
                                pt, free = T_in()
                                dst = yacc[:, t, half * W:(half + 1) * W]
                                V.scalar_tensor_tensor(dst, pt[:, :], gate16[:, t, bass.ds(e, 1)], dst, ALU.mult, ALU.add).then_inc(free, 1)
                    link(dve.drain())
                for t in range(TT):
                    link(V.tensor_tensor(yacc[:, t, :], yacc[:, t, :], gw[:, :], ALU.mult))
                    link(V.tensor_tensor(x[:, t, :], x[:, t, :], yacc[:, t, :], ALU.add))
            dve.wait_ge(final_in, 16)
            normalise(final=True)


NAMES = ["x", "c", "ada_w", "ada_b", "norm_mix", "norm_ffn", "w_in", "cmp_k_pe", "cmp_k_w1", "cmp_k_w2", "cmp_v_pe",
         "cmp_v_w1", "cmp_v_w2", "fox_f_bias", "w_read_nsa", "w_read_ret", "w_read_fox", "w_out", "ffn_w1", "ffn_w3",
         "ffn_w2", "router_w", "moe_w1", "moe_w3", "moe_w2", "final_norm"]


def kernel(**inputs):
    import concourse.bacc as bacc
    from concourse.bass_utils import run_bass_kernel_spmd

    nc = bacc.Bacc("TRN2", target_bir_lowering=False, num_devices=1)
    arrays, aps = {}, {}
    for name in NAMES:
        v = np.ascontiguousarray(inputs[name])
        arrays[f"in_{name}"] = v
        aps[name] = nc.dram_tensor(f"in_{name}", v.shape, mybir.dt.from_np(v.dtype), kind="ExternalInput").ap()
    arrays["in_tables"] = tables()
    table = nc.dram_tensor("in_tables", (P, TABLE_W), F32, kind="ExternalInput").ap()
    out = nc.dram_tensor("out_0", (1, SEQ, D), F32, kind="ExternalOutput").ap()
    build(nc, aps, table, out)
    return run_bass_kernel_spmd(nc, [arrays], core_ids=[0]).results[0]["out_0"]
```
